# Optimizing a Trainium2 kernel written in Bass

```python
import jax
import jax.numpy as jnp
from jax import lax
import numpy as np
import math
import jax, jax.numpy as jnp

D_MODEL = 1024
BATCH = 1
SEQ = 512
DEPTH = 2

CHUNK = 64
Q_BLOCK = 128
MEM_LEN = 256

MLA_HEADS = 8
QK_NOPE_DIM = 64
QK_ROPE_DIM = 32
V_HEAD_DIM = 64
Q_LORA_RANK = 256
KV_LORA_RANK = 256
MLA_WIDTH = MLA_HEADS * V_HEAD_DIM
CONV_WIDTH = D_MODEL - MLA_WIDTH
CONV_TAPS = 31
IN_COLS = Q_LORA_RANK + KV_LORA_RANK + QK_ROPE_DIM + 2 * CONV_WIDTH

XA_HEADS = 4
XA_HEAD_DIM = D_MODEL // XA_HEADS

FFN_HIDDEN = ((8 * D_MODEL + 3 * 256 - 1) // (3 * 256)) * 256

ALPHA = (2.0 * DEPTH) ** 0.25
BETA = (8.0 * DEPTH) ** -0.25

ROPE_BASE = 10000.0
LN_EPS = 1e-5
RMS_EPS = 1e-6


def layer_norm(x, g, b):
    xf = x.astype(jnp.float32)
    mu = jnp.mean(xf, axis=-1, keepdims=True)
    var = jnp.mean(jnp.square(xf - mu), axis=-1, keepdims=True)
    y = (xf - mu) * lax.rsqrt(var + LN_EPS)
    return (y * g.astype(jnp.float32) + b.astype(jnp.float32)).astype(x.dtype)

def rms_norm(x, g):
    xf = x.astype(jnp.float32)
    y = xf * lax.rsqrt(jnp.mean(jnp.square(xf), axis=-1, keepdims=True) + RMS_EPS)
    return (y * g.astype(jnp.float32)).astype(x.dtype)

def rope_cos_sin(positions, dim):
    inv_freq = ROPE_BASE ** (-jnp.arange(0, dim, 2, dtype=jnp.float32) / dim)
    ang = positions.astype(jnp.float32)[..., None] * inv_freq
    return jnp.cos(ang), jnp.sin(ang)

def apply_rope(x, cos, sin):
    half = x.shape[-1] // 2
    x1 = x[..., :half].astype(jnp.float32)
    x2 = x[..., half:].astype(jnp.float32)
    return jnp.concatenate([x1 * cos - x2 * sin, x1 * sin + x2 * cos], axis=-1).astype(x.dtype)

def mla_group(c_q, c_kv, k_r, cos, sin, q_norm_g, w_uq, kv_norm_g, w_ukv):
    B, S, _ = c_q.shape
    q = (rms_norm(c_q, q_norm_g) @ w_uq).reshape(B, S, MLA_HEADS, QK_NOPE_DIM + QK_ROPE_DIM)
    q_nope, q_rope = q[..., :QK_NOPE_DIM], q[..., QK_NOPE_DIM:]
    q_rope = apply_rope(q_rope, cos[:, :, None, :], sin[:, :, None, :])
    kv = (rms_norm(c_kv, kv_norm_g) @ w_ukv).reshape(B, S, MLA_HEADS, QK_NOPE_DIM + V_HEAD_DIM)
    k_nope, v = kv[..., :QK_NOPE_DIM], kv[..., QK_NOPE_DIM:]
    k_rope = apply_rope(k_r, cos, sin)
    scale = (QK_NOPE_DIM + QK_ROPE_DIM) ** -0.5
    outs = []
    for start in range(0, S, Q_BLOCK):
        end = start + Q_BLOCK
        s = (jnp.einsum('bqhd,bkhd->bhqk', q_nope[:, start:end], k_nope[:, :end])
             + jnp.einsum('bqhr,bkr->bhqk', q_rope[:, start:end], k_rope[:, :end]))
        q_chunk = jnp.arange(start, end) // CHUNK
        k_chunk = jnp.arange(end) // CHUNK
        mask = k_chunk[None, :] <= q_chunk[:, None]
        s = jnp.where(mask[None, None], s.astype(jnp.float32) * scale, -jnp.inf)
        p = jax.nn.softmax(s, axis=-1).astype(v.dtype)
        outs.append(jnp.einsum('bhqk,bkhd->bqhd', p, v[:, :end]))
    o = jnp.concatenate(outs, axis=1)
    return o.reshape(B, S, MLA_WIDTH)

def conformer_conv_group(u, dw_w, dw_b, norm_g, norm_b):
    a, g = jnp.split(u, 2, axis=-1)
    h = a * jax.nn.sigmoid(g)
    h = jnp.pad(h, ((0, 0), (CONV_TAPS - 1, 0), (0, 0)))
    h = lax.conv_general_dilated(
        h, dw_w[:, None, :], window_strides=(1,), padding='VALID',
        dimension_numbers=('NWC', 'WIO', 'NWC'), feature_group_count=CONV_WIDTH) + dw_b
    h = layer_norm(h, norm_g, norm_b)
    return jax.nn.silu(h)

def hybrid_mixer(x, cos, sin, w_in, b_in, q_norm_g, w_uq, kv_norm_g, w_ukv,
                 dw_w, dw_b, cn_g, cn_b, w_o):
    proj = x @ w_in + b_in
    o1 = Q_LORA_RANK
    o2 = o1 + KV_LORA_RANK
    o3 = o2 + QK_ROPE_DIM
    c_q, c_kv, k_r, u = proj[..., :o1], proj[..., o1:o2], proj[..., o2:o3], proj[..., o3:]
    y_att = mla_group(c_q, c_kv, k_r, cos, sin, q_norm_g, w_uq, kv_norm_g, w_ukv)
    y_conv = conformer_conv_group(u, dw_w, dw_b, cn_g, cn_b)
    return jnp.concatenate([y_att, y_conv], axis=-1) @ w_o

def memory_cross_attention(x, mem, w_q, w_kv, w_o):
    B, S, D = x.shape
    M = mem.shape[1]
    q = (x @ w_q).reshape(B, S, XA_HEADS, XA_HEAD_DIM)
    kv = (mem @ w_kv).reshape(B, M, 2, XA_HEADS, XA_HEAD_DIM)
    k, v = kv[:, :, 0], kv[:, :, 1]
    s = jnp.einsum('bshd,bmhd->bhsm', q, k).astype(jnp.float32) * (XA_HEAD_DIM ** -0.5)
    p = jax.nn.softmax(s, axis=-1).astype(v.dtype)
    o = jnp.einsum('bhsm,bmhd->bshd', p, v).reshape(B, S, D)
    return o @ w_o

def swiglu_ffn(x, w_in, w_down):
    gu = x @ w_in
    g, up = gu[..., :FFN_HIDDEN], gu[..., FFN_HIDDEN:]
    return (jax.nn.silu(g) * up) @ w_down

def first_inputs(seed: int = 0) -> dict:
    key = jax.random.key(seed)
    ks = jax.random.split(key, 32)
    L, D = DEPTH, D_MODEL

    def normal(k, shape, fan_in, scale=1.0):
        return jax.random.normal(k, shape, jnp.float32) * (scale * fan_in ** -0.5)

    def gain(k, shape):
        return 1.0 + 0.02 * jax.random.normal(k, shape, jnp.float32)

    def small(k, shape):
        return 0.02 * jax.random.normal(k, shape, jnp.float32)

    x = jax.random.normal(ks[0], (BATCH, SEQ, D), jnp.float32)
    mem = jax.random.normal(ks[1], (BATCH, MEM_LEN, D), jnp.float32)
    offset = jax.random.randint(ks[2], (BATCH, 1), 0, 4096, dtype=jnp.int32)
    positions = offset + jnp.arange(SEQ, dtype=jnp.int32)[None, :]

    w_uk = normal(ks[7], (L, KV_LORA_RANK, MLA_HEADS, QK_NOPE_DIM), KV_LORA_RANK)
    w_uv = normal(ks[8], (L, KV_LORA_RANK, MLA_HEADS, V_HEAD_DIM), KV_LORA_RANK, BETA)
    mla_w_ukv = jnp.concatenate([w_uk, w_uv], axis=-1).reshape(
        L, KV_LORA_RANK, MLA_HEADS * (QK_NOPE_DIM + V_HEAD_DIM))
    xa_w_k = normal(ks[18], (L, D, D), D)
    xa_w_v = normal(ks[19], (L, D, D), D, BETA)
    xa_w_kv = jnp.concatenate([xa_w_k, xa_w_v], axis=-1)

    return {
        "x": x,
        "mem": mem,
        "positions": positions,
        "mix_w_in": normal(ks[3], (L, D, IN_COLS), D),
        "mix_b_in": small(ks[4], (L, IN_COLS)),
        "mla_q_norm": gain(ks[5], (L, Q_LORA_RANK)),
        "mla_w_uq": normal(ks[6], (L, Q_LORA_RANK, MLA_HEADS * (QK_NOPE_DIM + QK_ROPE_DIM)), Q_LORA_RANK),
        "mla_kv_norm": gain(ks[9], (L, KV_LORA_RANK)),
        "mla_w_ukv": mla_w_ukv,
        "conv_dw_w": normal(ks[10], (L, CONV_TAPS, CONV_WIDTH), CONV_TAPS),
        "conv_dw_b": small(ks[11], (L, CONV_WIDTH)),
        "conv_norm_g": gain(ks[12], (L, CONV_WIDTH)),
        "conv_norm_b": small(ks[13], (L, CONV_WIDTH)),
        "mix_w_o": normal(ks[14], (L, D, D), D, BETA),
        "ln1_g": gain(ks[15], (L, D)),
        "ln1_b": small(ks[16], (L, D)),
        "xa_w_q": normal(ks[17], (L, D, D), D),
        "xa_w_kv": xa_w_kv,
        "xa_w_o": normal(ks[20], (L, D, D), D, BETA),
        "ln2_g": gain(ks[21], (L, D)),
        "ln2_b": small(ks[22], (L, D)),
        "ffn_w_in": normal(ks[23], (L, D, 2 * FFN_HIDDEN), D),
        "ffn_w_down": normal(ks[24], (L, FFN_HIDDEN, D), FFN_HIDDEN, BETA),
        "ln3_g": gain(ks[25], (L, D)),
        "ln3_b": small(ks[26], (L, D)),
    }

def first_block(x, mem, positions, mix_w_in, mix_b_in, mla_q_norm, mla_w_uq, mla_kv_norm,
              mla_w_ukv, conv_dw_w, conv_dw_b, conv_norm_g, conv_norm_b, mix_w_o,
              ln1_g, ln1_b, xa_w_q, xa_w_kv, xa_w_o, ln2_g, ln2_b,
              ffn_w_in, ffn_w_down, ln3_g, ln3_b):
    cos, sin = rope_cos_sin(positions, QK_ROPE_DIM)
    for l in range(DEPTH):
        y = hybrid_mixer(x, cos, sin, mix_w_in[l], mix_b_in[l], mla_q_norm[l], mla_w_uq[l],
                         mla_kv_norm[l], mla_w_ukv[l], conv_dw_w[l], conv_dw_b[l],
                         conv_norm_g[l], conv_norm_b[l], mix_w_o[l])
        x = layer_norm(ALPHA * x + y, ln1_g[l], ln1_b[l])
        y = memory_cross_attention(x, mem, xa_w_q[l], xa_w_kv[l], xa_w_o[l])
        x = layer_norm(ALPHA * x + y, ln2_g[l], ln2_b[l])
        y = swiglu_ffn(x, ffn_w_in[l], ffn_w_down[l])
        x = layer_norm(ALPHA * x + y, ln3_g[l], ln3_b[l])
    return x


DEPTH_2 = 1

GRID_W = 64
CTX_LEN = 256
MIX_WIDTH = D_MODEL
DN_WIDTH = MIX_WIDTH // 2
DN_HEADS = 4
DN_HEAD_DIM = DN_WIDTH // DN_HEADS
N_DIR = 2
CONV_K = 4
POOL_WIDTH = MIX_WIDTH - DN_WIDTH
POOL_WINDOWS = (2, 4, 8, 16)
POOL_GROUPS = len(POOL_WINDOWS)
POOL_GROUP_DIM = POOL_WIDTH // POOL_GROUPS
N_EXPERTS = 16
EC_CAPACITY = 2
EXPERT_FF = D_MODEL
EPS = 1e-6
QKV_COLS = 3 * DN_WIDTH
GATE_COLS = N_DIR * DN_HEADS
STATE_COLS = QKV_COLS + 2 * GATE_COLS
IN_COLS_2 = STATE_COLS + DN_WIDTH + POOL_WIDTH


def rmsnorm(x, g):
    xf = x.astype(jnp.float32)
    y = xf * lax.rsqrt(jnp.mean(xf * xf, axis=-1, keepdims=True) + EPS)
    return (y * g.astype(jnp.float32)).astype(x.dtype)

def l2norm(x):
    xf = x.astype(jnp.float32)
    return xf * lax.rsqrt(jnp.sum(xf * xf, axis=-1, keepdims=True) + EPS)

def adaln_params(cond, w_mod, b_mod):
    return jnp.split(jax.nn.silu(cond) @ w_mod + b_mod, 6, axis=-1)

def modulate(h, shift, scale):
    return h * (1 + scale) + shift

def window_bounds(n, w):
    pos = jnp.arange(n)
    return jnp.clip(pos - w // 2, 0, n), jnp.clip(pos - w // 2 + w, 0, n)

def centred_box_mean(u, rows):
    B_, L, C = u.shape
    uf = u.astype(jnp.float32)
    outs = []
    if rows is None:
        s = jnp.pad(jnp.cumsum(uf, axis=1), ((0, 0), (1, 0), (0, 0)))
        for i, w in enumerate(POOL_WINDOWS):
            sg = s[..., i * POOL_GROUP_DIM:(i + 1) * POOL_GROUP_DIM]
            lo, hi = window_bounds(L, w)
            cnt = (hi - lo).astype(jnp.float32)
            outs.append((jnp.take(sg, hi, axis=1) - jnp.take(sg, lo, axis=1)) / cnt[None, :, None])
        return jnp.concatenate(outs, axis=-1)
    grid = uf.reshape(B_, rows, GRID_W, C)
    s = jnp.pad(jnp.cumsum(jnp.cumsum(grid, axis=1), axis=2), ((0, 0), (1, 0), (1, 0), (0, 0)))
    for i, w in enumerate(POOL_WINDOWS):
        sg = s[..., i * POOL_GROUP_DIM:(i + 1) * POOL_GROUP_DIM]
        lr, hr = window_bounds(rows, w)
        lc, hc = window_bounds(GRID_W, w)
        s_hi = jnp.take(sg, hr, axis=1)
        s_lo = jnp.take(sg, lr, axis=1)
        tot = (jnp.take(s_hi, hc, axis=2) - jnp.take(s_hi, lc, axis=2)
               - jnp.take(s_lo, hc, axis=2) + jnp.take(s_lo, lc, axis=2))
        cnt = ((hr - lr)[:, None] * (hc - lc)[None, :]).astype(jnp.float32)
        outs.append(tot / cnt[None, :, :, None])
    return jnp.concatenate(outs, axis=-1).reshape(B_, L, C)

def pool_mixer(u, pool_w, pool_scale, rows):
    B_, L, _ = u.shape
    m = (centred_box_mean(u, rows) - u.astype(jnp.float32)).astype(u.dtype)
    m = m.reshape(B_, L, POOL_GROUPS, POOL_GROUP_DIM)
    y = jnp.einsum('blgc,gcd->blgd', m, pool_w).reshape(B_, L, POOL_WIDTH)
    return y * pool_scale

def short_conv(x, w):
    C = x.shape[-1]
    return lax.conv_general_dilated(
        x, w[:, None, :], window_strides=(1,),
        padding=[(CONV_K // 2, CONV_K - 1 - CONV_K // 2)],
        dimension_numbers=('NWC', 'WIO', 'NWC'), feature_group_count=C)

def deltanet_inputs(feat_pre, ab_pre, conv_w, a_log, dt_bias):
    B_, L, _ = feat_pre.shape
    feats = jax.nn.silu(short_conv(feat_pre, conv_w))
    heads = lambda t: jnp.transpose(t.reshape(B_, L, DN_HEADS, DN_HEAD_DIM), (0, 2, 1, 3))
    parts = [heads(t) for t in jnp.split(feats, feats.shape[-1] // DN_WIDTH, axis=-1)]
    ab = ab_pre.astype(jnp.float32).reshape(B_, L, 2, N_DIR, DN_HEADS)
    log_a = -jnp.exp(a_log.astype(jnp.float32)) * jax.nn.softplus(ab[:, :, 0] + dt_bias.astype(jnp.float32))
    beta = jax.nn.sigmoid(ab[:, :, 1])
    to_dir = lambda t: jnp.transpose(t, (2, 0, 3, 1))
    return parts, to_dir(log_a), to_dir(beta)

def chunk_gated_delta(q, k, v, log_a, beta, s0):
    B_, H, L, _ = k.shape
    n = L // CHUNK
    f32 = jnp.float32
    blocks = lambda t: t.astype(f32).reshape(B_, H, n, CHUNK, t.shape[-1])
    kc, vc = blocks(k), blocks(v)
    g = jnp.cumsum(log_a.astype(f32).reshape(B_, H, n, CHUNK), axis=-1)
    bc = beta.astype(f32).reshape(B_, H, n, CHUNK, 1)
    idx = jnp.arange(CHUNK)
    incl = idx[:, None] >= idx[None, :]
    decay = jnp.where(incl, jnp.exp(jnp.minimum(g[..., :, None] - g[..., None, :], 0.0)), 0.0)
    k_beta = kc * bc
    m = jnp.where(idx[:, None] > idx[None, :], jnp.einsum('bhnik,bhnjk->bhnij', k_beta, kc) * decay, 0.0)
    eye = jnp.eye(CHUNK, dtype=f32)
    p = -m
    t_inv = eye + p
    for _ in range(CHUNK.bit_length() - 2):
        p = p @ p
        t_inv = t_inv @ (eye + p)
    w_blk = jnp.einsum('bhnij,bhnjk->bhnik', t_inv, k_beta * jnp.exp(g)[..., None])
    u_blk = jnp.einsum('bhnij,bhnjv->bhniv', t_inv, vc * bc)
    g_last = g[..., -1:]
    k_tail = kc * jnp.exp(g_last - g)[..., None]
    s_decay = jnp.exp(g_last)[..., None]
    first = lambda t: jnp.moveaxis(t, 2, 0)

    def advance(s, w_n, u_n, kt_n, sd_n):
        u_new = u_n - jnp.einsum('bhik,bhkv->bhiv', w_n, s)
        return s * sd_n + jnp.einsum('bhik,bhiv->bhkv', kt_n, u_new), u_new

    if q is None:
        def state_step(s, xs):
            s_next, _ = advance(s, *xs)
            return s_next, None
        s_fin, _ = lax.scan(state_step, s0, tuple(map(first, (w_blk, u_blk, k_tail, s_decay))))
        return None, s_fin

    qc = blocks(q)
    q_dec = qc * jnp.exp(g)[..., None]
    qk = jnp.einsum('bhnik,bhnjk->bhnij', qc, kc) * decay

    def out_step(s, xs):
        w_n, u_n, kt_n, sd_n, qd_n, qk_n = xs
        s_next, u_new = advance(s, w_n, u_n, kt_n, sd_n)
        o_n = jnp.einsum('bhik,bhkv->bhiv', qd_n, s) + jnp.einsum('bhij,bhjv->bhiv', qk_n, u_new)
        return s_next, o_n

    s_fin, o = lax.scan(out_step, s0, tuple(map(first, (w_blk, u_blk, k_tail, s_decay, q_dec, qk))))
    return jnp.moveaxis(o, 0, 2).reshape(B_, H, L, -1), s_fin

def bidir_delta(q, k, v, log_a, beta, s0):
    rev = lambda t: None if t is None else jnp.flip(t, axis=2)
    o_f, s_f = chunk_gated_delta(q, k, v, log_a[0], beta[0], s0[0])
    o_b, s_b = chunk_gated_delta(rev(q), rev(k), rev(v), rev(log_a[1]), rev(beta[1]), s0[1])
    o = None if q is None else o_f + rev(o_b)
    return o, (s_f, s_b)

def token_mixer(h, w_in, conv_w, a_log, dt_bias, dn_norm, pool_w, pool_scale, w_out, s0, rows):
    B_, L, _ = h.shape
    proj = h @ w_in
    (q, k, v), log_a, beta = deltanet_inputs(proj[..., :QKV_COLS], proj[..., QKV_COLS:STATE_COLS],
                                             conv_w, a_log, dt_bias)
    q = l2norm(q) * DN_HEAD_DIM ** -0.5
    k = l2norm(k)
    o, states = bidir_delta(q, k, v, log_a, beta, s0)
    o = jnp.transpose(o, (0, 2, 1, 3))
    gate = proj[..., STATE_COLS:STATE_COLS + DN_WIDTH].reshape(B_, L, DN_HEADS, DN_HEAD_DIM)
    o = (rmsnorm(o, dn_norm) * jax.nn.silu(gate.astype(jnp.float32))).astype(h.dtype)
    o = o.reshape(B_, L, DN_WIDTH)
    pooled = pool_mixer(proj[..., STATE_COLS + DN_WIDTH:], pool_w, pool_scale, rows)
    return jnp.concatenate([o, pooled], axis=-1) @ w_out, states

def context_states(h, w_in, conv_w, a_log, dt_bias, s0):
    proj = h @ w_in[:, DN_WIDTH:STATE_COLS]
    (k, v), log_a, beta = deltanet_inputs(proj[..., :2 * DN_WIDTH], proj[..., 2 * DN_WIDTH:],
                                          conv_w[:, DN_WIDTH:], a_log, dt_bias)
    _, states = bidir_delta(None, l2norm(k), v, log_a, beta, s0)
    return states

def expert_choice_ffn(h, w_router, w_gate, w_up, w_down):
    B_, L, D = h.shape
    cap = EC_CAPACITY * L // N_EXPERTS
    aff = jax.nn.softmax((h @ w_router).astype(jnp.float32), axis=-1)
    top_aff, top_idx = lax.top_k(jnp.swapaxes(aff, 1, 2), cap)
    xe = jax.vmap(lambda hb, ib: hb[ib])(h, top_idx)
    hid = jax.nn.silu(jnp.einsum('becd,edf->becf', xe, w_gate)) * jnp.einsum('becd,edf->becf', xe, w_up)
    ye = jnp.einsum('becf,efd->becd', hid, w_down) * top_aff[..., None].astype(h.dtype)
    combine = lambda ib, yb: jnp.zeros((L, D), yb.dtype).at[ib.reshape(-1)].add(yb.reshape(-1, D))
    return jax.vmap(combine)(top_idx, ye)

def second_inputs(seed: int = 0) -> dict:
    key = jax.random.key(seed)
    ks = jax.random.split(key, 21)
    nrm = lambda k, shape, scale: jax.random.normal(k, shape, jnp.float32) * scale
    D = D_MODEL
    dt = jnp.exp(jax.random.uniform(ks[11], (DEPTH_2, N_DIR, DN_HEADS), jnp.float32,
                                    minval=math.log(1e-3), maxval=math.log(1e-1)))
    return {
        'x': nrm(ks[0], (BATCH, SEQ, D), 1.0),
        'c': nrm(ks[1], (BATCH, D), 1.0),
        'ctx': nrm(ks[2], (BATCH, CTX_LEN, D), 1.0),
        'c_ctx': nrm(ks[3], (D,), 1.0),
        'w_mod': nrm(ks[4], (DEPTH_2, D, 6 * D), 0.5 * D ** -0.5),
        'b_mod': nrm(ks[5], (DEPTH_2, 6 * D), 0.01),
        'norm1': 1.0 + nrm(ks[6], (DEPTH_2, D), 0.02),
        'norm2': 1.0 + nrm(ks[7], (DEPTH_2, D), 0.02),
        'w_in': nrm(ks[8], (DEPTH_2, D, IN_COLS_2), D ** -0.5),
        'conv_w': nrm(ks[9], (DEPTH_2, CONV_K, QKV_COLS), CONV_K ** -0.5),
        'a_log': jnp.log(jax.random.uniform(ks[10], (DEPTH_2, N_DIR, DN_HEADS), jnp.float32, minval=1.0, maxval=16.0)),
        'dt_bias': dt + jnp.log(-jnp.expm1(-dt)),
        'dn_norm': 1.0 + nrm(ks[12], (DEPTH_2, DN_HEAD_DIM), 0.02),
        'pool_w': nrm(ks[13], (DEPTH_2, POOL_GROUPS, POOL_GROUP_DIM, POOL_GROUP_DIM), POOL_GROUP_DIM ** -0.5),
        'pool_scale': 1.0 + nrm(ks[14], (DEPTH_2, POOL_WIDTH), 0.1),
        'w_out': nrm(ks[15], (DEPTH_2, MIX_WIDTH, D), MIX_WIDTH ** -0.5),
        'w_router': nrm(ks[16], (DEPTH_2, D, N_EXPERTS), D ** -0.5),
        'w_gate': nrm(ks[17], (DEPTH_2, N_EXPERTS, D, EXPERT_FF), D ** -0.5),
        'w_up': nrm(ks[18], (DEPTH_2, N_EXPERTS, D, EXPERT_FF), D ** -0.5),
        'w_down': nrm(ks[19], (DEPTH_2, N_EXPERTS, EXPERT_FF, D), EXPERT_FF ** -0.5),
        'norm_f': 1.0 + nrm(ks[20], (D,), 0.02),
    }

def second_block(x, c, ctx, c_ctx, w_mod, b_mod, norm1, norm2, w_in, conv_w, a_log, dt_bias, dn_norm,
              pool_w, pool_scale, w_out, w_router, w_gate, w_up, w_down, norm_f):
    rows = x.shape[1] // GRID_W
    zero = jnp.zeros((ctx.shape[0], DN_HEADS, DN_HEAD_DIM, DN_HEAD_DIM), jnp.float32)
    z = ctx
    for l in range(DEPTH_2):
        mix_w = (w_in[l], conv_w[l], a_log[l], dt_bias[l], dn_norm[l], pool_w[l], pool_scale[l], w_out[l])
        csh1, csc1, cg1, csh2, csc2, cg2 = adaln_params(c_ctx, w_mod[l], b_mod[l])
        sh1, sc1, g1, sh2, sc2, g2 = [t[:, None, :] for t in adaln_params(c, w_mod[l], b_mod[l])]
        hz = modulate(rmsnorm(z, norm1[l]), csh1, csc1)
        if l < DEPTH_2 - 1:
            yz, ctx_st = token_mixer(hz, *mix_w, (zero, zero), None)
            z = z + cg1 * yz
            hz2 = modulate(rmsnorm(z, norm2[l]), csh2, csc2)
            z = z + cg2 * expert_choice_ffn(hz2, w_router[l], w_gate[l], w_up[l], w_down[l])
        else:
            ctx_st = context_states(hz, w_in[l], conv_w[l], a_log[l], dt_bias[l], (zero, zero))
        h = modulate(rmsnorm(x, norm1[l]), sh1, sc1)
        y, _ = token_mixer(h, *mix_w, ctx_st, rows)
        x = x + g1 * y
        h = modulate(rmsnorm(x, norm2[l]), sh2, sc2)
        x = x + g2 * expert_choice_ffn(h, w_router[l], w_gate[l], w_up[l], w_down[l])
    return rmsnorm(x, norm_f)


def setup_inputs(seed=0):
    out = dict(first_inputs(seed))
    for name, value in second_inputs(seed + 1).items():
        if name != "x":
            out[name + "_2"] = value
    return out


def reference(
    x, mem, positions, mix_w_in, mix_b_in, mla_q_norm, mla_w_uq, mla_kv_norm, mla_w_ukv,
    conv_dw_w, conv_dw_b, conv_norm_g, conv_norm_b, mix_w_o, ln1_g, ln1_b, xa_w_q, xa_w_kv,
    xa_w_o, ln2_g, ln2_b, ffn_w_in, ffn_w_down, ln3_g, ln3_b, c_2, ctx_2, c_ctx_2, w_mod_2,
    b_mod_2, norm1_2, norm2_2, w_in_2, conv_w_2, a_log_2, dt_bias_2, dn_norm_2, pool_w_2,
    pool_scale_2, w_out_2, w_router_2, w_gate_2, w_up_2, w_down_2, norm_f_2,
):
    x = first_block(
        x, mem, positions, mix_w_in, mix_b_in, mla_q_norm, mla_w_uq, mla_kv_norm, mla_w_ukv,
        conv_dw_w, conv_dw_b, conv_norm_g, conv_norm_b, mix_w_o, ln1_g, ln1_b, xa_w_q, xa_w_kv,
        xa_w_o, ln2_g, ln2_b, ffn_w_in, ffn_w_down, ln3_g, ln3_b,
    )
    return second_block(
        x, c_2, ctx_2, c_ctx_2, w_mod_2, b_mod_2, norm1_2, norm2_2, w_in_2, conv_w_2, a_log_2,
        dt_bias_2, dn_norm_2, pool_w_2, pool_scale_2, w_out_2, w_router_2, w_gate_2, w_up_2,
        w_down_2, norm_f_2,
    )


_drawn_inputs = setup_inputs


def setup_inputs(seed=0):
    import zlib

    import numpy as np

    out = dict(_drawn_inputs(seed))
    spreads = {}
    factors = {'mix_b_in': 7.782,
     'mla_q_norm': 8.0,
     'mla_w_uq': 2.72,
     'mla_kv_norm': 8.0,
     'conv_dw_b': 5.636,
     'conv_norm_g': 8.0,
     'conv_norm_b': 8.0,
     'ctx_2': 4.191,
     'c_ctx_2': 5.528,
     'b_mod_2': 5.238,
     'norm1_2': 8.0,
     'norm2_2': 8.0,
     'dn_norm_2': 8.0,
     'norm_f_2': 2.826}
    for name, (base, spread) in spreads.items():
        noise = np.random.default_rng([zlib.crc32(name.encode()), seed]).standard_normal(out[name].shape)
        drawn = base * np.exp(spread * noise) if base else spread * noise
        out[name] = jnp.asarray(drawn.astype(out[name].dtype))
    for name, factor in factors.items():
        out[name] = (out[name] * factor).astype(out[name].dtype)
    return out
```

```python
from contextlib import ExitStack

import numpy as np

import concourse.bass as bass
from concourse import mybir

F32 = mybir.dt.float32
I32 = mybir.dt.int32
U32 = mybir.dt.uint32
ACT = mybir.ActivationFunctionType
ALU = mybir.AluOpType
AX = mybir.AxisListType.X

P = 128
D = 1024
KT = D // P
S = 512
ST = S // P
MEM = 256
MT = MEM // P
DEPTH = 2
HEADS, NOPE, ROPE, VD = 8, 64, 32, 64
QK = NOPE + ROPE
LORA = 256
CW = 512
CT = CW // P
TAPS = 31
CONV0 = 2 * LORA + ROPE
IN_COLS = CONV0 + 2 * CW
XH, XD = 4, 256
FFN = 2816
FT = FFN // P
ALPHA = (2.0 * DEPTH) ** 0.25
LN_EPS = 1e-5
RMS_EPS = 1e-6
CHUNK = 64
NEG = -1e30
CTX = 256
DH = 4
CONV_K = 4
Q_BMOD, Q_N1, Q_N2, Q_NF, Q_C, Q_CC, Q_PS, Q_DN = 0, 48, 56, 64, 72, 80, 88, 92
NPAR2 = 93
NE, CAP = 16, 64
GRID_W = 64
ROWS = S // GRID_W
WINDOWS = (2, 4, 8, 16)

TWO_PI = 2.0 * np.pi
PI_A = 6.28125
PI_B = float(np.float32(int((TWO_PI - PI_A) * 2 ** 19)) / 2 ** 19)
PI_C = float(TWO_PI - PI_A - PI_B)
ROUND = 1.5 * 2.0 ** 23
PI_MAX = 3.1415925

SLOT = 4352
NSLOT = 3
LAYER_CHUNKS = 33
C_QKV, C_A, C_G, C_UP = 0, 1, 2, 3
C_XKV, C_MO, C_XQ, C_XO, C_FI, C_FD = 4, 8, 10, 12, 14, 25

PB_CQ, PB_KR, PB_A, PB_G, P_QN, P_KVN = 0, 4, 5, 9, 13, 15
P_DWB, P_CNG, P_CNB, P_LN = 17, 21, 25, 29
NPAR = P_LN + 6 * KT

K_ID, K_ONE, K_SWAP = 0, P, 2 * P
K_FREQ = 3 * P
N_FIRST = K_FREQ + 1
K_TRI, K_STRICT = N_FIRST, N_FIRST + 2 * P
K_SAME = K_STRICT + 2 * P
K_HALF = K_SAME + P
K_IOTA = K_HALF + 2 * 2 * DH
K_CNT = K_IOTA + CAP
NCONST = K_CNT + 4 * S
ARENA = 26744


def shape_constants():
    c = np.zeros((P, NCONST), np.float32)
    i = np.arange(P)
    same = (i[:, None] // CHUNK) == (i[None, :] // CHUNK)
    c[:, K_ID:K_ID + P] = np.eye(P)
    c[:, K_ONE:K_ONE + P] = 1.0
    h = ROPE // 2
    for j in range(h):
        c[NOPE + h + j, K_SWAP + NOPE + j] = -1.0
        c[NOPE + j, K_SWAP + NOPE + h + j] = 1.0
    before = i[:, None] <= i[None, :]
    for d, m in enumerate((before, before.T)):
        c[:, K_TRI + d * P:K_TRI + (d + 1) * P] = m & same
        c[:, K_STRICT + d * P:K_STRICT + (d + 1) * P] = m & same & (i[:, None] != i[None, :])
    c[:, K_SAME:K_SAME + P] = same
    for u in range(2 * DH):
        for n in range(2):
            c[:, K_HALF + 2 * u + n] = (i // CHUNK) == (n if u < DH else 1 - n)
    c[:, K_IOTA:K_IOTA + CAP] = np.arange(CAP) + 1
    freq = np.float32(10000.0) ** (-np.arange(0, ROPE, 2, dtype=np.float32) / np.float32(ROPE))
    c[:, K_FREQ] = freq[i % h]
    for g, w in enumerate(WINDOWS):
        def span(n):
            p = np.arange(n)
            return np.clip(p - w // 2 + w, 0, n) - np.clip(p - w // 2, 0, n)
        cnt = (span(ROWS)[:, None] * span(GRID_W)[None, :]).astype(np.float32)
        c[:, K_CNT + g * S:K_CNT + (g + 1) * S] = (np.float32(1.0) / cnt).reshape(1, S)
    return c


class Signal:

    def __init__(self, sem, per):
        self.sem, self.per = sem, per

    def at(self, layer, n):
        return layer * self.per + n


def build(nc, A, out, debug=None):
    with ExitStack() as ctx:
        def sb(name, shape, dt=F32):
            return ctx.enter_context(nc.sbuf_tensor(name, shape, dt))

        def sem(name):
            return ctx.enter_context(nc.semaphore(name))

        def signal(name, per):
            return Signal(sem(name), per)

        banks = ctx.enter_context(nc.psum_tensor("banks", [P, 8, 512], F32))
        ps = [banks[:, i, :] for i in range(8)]
        ring = sb("ring", [P, NSLOT, SLOT])
        xT = sb("xT", [P, KT, S])
        zT = sb("zT", [P, KT, S])
        arena = sb("arena", [P, ARENA])
        consts = sb("consts", [P, N_FIRST])
        cosT = sb("cosT", [P, S])
        sinT = sb("sinT", [P, S])
        squares = sb("squares", [P, 2, S])
        std = sb("std", [P, S])
        gates = sb("gates", [P, 2, S])
        par_rows = sb("par_rows", [P, P])
        tap_rows = sb("tap_rows", [P, P])
        par = sb("par", [P, NPAR])
        taps = sb("taps", [P, TAPS * CT])
        stat = sb("stat", [P, 4, 8])
        eps = sb("eps", [P, 2])

        def view(lo, *shape, of=None):
            n = int(np.prod(shape))
            v = (arena if of is None else of)[:, lo:lo + n]
            if len(shape) == 2:
                return v.rearrange("p (a b) -> p a b", a=shape[0])
            if len(shape) == 3:
                return v.rearrange("p (a b c) -> p a b c", a=shape[0], b=shape[1])
            return v

        BIG = 0
        memT = view(24 * S, KT, MEM)
        hpad = view(24 * S + KT * MEM, CT, TAPS - 1 + S)
        MIX = 24 * S + KT * MEM + CT * (TAPS - 1 + S)
        mixT = view(MIX, KT, S)
        probsT = view(MIX + KT * S, ST, S)
        xk = view(MIX + (KT + ST) * S, KT, MEM)
        xv = view(MIX + (KT + ST) * S + KT * MEM, MT, D)

        ident = consts[:, K_ID:K_ID + P]
        ones = consts[:, K_ONE:K_ONE + P]
        swap = consts[0:QK, K_SWAP:K_SWAP + QK]

        cqkv = view(0, 4, S)
        qh = view(4 * S, HEADS, S)
        kh = view(12 * S, HEADS, S)
        vt = view(20 * S, ST, HEADS * VD)
        xload = view(0, ST, D)
        memload = view(ST * D, MT, D)
        qx = view(0, KT, S)
        ox = view(KT * S, KT, S)
        hidden = view(0, FT, S)
        kr_raw = probsT[:, 0, :]
        rope_a = probsT[:, 2, :]
        rope_b = probsT[:, 3, :]
        probs = zT[:, :, :].rearrange("p (b t) n -> p b t n", b=2)

        loaded = [sem(f"slot{i}_loaded") for i in range(NSLOT)]
        used = sem("chunks_used")
        const_in = sem("const_in")
        x_in = sem("x_in")
        rows_in = sem("rows_in")
        rows_used = sem("rows_used")
        ready = sem("fills_ready")
        turned = sem("inputs_turned")
        turned_out = sem("inputs_turned_out")
        rope_v = sem("rope_angles")
        rope_s = sem("rope_sines")
        par_mm = signal("par_turned", 2)
        par_ev = signal("par_copied", 2)
        proj_mm = signal("proj_mm", 13)
        proj_ev = signal("proj_ev", 5)
        sig_ev = signal("gate_sigmoid", 4)
        glu = signal("glu", 4)
        lsq = signal("lora_squares", 4)
        lsum = signal("lora_sums", 2)
        lstd = signal("lora_std", 2)
        lnorm = signal("lora_normed", 4)
        krot_mm = signal("krot_mm", 1)
        krot = signal("krot_parts", 2)
        kcopy = signal("kr_in_heads", 1)
        up_mm = signal("up_mm", 20)
        q_ev = signal("q_ev", 8)
        kv_ev = signal("kv_ev", 12)
        qrot_mm = signal("qrot_mm", 8)
        qrot_sin = signal("qrot_sin", 8)
        qrot_cos = signal("qrot_cos", 8)
        qrot = signal("qrot", 8)
        sc_mm = signal("scores_mm", 32)
        sc_max = signal("scores_max", 32)
        sc_exp = signal("scores_exp", 32)
        sc_norm = signal("scores_norm", 32)
        pt_mm = signal("probsT_mm", 32)
        pt_ev = signal("probsT_ev", 32)
        pv_mm = signal("pv_mm", 8)
        pv_ev = signal("pv_ev", 8)
        xkv_mm = signal("xkv_mm", 12)
        xkv_ev = signal("xkv_ev", 12)
        conv = signal("conv", CT * TAPS)
        cstat_mm = signal("conv_stat_mm", 1)
        ccen = signal("conv_centred", CT)
        csq = signal("conv_squares", CT)
        cvar = signal("conv_var_mm", CT)
        cstd = signal("conv_std", 1)
        cmul = signal("conv_scaled", CT)
        cout = signal("conv_out", CT)
        res_mm = signal("residual_mm", 3 * KT)
        z_ok = signal("z_summed", 3 * KT)
        mean_mm = signal("mean_mm", 3)
        cen = signal("centred", 3 * KT)
        sq_ok = signal("squared", 3 * KT)
        var_mm = signal("var_mm", 3 * KT)
        std_ok = signal("std_ok", 3)
        scaled = signal("scaled", 3 * KT)
        x_ok = signal("x_normed", 3 * KT)
        xq_mm = signal("xq_mm", KT)
        xq_ev = signal("xq_ev", KT)
        xs_mm = signal("xscores_mm", 8)
        xs_max = signal("xscores_max", 8)
        xs_exp = signal("xscores_exp", 16)
        xs_norm = signal("xscores_norm", 16)
        xt_mm = signal("xprobsT_mm", 8)
        xt_ev = signal("xprobsT_ev", 8)
        xo_mm = signal("xpv_mm", 8)
        xo_ev = signal("xpv_ev", 8)
        ffn_mm = signal("ffn_mm", 2 * FT)
        ffn_act = signal("ffn_silu", FT)
        ffn_ok = signal("ffn_hidden", FT)
        vec = signal("vector_order", 118)
        stored = [sem(f"stored{i}") for i in range(2)]

        at = [0]

        def take(*shape):
            lo = at[0]
            at[0] += int(np.prod(shape))
            return view(lo, *shape)

        NC2 = K_CNT - K_TRI
        c2 = take(NC2)
        tri = c2[:, 0:2 * P].rearrange("p (d n) -> p d n", d=2)
        strict = c2[:, K_STRICT - K_TRI:K_STRICT - K_TRI + 2 * P].rearrange("p (d n) -> p d n", d=2)
        same = c2[:, K_SAME - K_TRI:K_SAME - K_TRI + P]
        half = c2[:, K_HALF - K_TRI:K_HALF - K_TRI + 4 * DH].rearrange("p (u c) -> p u c", c=2)
        iota = c2[:, K_IOTA - K_TRI:K_IOTA - K_TRI + CAP]
        par2 = take(NPAR2)
        taps2 = take(CONV_K * 3 * DH)
        mod = take(6 * KT, 2)
        cond = take(KT, 2)
        gain = take(4, KT)
        a_log = take(2 * DH)
        dt_bias = take(2 * DH)
        w_rt = take(KT, NE)
        NT = (CTX + S) // P
        U8 = 2 * DH
        ab = take(NT, 2, U8)
        sp_s = take(NT * U8)
        sp_e = take(NT * U8)
        la = take(NT, U8)
        la_half = take(NT * U8, 2)
        beta = take(NT, U8)
        nbeta = take(NT, U8)
        eg = take(NT, U8)
        gsum = take(NT, U8)
        beg = take(NT, U8)
        tail = take(NT, U8)
        tail_half = take(NT * U8, 2)
        sdec = take(NT * U8, 2)
        PHASE = at[0]
        kT = take(DH, NT * P)
        vT = take(DH, NT * P)
        qT = take(DH, S)
        gateT = take(DH, S)
        mix2 = take(KT, S)
        SCRATCH = at[0]
        hz = take(KT, CTX)
        ctx_in = take(CTX // P, D)
        PRE = S + CTX + 2 * (CONV_K - 1)
        pre = take(2, PRE)
        acc = take(2, PRE)
        pool_w = take(4, P)
        u = take(4, S)
        assert at[0] <= ARENA
        ctxT = view(SCRATCH + 2 * KT * CTX, KT, CTX)
        pool_a = mix2[:, 0:DH, :].rearrange("p a n -> p (a n)")
        pool_b = ctx_in.rearrange("p a n -> p (a n)")
        inv_cnt = mix2[:, DH:, :]
        at[0] = SCRATCH
        E, ETS, ETI, EG, KBG, KT0, KT1, VB, PA, PB = [take(U8, P) for _ in range(10)]
        assert at[0] <= ARENA
        zf = zT.rearrange("p a n -> p (a n)")
        PTA, PTB, TT, ST8 = [view(i * U8 * P, U8, P, of=zf) for i in range(4)]
        SD = squares.rearrange("p a (u n) -> p (a u) n", n=P)
        head_dev = view(SCRATCH, DH, S)
        at[0] = PHASE
        ye = take(NE // 2, D)
        h_tok = view(PHASE, ST, D)
        sel = view(PHASE + ST * D, ST, NE * CAP)
        at[0] = PHASE + 2 * ST * D
        sel_w = view(at[0], ST, NE * CAP)
        xs = view(at[0], 2, KT, CAP)
        hid = view(at[0] + 2 * KT * CAP, 2, D)
        hidT = view(at[0] + 2 * KT * CAP + 2 * D, 2, KT, CAP)
        at[0] += ST * D
        xeT = take(KT, NE * CAP)
        sel_wT = take(NE // 2, S)
        assert at[0] <= ARENA
        aff = gates[:, 0, 0:ST * NE].rearrange("p (t e) -> p t e", e=NE)
        pos = gates[:, 1, 0:ST * NE].rearrange("p (t e) -> p t e", e=NE)
        out_tok = view(PHASE, 2, D)

        def pair(i):
            return banks[:, 2 * i:2 * i + 2, :].rearrange("p b (h n) -> p (b h) n", n=P)

        def tile_of(step, d):
            n0, n1 = CTX // P, NT
            if d == 0:
                return step
            return n0 - 1 - step if step < n0 else n0 + n1 - 1 - step

        small_in = sem("small_in")
        p2_mm, p2_ev = sem("params2_turned"), sem("params2_copied")
        ctx_mm, ctx_ev = sem("ctx_turned"), sem("ctx_copied")
        cond_ok, mod_mm, mod_ok = sem("cond_silu"), sem("mod_mm"), sem("mod_ok")
        n_sq, n_mm, n_std, n_mul, n_out = (sem(f"rms_{x}") for x in ("squared", "summed", "std", "scaled", "out"))
        pj_mm, pj_ev = sem("in_proj_mm"), sem("in_proj_out")
        cv_ok, cv_out = sem("short_conv"), sem("short_conv_silu")
        l2_sq, l2_mm, l2_std, l2_ok = (sem(f"l2_{x}") for x in ("squared", "summed", "std", "ok"))
        ab_a, ab_v, ab_mm = sem("decay_act"), sem("decay_vec"), sem("decay_mm")
        pl_ok, pl_mm, pl_ev = sem("pool_step"), sem("pool_mm"), sem("pool_out")
        vec2 = sem("vector_order2")
        padded = sem("short_conv_padded")
        wo_mm, wo_ok = sem("out_proj_mm"), sem("out_proj_ok")
        rt_mm, rt_v, rt_a = sem("router_mm"), sem("router_vec"), sem("router_act")
        ht_mm, ht_ev = sem("h_turned"), sem("h_copied")
        se_ok, sw_ok = sem("slots_known"), sem("slots_weighted")
        xe_mm, xe_ev = sem("gathered_mm"), sem("gathered")
        sw_mm, sw_ev = sem("slots_turned"), sem("slots_copied")
        ex_x = Signal(sem("expert_tokens"), 2)
        ex_gu = Signal(sem("expert_gate_up"), 8)
        ex_silu = Signal(sem("expert_silu"), 4)
        ex_hid = Signal(sem("expert_hidden"), 4)
        ex_tm = Signal(sem("expert_hidden_turned"), 4)
        ex_ht = Signal(sem("expert_hidden_copied"), 4)
        ex_ye = Signal(sem("expert_out"), 4)
        cb_mm, cb_ok = sem("combine_mm"), sem("combine_ok")
        fin_mm, fin_ev = sem("out_turned"), sem("out_copied")

        def events(step):
            x = step >= CTX // P
            r5 = range(1, 6)
            return {
                "pe": ["G", "KK"] + x * ["QK"] + ["KTOK", "VTOK", "L", "PT"]
                + [f"{n}{r}" for r in r5 for n in (("SQ", "SQT", "TT") if r < 5 else ("SQ", "TT"))]
                + ["WT", "U", "WS0"] + x * ["Y0"] + ["SU0", "WS1"] + x * ["Y1"] + ["SU1"] + x * ["X"],
                "dve": ["TRILA", "SUB", "MIN", "LT"] + x * ["QKD"] + ["PM", "TT0"]
                + [f"{n}{r}" for r in r5 for n in (("SQT", "TT") if r < 5 else ("TT",))]
                + ["U"] + [f"{n}{c}" for c in (0, 1) for n in ("UF", "UB", "S")] + x * ["Y0", "X0", "Y1", "X1"],
                "act": ["E"] + x * ["EG"] + ["KTOK", "VTOK", "PT"] + [f"SQ{r}" for r in r5] + ["WT"],
                "pool": ["ETS", "ETI"] + x * ["QD"] + ["KBG", "KT0", "KT1", "VB", "SD0", "SD1"],
            }

        class Delta:

            def __init__(self):
                self.sem = {e: sem(f"delta_{e}") for e in ("pe", "dve", "act", "pool")}
                self.value = {}
                n = {e: 0 for e in self.sem}
                for step in range(NT):
                    for e, names in events(step).items():
                        for name in names:
                            n[e] += 1
                            self.value[e, step, name] = n[e]
                self.said = {e: 0 for e in self.sem}

            def says(self, e, step, name, ins):
                self.said[e] += 1
                assert self.value[e, step, name] == self.said[e], (e, step, name)
                ins.then_inc(self.sem[e], 1)

            def wait(self, eng, e, step, name):
                eng.wait_ge(self.sem[e], self.value[e, step, name])

            def last(self, e):
                return max(v for (x, _, _), v in self.value.items() if x == e)

        delta = Delta()
        POOL_STEPS = list(np.cumsum([6 + 2 * int(np.log2(win)) for win in WINDOWS]))
        POOL_STEPS = [int(n) for n in POOL_STEPS] + [int(POOL_STEPS[-1]) + 1]
        ROUNDS = CAP // 8
        POS_KNOWN = 5 + 1 + 2 * ROUNDS + 3
        LAYERS_DONE = DEPTH * x_ok.per
        C2 = DEPTH * LAYER_CHUNKS
        C_MOD, C_IN, C_OUT2, C_EXP = C2, C2 + 12, C2 + 17, C2 + 19
        DW = DH * P
        IN_RANGES = ((3 * DW + 16 + DW, 4 * DW + 16 + DW), (DW, 2 * DW), (2 * DW, 3 * DW + 16), (0, DW),
                     (3 * DW + 16, 4 * DW + 16))
        EXP_CHUNKS = 6

        def slot(c):
            return c % NSLOT

        def w(c, lo, *shape):
            n = int(np.prod(shape))
            v = ring[:, slot(c), lo:lo + n]
            if len(shape) == 2:
                return v.rearrange("p (a b) -> p a b", a=shape[0])
            return v.rearrange("p (a b c) -> p a b c", a=shape[0], b=shape[1])

        block = ctx.enter_context(nc.Block())

        @block.sync
        def _(sp):
            sp.dma_start(consts[:, :], A["consts"][:, 0:N_FIRST]).then_inc(const_in, 16)
            sp.dma_start(rope_a.bitcast(I32), A["positions"].broadcast_to([P, S])).then_inc(const_in, 16)
            sp.dma_start(xload, A["x"][0].rearrange("(t p) d -> p t d", p=P)).then_inc(x_in, 16)
            sp.dma_start(memload, A["mem"][0].rearrange("(t p) d -> p t d", p=P)).then_inc(x_in, 16)
            sp.wait_ge(ready, 2)

            with sp.Fori(0, DEPTH) as l:
                def layer(name):
                    return A[name][bass.ds(l, 1)]

                def row(dst, name, lo, n):
                    src = layer(name)[:, lo:lo + n * P].rearrange("a (r c) -> (a r) c", c=P)
                    sp.dma_start(par_rows[dst:dst + n, :], src).then_inc(rows_in, 16)

                def load(c, halves):
                    sp.wait_ge(used, l * LAYER_CHUNKS + c + 1)
                    for dst, src in halves:
                        sp.dma_start(dst, src).then_inc(loaded[slot(c)], 16)

                def matrix(c, name, lo, n, lo2=None):
                    src = layer(name).rearrange("a (k p) n -> p (a k) n", p=P)
                    m = KT // 2
                    if lo2 is None:
                        dst = w(c, 0, KT, n)
                        load(c, [(dst[:, h * m:(h + 1) * m], src[:, h * m:(h + 1) * m, lo:lo + n])
                                 for h in range(2)])
                    else:
                        load(c, [(w(c, h * KT * n, KT, n), src[:, :, at:at + n])
                                 for h, at in enumerate((lo, lo2))])

                matrix(C_QKV, "mix_w_in", 0, CONV0)
                sp.wait_ge(rows_used, l + 1)
                row(PB_CQ, "mix_b_in", 0, 4)
                sp.dma_start(par_rows[PB_KR:PB_KR + 1, 0:QK],
                             layer("mix_b_in")[:, CONV0 - QK:CONV0]).then_inc(rows_in, 16)
                row(PB_A, "mix_b_in", CONV0, 2 * CT)
                row(P_QN, "mla_q_norm", 0, 2)
                row(P_KVN, "mla_kv_norm", 0, 2)
                row(P_DWB, "conv_dw_b", 0, CT)
                row(P_CNG, "conv_norm_g", 0, CT)
                row(P_CNB, "conv_norm_b", 0, CT)
                for j, name in enumerate(("ln1_g", "ln1_b", "ln2_g", "ln2_b", "ln3_g", "ln3_b")):
                    row(P_LN + j * KT, name, 0, KT)
                sp.dma_start(tap_rows[0:TAPS * CT, :],
                             layer("conv_dw_w").rearrange("a k (t p) -> (a k t) p", p=P)).then_inc(rows_in, 16)
                matrix(C_A, "mix_w_in", CONV0, CW)
                matrix(C_G, "mix_w_in", CONV0 + CW, CW)
                nq, nkv = HEADS * QK, HEADS * (NOPE + VD)
                load(C_UP, [(w(C_UP, 0, 2, nq), layer("mla_w_uq").rearrange("a (k p) n -> p (a k) n", p=P)),
                            (w(C_UP, 2 * nq, 2, nkv), layer("mla_w_ukv").rearrange("a (k p) n -> p (a k) n", p=P))])
                for j in range(4):
                    matrix(C_XKV + j, "xa_w_kv", j * 512, 512)
                for j in range(2):
                    matrix(C_MO + j, "mix_w_o", j * 512, 512)
                for j in range(2):
                    matrix(C_XQ + j, "xa_w_q", j * 512, 512)
                for j in range(2):
                    matrix(C_XO + j, "xa_w_o", j * 512, 512)
                for j in range(FT // 2):
                    matrix(C_FI + j, "ffn_w_in", j * 2 * P, 2 * P, FFN + j * 2 * P)
                down = layer("ffn_w_down").rearrange("a (k p) n -> p (a k) n", p=P)
                for j in range(KT):
                    dst = w(C_FD + j, 0, FT, P)
                    load(C_FD + j, [(dst[:, h * FT // 2:(h + 1) * FT // 2],
                                     down[:, h * FT // 2:(h + 1) * FT // 2, j * P:(j + 1) * P]) for h in range(2)])
            sp.wait_ge(rows_used, DEPTH + 1)
            for dst, name, n in ((Q_BMOD, "b_mod_2", 6 * KT), (Q_N1, "norm1_2", KT), (Q_N2, "norm2_2", KT),
                                 (Q_C, "c_2", KT), (Q_PS, "pool_scale_2", 4), (Q_DN, "dn_norm_2", 1)):
                sp.dma_start(par_rows[dst:dst + n, :], A[name].rearrange("a (r c) -> (a r) c", c=P)).then_inc(small_in, 16)
            for dst, name in ((Q_NF, "norm_f_2"), (Q_CC, "c_ctx_2")):
                sp.dma_start(par_rows[dst:dst + KT, :], A[name].rearrange("(r c) -> r c", c=P)).then_inc(small_in, 16)
            sp.dma_start(tap_rows[0:CONV_K * 3 * DH, :],
                         A["conv_w_2"].rearrange("a k (t p) -> (a k t) p", p=P)).then_inc(small_in, 16)

            def load2(c, halves):
                sp.wait_ge(used, c + 1)
                for dst, src in halves:
                    sp.dma_start(dst, src).then_inc(loaded[slot(c)], 16)

            def matrix2(c, src, lo, hi):
                src = src.rearrange("(k p) n -> p k n", p=P)
                dst, m = w(c, 0, KT, hi - lo), KT // 2
                load2(c, [(dst[:, h * m:(h + 1) * m], src[:, h * m:(h + 1) * m, lo:hi]) for h in range(2)])

            for j in range(NSLOT):
                matrix2(C_MOD + j, A["w_mod_2"][0], j * 512, (j + 1) * 512)
            sp.wait_ge(x_ok.sem, LAYERS_DONE)
            sp.dma_start(c2, A["consts"][:, K_TRI:K_CNT]).then_inc(small_in, 16)
            sp.dma_start(inv_cnt, A["consts"][:, K_CNT:].rearrange("p (g n) -> p g n", g=4)).then_inc(small_in, 16)
            sp.dma_start(a_log, A["a_log_2"].rearrange("a d h -> a (d h)").broadcast_to([P, U8])).then_inc(small_in, 16)
            sp.dma_start(dt_bias, A["dt_bias_2"].rearrange("a d h -> a (d h)").broadcast_to([P, U8])).then_inc(small_in, 16)
            sp.dma_start(w_rt, A["w_router_2"][0].rearrange("(k p) n -> p k n", p=P)).then_inc(small_in, 16)
            sp.dma_start(pool_w, A["pool_w_2"][0].rearrange("g c d -> c g d")).then_inc(small_in, 16)
            sp.dma_start(ctx_in, A["ctx_2"][0].rearrange("(t p) d -> p t d", p=P)).then_inc(small_in, 16)
            for j in range(NSLOT, 12):
                matrix2(C_MOD + j, A["w_mod_2"][0], j * 512, (j + 1) * 512)
            for j, (lo, hi) in enumerate(IN_RANGES):
                matrix2(C_IN + j, A["w_in_2"][0], lo, hi)
            for j in range(2):
                matrix2(C_OUT2 + j, A["w_out_2"][0], j * 512, (j + 1) * 512)
            with sp.Fori(0, NE) as e:
                for i in range(EXP_CHUNKS):
                    c = C_EXP + i
                    sp.wait_ge(used, e * EXP_CHUNKS + c + 1)
                    name = ("w_gate_2", "w_up_2", "w_gate_2", "w_up_2", "w_down_2", "w_down_2")[i]
                    src = A[name][0][bass.ds(e, 1)].rearrange("a (k p) n -> p (a k) n", p=P)
                    for h in range(2):
                        if i < 4:
                            dst, n0 = w(c, 0, KT, 512)[:, 4 * h:4 * h + 4], (i // 2) * 512
                            sp.dma_start(dst, src[:, 4 * h:4 * h + 4, n0:n0 + 512]).then_inc(loaded[slot(c)], 16)
                        else:
                            k0 = 4 * (i - 4) + 2 * h
                            sp.dma_start(w(c, 0, KT // 2, D)[:, 2 * h:2 * h + 2], src[:, k0:k0 + 2])\
                                .then_inc(loaded[slot(c)], 16)
            for t in range(ST):
                sp.wait_ge(fin_ev, 2 * (t + 1))
                sp.dma_start(out[0, t * P:(t + 1) * P, :], out_tok[:, t % 2, :]).then_inc(stored[t % 2], 16)
            for i in range(2):
                sp.wait_ge(stored[i], 16 * ST // 2)

        @block.tensor
        def _(pe):
            pe.sem_inc(used, NSLOT)
            pe.sem_inc(rows_used, 1)
            pe.wait_ge(const_in, 32)
            pe.wait_ge(x_in, 32)
            for f in range(2 * KT):
                if f >= 4:
                    pe.wait_ge(turned_out, f - 3)
                src, n = (xload, ST) if f < KT else (memload, MT)
                for t in range(n):
                    mm = pe.transpose(ps[f % 4][:, t * P:(t + 1) * P],
                                      src[:, t, (f % KT) * P:(f % KT + 1) * P], ident)
                mm.then_inc(turned, 1)
            pe.wait_ge(turned_out, 2 * KT)

            with pe.Fori(0, DEPTH) as l:
                def arrived(c):
                    per = LAYER_CHUNKS // NSLOT
                    pe.wait_ge(loaded[slot(c)], l * (32 * per) + 32 * (c // NSLOT + 1))

                spent = [0]

                def give_back(n):
                    spent[0] += n

                def say_spent(mm):
                    if spent[0]:
                        mm.then_inc(used, spent[0])
                        spent[0] = 0

                def product(bank, weights, rhs, n=KT, width=S, m=P):
                    for k in range(n):
                        mm = pe.matmul(bank[0:m, 0:width], weights(k), rhs(k), start=(k == 0), stop=(k == n - 1))
                        if k == 0:
                            say_spent(mm)
                    return mm

                def residual(i, weights, rhs, n, chunk, per_chunk):
                    for t in range(KT):
                        if t % per_chunk == 0:
                            arrived(chunk + t // per_chunk)
                        if t >= 4:
                            pe.wait_ge(z_ok.sem, z_ok.at(l, i * KT + t - 3))
                        mm = product(ps[4 + t % 4], lambda k: weights(t, k), rhs, n)
                        mm.then_inc(res_mm.sem, 1)
                        if t % per_chunk == per_chunk - 1:
                            give_back(1)

                def norm_sums(i):
                    for t in range(KT):
                        pe.wait_ge(z_ok.sem, z_ok.at(l, i * KT + t + 1))
                        mm = pe.matmul(ps[0][:, :], ones, zT[:, t, :], start=(t == 0), stop=(t == KT - 1))
                        if t == 0:
                            say_spent(mm)
                    mm.then_inc(mean_mm.sem, 1)
                    for t in range(KT):
                        pe.wait_ge(sq_ok.sem, sq_ok.at(l, i * KT + t + 1))
                        mm = pe.matmul(ps[1][:, :], ones, squares[:, t % 2, :], start=(t == 0), stop=(t == KT - 1))
                        mm.then_inc(var_mm.sem, 1)

                pe.wait_ge(rows_in, l * (15 * 16) + 15 * 16)
                pe.transpose(ps[6][:, 0:P], par_rows[:, :], ident).then_inc(par_mm.sem, 1)
                pe.transpose(ps[7][:, 0:P], tap_rows[:, :], ident).then_inc(par_mm.sem, 1)
                pe.wait_ge(par_ev.sem, par_ev.at(l, 2))
                pe.sem_inc(rows_used, 1)

                arrived(C_QKV)
                wq = w(C_QKV, 0, KT, CONV0)
                for n in range(5):
                    lo, m = (n * P, P) if n < 4 else (CONV0 - QK, QK)
                    mm = product(ps[n], lambda k: wq[:, k, lo:lo + m], lambda k: xT[:, k, :], m=m)
                    mm.then_inc(proj_mm.sem, 1)
                give_back(1)
                arrived(C_A)
                arrived(C_G)
                for t in range(CT):
                    for j in range(2):
                        n = 5 + 2 * t + j
                        if n >= 8:
                            pe.wait_ge(proj_ev.sem, proj_ev.at(l, n - 7))
                        wc = w(C_A + j, 0, KT, CW)
                        mm = product(ps[n % 8], lambda k: wc[:, k, t * P:(t + 1) * P], lambda k: xT[:, k, :])
                        mm.then_inc(proj_mm.sem, 1)
                give_back(2)

                pe.wait_ge(glu.sem, glu.at(l, 2))
                for n in range(2):
                    for k in range(2):
                        pe.wait_ge(lsq.sem, lsq.at(l, 2 * n + k + 1))
                        mm = pe.matmul(ps[5 + n][:, :], ones, mixT[:, 2 * n + k, :], start=(k == 0), stop=(k == 1))
                    mm.then_inc(lsum.sem, 1)
                pe.wait_ge(proj_ev.sem, proj_ev.at(l, 5))
                pe.matmul(ps[7][0:QK, :], swap, kr_raw[0:QK, :], start=True, stop=True).then_inc(krot_mm.sem, 1)

                arrived(C_UP)
                wuq = w(C_UP, 0, 2, HEADS * QK)
                wukv = w(C_UP, 2 * HEADS * QK, 2, HEADS * (NOPE + VD))
                wv = w(C_UP, 2 * HEADS * QK, 2, HEADS, NOPE + VD)
                pe.wait_ge(glu.sem, glu.at(l, CT))
                pe.wait_ge(lnorm.sem, lnorm.at(l, 2))
                for h in range(HEADS):
                    if h == 7:
                        pe.wait_ge(krot.sem, krot.at(l, 2))
                    if h == 5:
                        pe.wait_ge(lnorm.sem, lnorm.at(l, 4))
                    mm = product(ps[h], lambda k: wuq[:, k, h * QK:(h + 1) * QK], lambda k: cqkv[:, k, :], 2, m=QK)
                    mm.then_inc(up_mm.sem, 1)
                for h in range(HEADS):
                    pe.wait_ge(q_ev.sem, q_ev.at(l, h + 1))
                    lo = h * (NOPE + VD)
                    mm = product(ps[h], lambda k: wukv[:, k, lo:lo + NOPE], lambda k: cqkv[:, 2 + k, :], 2, m=NOPE)
                    mm.then_inc(up_mm.sem, 1)
                for t in range(ST):
                    pe.wait_ge(kv_ev.sem, kv_ev.at(l, t + 1))
                    mm = product(ps[t], lambda k: cqkv[:, 2 + k, t * P:(t + 1) * P], lambda k: wv[:, k, :, NOPE:], 2)
                    mm.then_inc(up_mm.sem, 1)
                give_back(1)
                for h in range(HEADS):
                    b = 4 + h % 4
                    pe.wait_ge(kv_ev.sem, kv_ev.at(l, 5 + h % 4))
                    if h >= 4:
                        pe.wait_ge(qrot_sin.sem, qrot_sin.at(l, h - 3))
                    pe.matmul(ps[b][0:QK, :], swap, qh[0:QK, h, :], start=True, stop=True).then_inc(qrot_mm.sem, 1)

                sc_bank = (0, 1, 6, 7)

                def scores(h):
                    pe.wait_ge(qrot.sem, qrot.at(l, h + 1))
                    for t in range(ST):
                        n = h * ST + t
                        if n == 0:
                            pe.wait_ge(kv_ev.sem, kv_ev.at(l, 12))
                            pe.wait_ge(kcopy.sem, kcopy.at(l, 1))
                            pe.wait_ge(qrot_sin.sem, qrot_sin.at(l, HEADS))
                        if n >= 4:
                            pe.wait_ge(sc_exp.sem, sc_exp.at(l, n - 3))
                        pe.matmul(ps[sc_bank[t]][:, 0:(t + 1) * P], qh[0:QK, h, t * P:(t + 1) * P],
                                  kh[0:QK, h, 0:(t + 1) * P], start=True, stop=True).then_inc(sc_mm.sem, 1)

                def values(h):
                    for kt in range(ST):
                        n = h * ST + kt
                        if n >= 2:
                            pe.wait_ge(pt_ev.sem, pt_ev.at(l, n - 1))
                        for t in range(kt, ST):
                            if kt == 0:
                                pe.wait_ge(sc_norm.sem, sc_norm.at(l, h * ST + t + 1))
                            mm = pe.transpose(ps[2 + n % 2][:, t * P:(t + 1) * P],
                                              probs[:, h % 2, t, kt * P:(kt + 1) * P], ident)
                        mm.then_inc(pt_mm.sem, 1)
                    if h >= 2:
                        pe.wait_ge(pv_ev.sem, pv_ev.at(l, h - 1))
                    for kt in range(ST):
                        pe.wait_ge(pt_ev.sem, pt_ev.at(l, h * ST + kt + 1))
                        mm = pe.matmul(ps[4 + h % 2][0:VD, kt * P:S], vt[:, kt, h * VD:(h + 1) * VD],
                                       probsT[:, kt, kt * P:S], start=(kt == 0), stop=(kt == ST - 1))
                    mm.then_inc(pv_mm.sem, 1)

                for h in range(HEADS + 1):
                    if h < HEADS:
                        scores(h)
                    if h >= 1:
                        values(h - 1)

                pe.wait_ge(sc_exp.sem, sc_exp.at(l, 32))
                for n in range(12):
                    b = sc_bank[n % 4]
                    c = C_XKV + (n // 4 if n < 8 else 2 + (n - 8) % 2)
                    if n in (0, 4, 8, 9):
                        arrived(c)
                    if n >= 4:
                        pe.wait_ge(xkv_ev.sem, xkv_ev.at(l, n - 3))
                    wkv = w(c, 0, KT, 512)
                    if n < 8:
                        mm = product(ps[b], lambda k: wkv[:, k, (n % 4) * P:(n % 4 + 1) * P],
                                     lambda k: memT[:, k, :], width=MEM)
                    else:
                        t = (n - 8) // 2
                        mm = product(ps[b], lambda k: memT[:, k, t * P:(t + 1) * P], lambda k: wkv[:, k, :])
                    mm.then_inc(xkv_mm.sem, 1)
                    if n in (3, 7):
                        give_back(1)
                give_back(2)

                pe.wait_ge(pt_ev.sem, pt_ev.at(l, 32))
                for t in range(CT):
                    pe.wait_ge(conv.sem, conv.at(l, CT * (TAPS - 1) + t + 1))
                    mm = pe.matmul(ps[2][:, :], ones, mixT[:, CT + t, :], start=(t == 0), stop=(t == CT - 1))
                mm.then_inc(cstat_mm.sem, 1)
                for t in range(CT):
                    pe.wait_ge(csq.sem, csq.at(l, t + 1))
                    mm = pe.matmul(ps[3][:, :], ones, squares[:, t % 2, :], start=(t == 0), stop=(t == CT - 1))
                    mm.then_inc(cvar.sem, 1)

                pe.wait_ge(pv_ev.sem, pv_ev.at(l, HEADS))
                pe.wait_ge(xkv_ev.sem, xkv_ev.at(l, 12))
                pe.wait_ge(cout.sem, cout.at(l, CT))
                residual(0, lambda t, k: w(C_MO + t // 4, 0, KT, 512)[:, k, (t % 4) * P:(t % 4 + 1) * P],
                         lambda k: mixT[:, k, :], KT, C_MO, 4)
                norm_sums(0)

                pe.wait_ge(x_ok.sem, x_ok.at(l, KT))
                for t in range(KT):
                    if t % 4 == 0:
                        arrived(C_XQ + t // 4)
                    if t >= 4:
                        pe.wait_ge(xq_ev.sem, xq_ev.at(l, t - 3))
                    wx = w(C_XQ + t // 4, 0, KT, 512)
                    mm = product(ps[2 + t % 4], lambda k: wx[:, k, (t % 4) * P:(t % 4 + 1) * P], lambda k: xT[:, k, :])
                    mm.then_inc(xq_mm.sem, 1)
                    if t % 4 == 3:
                        give_back(1)

                def xscores(h):
                    pe.wait_ge(xq_ev.sem, xq_ev.at(l, min(2 * h + 2, KT)))
                    for j in range(2):
                        n = 2 * h + j
                        if n >= 4:
                            pe.wait_ge(xs_exp.sem, xs_exp.at(l, 2 * (n - 3)))
                        for i in range(2):
                            t = 2 * j + i
                            for k in range(2):
                                mm = pe.matmul(ps[sc_bank[n % 4]][:, i * MEM:(i + 1) * MEM],
                                               qx[:, 2 * h + k, t * P:(t + 1) * P], xk[:, 2 * h + k, :],
                                               start=(k == 0), stop=(k == 1))
                        mm.then_inc(xs_mm.sem, 1)

                def xvalues(h):
                    for kt in range(MT):
                        n = 2 * h + kt
                        if n >= 2:
                            pe.wait_ge(xt_ev.sem, xt_ev.at(l, n - 1))
                        else:
                            pe.wait_ge(xq_ev.sem, xq_ev.at(l, KT))
                        for t in range(ST):
                            if kt == 0:
                                pe.wait_ge(xs_norm.sem, xs_norm.at(l, ST * h + t + 1))
                            mm = pe.transpose(ps[2 + kt][:, t * P:(t + 1) * P],
                                              probs[:, h % 2, t, kt * P:(kt + 1) * P], ident)
                        mm.then_inc(xt_mm.sem, 1)
                    for v in range(2):
                        n = 2 * h + v
                        if n >= 2:
                            pe.wait_ge(xo_ev.sem, xo_ev.at(l, n - 1))
                        for kt in range(MT):
                            pe.wait_ge(xt_ev.sem, xt_ev.at(l, 2 * h + kt + 1))
                            mm = pe.matmul(ps[4 + v][:, :], xv[:, kt, h * XD + v * P:h * XD + (v + 1) * P],
                                           probsT[:, kt, :], start=(kt == 0), stop=(kt == MT - 1))
                        mm.then_inc(xo_mm.sem, 1)

                for h in range(XH + 1):
                    if h < XH:
                        xscores(h)
                    if h >= 1:
                        xvalues(h - 1)
                pe.wait_ge(xo_ev.sem, xo_ev.at(l, KT))
                residual(1, lambda t, k: w(C_XO + t // 4, 0, KT, 512)[:, k, (t % 4) * P:(t % 4 + 1) * P],
                         lambda k: ox[:, k, :], KT, C_XO, 4)
                norm_sums(1)

                pe.wait_ge(x_ok.sem, x_ok.at(l, 2 * KT))
                for t in range(FT):
                    c = C_FI + t // 2
                    if t % 2 == 0:
                        arrived(c)
                    if t >= 4:
                        pe.wait_ge(ffn_ok.sem, ffn_ok.at(l, t - 3))
                    for j in range(2):
                        wf = w(c, j * KT * 2 * P, KT, 2 * P)
                        mm = product(ps[2 * (t % 4) + j], lambda k: wf[:, k, (t % 2) * P:(t % 2 + 1) * P],
                                     lambda k: xT[:, k, :])
                        mm.then_inc(ffn_mm.sem, 1)
                    if t % 2 == 1:
                        give_back(1)
                pe.wait_ge(ffn_ok.sem, ffn_ok.at(l, FT))
                residual(2, lambda t, k: w(C_FD + t, 0, FT, P)[:, k, :], lambda k: hidden[:, k, :], FT, C_FD, 1)
                norm_sums(2)
                pe.wait_ge(x_ok.sem, x_ok.at(l, 3 * KT))

            def arrived2(c):
                pe.wait_ge(loaded[slot(c)], 32 * (c // NSLOT + 1))

            spent = [0]

            def give_back(n):
                spent[0] += n

            def say_spent(mm):
                if spent[0]:
                    mm.then_inc(used, spent[0])
                    spent[0] = 0

            def product(out, weights, rhs, n=KT):
                for k in range(n):
                    mm = pe.matmul(out, weights(k), rhs(k), start=(k == 0), stop=(k == n - 1))
                    if k == 0:
                        say_spent(mm)
                return mm

            pe.wait_ge(small_in, 16 * 16)
            pe.transpose(ps[6][:, 0:P], par_rows[:, :], ident).then_inc(p2_mm, 1)
            pe.transpose(ps[7][:, 0:P], tap_rows[:, :], ident).then_inc(p2_mm, 1)
            for f in range(KT):
                if f >= 4:
                    pe.wait_ge(ctx_ev, f - 3)
                for t in range(CTX // P):
                    mm = pe.transpose(ps[2 + f % 4][:, t * P:(t + 1) * P], ctx_in[:, t, f * P:(f + 1) * P], ident)
                mm.then_inc(ctx_mm, 1)

            pe.wait_ge(cond_ok, 2)
            for j in range(6 * KT):
                if j % 4 == 0:
                    arrived2(C_MOD + j // 4)
                wm = w(C_MOD + j // 4, 0, KT, 512)
                mm = product(ps[0][:, 2 * j:2 * j + 2], lambda k: wm[:, k, (j % 4) * P:(j % 4 + 1) * P], lambda k: cond[:, k, :])
                if j % 4 == 3 and j + 1 < 6 * KT:
                    give_back(1)
            mm.then_inc(mod_mm, 1)
            give_back(1)

            def rms_sums(m, n=S):
                for t in range(KT):
                    pe.wait_ge(n_sq, m * KT + t + 1)
                    mm = pe.matmul(ps[1 + m % 2][:, 0:n], ones, squares[:, t % 2, 0:n], start=(t == 0), stop=(t == KT - 1))
                    mm.then_inc(n_mm, 1)

            rms_sums(0)
            rms_sums(1, CTX)

            pe.wait_ge(mod_ok, 4)
            pe.wait_ge(n_out, 2 * KT)
            g = 0
            for j in range(5):
                c = C_IN + j
                arrived2(c)
                lo, hi = IN_RANGES[j]
                wi = w(c, 0, KT, hi - lo)
                for t in range(4):
                    if g >= 4:
                        pe.wait_ge(pj_ev, g - 3)
                    wt = lambda k: wi[:, k, t * P:(t + 1) * P]
                    mm = product(ps[2 * (g % 4)], wt, lambda k: zT[:, k, :])
                    if j in (1, 2):
                        mm = product(ps[2 * (g % 4) + 1][:, 0:CTX], wt, lambda k: hz[:, k, :])
                    mm.then_inc(pj_mm, 1)
                    g += 1
                if j == 2:
                    pe.wait_ge(pj_ev, g - 3)
                    for t in range(NT):
                        src, t0 = (hz, t) if t < CTX // P else (zT, t - CTX // P)
                        mm = product(ps[2 * (g % 4)][:, 16 * t:16 * t + 16], lambda k: src[:, k, t0 * P:(t0 + 1) * P],
                                     lambda k: wi[:, k, 4 * P:4 * P + 16])
                    mm.then_inc(pj_mm, 1)
                    g += 1
                give_back(1)

            for i in range(2 * DH):
                b = 2 * (i % 2)
                if i < 2:
                    pe.wait_ge(pj_ev, g - 2 + i)
                if i >= 2:
                    pe.wait_ge(l2_std, i - 1)
                pe.wait_ge(l2_sq, i + 1)
                mm = pe.matmul(ps[b][:, :], ones, pre[:, i % 2, 0:S], start=True, stop=True)
                say_spent(mm)
                mm = pe.matmul(ps[b + 1][:, 0:CTX], ones, pre[:, i % 2, S:S + CTX], start=True, stop=True)
                mm.then_inc(l2_mm, 1)

            pe.wait_ge(pj_ev, g)
            pe.wait_ge(ab_v, 4)
            gs = ps[4][:, 0:NT * U8].rearrange("p (t u) -> p t u", u=U8)
            for d in range(2):
                pe.matmul(gs[:, :, d * DH:(d + 1) * DH], tri[:, d, :], la[:, :, d * DH:(d + 1) * DH], start=True, stop=True)
            pe.matmul(ps[5][:, 0:NT * U8], same, la.rearrange("p t u -> p (t u)"), start=True, stop=True)
            pe.matmul(ps[6][:, 0:2 * NT * U8], ones, la_half.rearrange("p t c -> p (t c)"), start=True, stop=True)\
                .then_inc(ab_mm, 1)

            for i in range(4):
                pe.wait_ge(pl_ok, POOL_STEPS[i])
                if i == 0:
                    pe.wait_ge(ab_a, 7)
                pe.matmul(ps[4 + i][:, :], pool_w[:, i, :], u[:, i, :], start=True, stop=True).then_inc(pl_mm, 1)
            pe.wait_ge(pl_ev, 4)
            pe.wait_ge(l2_std, 2 * DH)

            for step in range(NT):
                x = step >= CTX // P

                def needs(e, name, at_step=step):
                    delta.wait(pe, e, at_step, name)

                def says(name, mm):
                    delta.says("pe", step, name, mm)

                def cols(un):
                    t = tile_of(step, un // DH)
                    return slice(t * P, (t + 1) * P)

                def xcols(un):
                    t = tile_of(step, un // DH) - CTX // P
                    return slice(t * P, (t + 1) * P)

                def each(i, lhsT, rhs, turn=False):
                    for un in range(U8):
                        o = pair(i)[:, un, :]
                        mm = pe.transpose(o, lhsT(un), ident) if turn else \
                            pe.matmul(o, lhsT(un), rhs(un), start=True, stop=True)
                    return mm

                needs("dve", "TRILA")
                if step == 0:
                    pe.wait_ge(l2_ok, 2 * DH)
                for d in range(2):
                    mm = pe.matmul(ps[d][:, :], ones, E[:, d * DH:(d + 1) * DH, :].rearrange("p u n -> p (u n)"),
                                   start=True, stop=True)
                says("G", mm)
                key = lambda un: kT[:, un % DH, cols(un)]
                says("KK", each(1, key, key))
                if x:
                    says("QK", each(2, key, lambda un: qT[:, un % DH, xcols(un)]))
                says("KTOK", each(3, key, None, True))
                needs("dve", "SUB")
                if x:
                    needs("act", "EG")
                says("VTOK", each(0, lambda un: vT[:, un % DH, cols(un)], None, True))
                needs("dve", "LT")
                says("L", each(1, lambda un: ETS[:, un, :], None, True))
                needs("dve", "PM")
                says("PT", each(2, lambda un: PA[:, un, :], None, True))
                needs("act", "PT")
                Ps, PTs = (PA, PB), (PTA, PTB)
                for r in range(1, 6):
                    p0, pt0, p1 = Ps[(r - 1) % 2], PTs[(r - 1) % 2], Ps[r % 2]
                    if r == 1:
                        needs("act", "VTOK")
                    else:
                        needs("dve", f"SQT{r - 1}")
                    says(f"SQ{r}", each(3, lambda un: pt0[:, un, :], lambda un: p0[:, un, :]))
                    if r < 5:
                        says(f"SQT{r}", each(0, lambda un: p0[:, un, :], lambda un: pt0[:, un, :]))
                    needs("act", f"SQ{r}")
                    needs("dve", f"TT{r - 1}")
                    says(f"TT{r}", each(1 if r % 2 else 2, lambda un: p1[:, un, :], lambda un: TT[:, un, :]))
                needs("dve", "TT5")
                needs("pool", "VB")
                says("WT", each(3, lambda un: KBG[:, un, :], lambda un: TT[:, un, :]))
                says("U", each(0, lambda un: TT[:, un, :], lambda un: VB[:, un, :]))
                needs("act", "WT")
                for c in range(2):
                    if c == 0:
                        if step == 0:
                            pe.wait_ge(pl_ok, POOL_STEPS[-1])
                        else:
                            needs("dve", "S1", step - 1)
                    else:
                        needs("dve", "S0")
                    says(f"WS{c}", each(1, lambda un: PTB[:, un, :], lambda un: ST8[:, un, :]))
                    if x:
                        for un in range(U8):
                            h = c if un < DH else 1 - c
                            part = slice(h * CHUNK, (h + 1) * CHUNK)
                            mm = pe.matmul(pair(3)[:, un, part], ST8[:, un, :], EG[:, un, part], start=True, stop=True)
                        says(f"Y{c}", mm)
                    needs("dve", f"UB{c}")
                    says(f"SU{c}", each(2, lambda un: (KT0 if c == 0 else KT1)[:, un, :], lambda un: PTA[:, un, :]))
                if x:
                    says("X", each(0, lambda un: PTA[:, un, :], lambda un: ETI[:, un, :]))

            for h in range(DH):
                pe.wait_ge(l2_sq, 2 * DH + h + 1)
                if h == 0:
                    pe.wait_ge(delta.sem["dve"], delta.last("dve"))
                if h >= 2:
                    pe.wait_ge(l2_std, 2 * DH + h - 1)
                pe.matmul(ps[h % 2][:, :], ones, squares[:, h % 2, :], start=True, stop=True).then_inc(l2_mm, 1)
            pe.wait_ge(l2_ok, 2 * DH + DH)
            for t in range(KT):
                c = C_OUT2 + t // 4
                if t % 4 == 0:
                    arrived2(c)
                if t >= 4:
                    pe.wait_ge(wo_ok, t - 3)
                wo = w(c, 0, KT, 512)
                mm = product(ps[4 + t % 4], lambda k: wo[:, k, (t % 4) * P:(t % 4 + 1) * P], lambda k: mix2[:, k, :])
                mm.then_inc(wo_mm, 1)
                if t % 4 == 3:
                    give_back(1)

            pe.wait_ge(wo_ok, KT)
            rms_sums(2)
            pe.wait_ge(n_out, 3 * KT)
            for t in range(ST):
                mm = product(ps[0][:, t * NE:(t + 1) * NE], lambda k: zT[:, k, t * P:(t + 1) * P], lambda k: w_rt[:, k, :])
            mm.then_inc(rt_mm, 1)
            for t in range(ST):
                for hf in range(2):
                    n = 2 * t + hf
                    if n >= 4:
                        pe.wait_ge(ht_ev, n - 3)
                    for f in range(4):
                        mm = pe.transpose(ps[4 + n % 4][:, f * P:(f + 1) * P],
                                          zT[:, 4 * hf + f, t * P:(t + 1) * P], ident)
                    mm.then_inc(ht_mm, 1)
            pe.wait_ge(rt_v, 5)
            for t in range(ST):
                mm = pe.transpose(ps[1][0:NE, t * P:(t + 1) * P], aff[:, t, :], ident)
            mm.then_inc(rt_mm, 1)
            pe.wait_ge(rt_v, POS_KNOWN)
            slot_rows = std[0:NE, :]
            for t in range(ST):
                mm = pe.transpose(ps[2][:, t * NE:(t + 1) * NE], slot_rows[:, t * P:(t + 1) * P], ident[0:NE, 0:NE])
            mm.then_inc(rt_mm, 1)
            pe.wait_ge(se_ok, ST)
            pe.wait_ge(ht_ev, 2 * ST)
            for f in range(KT):
                for hf in range(2):
                    n = 2 * f + hf
                    if n >= 4:
                        pe.wait_ge(xe_ev, n - 3)
                    mm = product(ps[4 + n % 4], lambda t: h_tok[:, t, f * P:(f + 1) * P],
                                 lambda t: sel[:, t, hf * 512:(hf + 1) * 512], ST)
                    mm.then_inc(xe_mm, 1)
            pe.wait_ge(sw_ok, ST)
            for q in range(NE // 2):
                if q >= 4:
                    pe.wait_ge(sw_ev, q - 3)
                for t in range(ST):
                    mm = pe.transpose(ps[q % 4][:, t * P:(t + 1) * P], sel_w[:, t, q * P:(q + 1) * P], ident)
                mm.then_inc(sw_mm, 1)
            pe.wait_ge(sw_ev, NE // 2)
            pe.wait_ge(xe_ev, 2 * KT)

            with pe.Fori(0, NE // 2) as q:
                for j in range(2):
                    def arrived_e(i):
                        c = C_EXP + EXP_CHUNKS * j + i
                        pe.wait_ge(loaded[slot(c)], q * (32 * 2 * EXP_CHUNKS // NSLOT) + 32 * (c // NSLOT + 1))

                    def turn(hf):
                        pe.wait_ge(ex_hid.sem, ex_hid.at(q, 2 * j + hf + 1))
                        for f in range(4):
                            mm = pe.transpose(ps[4 + 3 * hf][:, f * P:(f + 1) * P],
                                              hid[:, j, (4 * hf + f) * P:(4 * hf + f + 1) * P], ident)
                        mm.then_inc(ex_tm.sem, 1)

                    def down(hf):
                        i = 4 + hf
                        c = C_EXP + EXP_CHUNKS * j + i
                        arrived_e(i)
                        pe.wait_ge(ex_ht.sem, ex_ht.at(q, 2 * j + hf + 1))
                        wd = w(c, 0, KT // 2, D)
                        for n in range(2):
                            for k in range(4):
                                mm = pe.matmul(ps[5 + n][0:CAP, :], hidT[:, j, 4 * hf + k, :],
                                               wd[:, k, n * 512:(n + 1) * 512], start=(hf == 0 and k == 0),
                                               stop=(hf == 1 and k == 3))
                                if n == 0 and k == 0:
                                    say_spent(mm)
                        return mm

                    pe.wait_ge(ex_x.sem, ex_x.at(q, j + 1))
                    if j == 1:
                        pe.wait_ge(ex_ye.sem, ex_ye.at(q, 2))
                    for i in range(4):
                        arrived_e(i)
                        wg = w(C_EXP + EXP_CHUNKS * j + i, 0, KT, 512)
                        mm = product(ps[i][0:CAP, :], lambda k: xs[:, j, k, :], lambda k: wg[:, k, :])
                        mm.then_inc(ex_gu.sem, 1)
                        give_back(1)
                        if i == 2:
                            turn(0)
                    down(0)
                    give_back(1)
                    turn(1)
                    mm = down(1)
                    mm.then_inc(used, 1)

            pe.wait_ge(ex_ye.sem, ex_ye.per * NE // 2)
            for f in range(KT):
                mm = product(ps[f], lambda q: ye[:, q, f * P:(f + 1) * P], lambda q: sel_wT[:, q, :], NE // 2)
                mm.then_inc(cb_mm, 1)
            pe.wait_ge(cb_ok, KT)
            rms_sums(3)
            for t in range(ST):
                for hf in range(2):
                    n = 2 * t + hf
                    if n == 0:
                        pe.wait_ge(n_out, 4 * KT)
                    if n >= 4:
                        pe.wait_ge(fin_ev, n - 3)
                    for f in range(4):
                        mm = pe.transpose(ps[4 + n % 4][:, f * P:(f + 1) * P], zT[:, 4 * hf + f, t * P:(t + 1) * P], ident)
                    mm.then_inc(fin_mm, 1)

        @block.scalar
        def _(act):
            act.wait_ge(const_in, 32)
            act.wait_ge(ready, 1)
            act.wait_ge(rope_v, 8)
            nc.scalar.activation(sinT[:, :], rope_b, ACT.Sin).then_inc(rope_s, 1)
            act.wait_ge(rope_v, 10)
            nc.scalar.activation(cosT[:, :], kr_raw, ACT.Sin).then_inc(rope_s, 1)
            for f in range(2 * KT):
                act.wait_ge(turned, f + 1)
                dst = xT[:, f, :] if f < KT else memT[:, f - KT, :]
                nc.scalar.activation(dst, ps[f % 4][:, 0:S if f < KT else MEM], ACT.Copy).then_inc(turned_out, 1)

            with act.Fori(0, DEPTH) as l:
                def col(j, m=P):
                    return par[0:m, j:j + 1]

                def norm(i):
                    for t in range(KT):
                        act.wait_ge(cen.sem, cen.at(l, i * KT + t + 1))
                        if t >= 2:
                            act.wait_ge(var_mm.sem, var_mm.at(l, i * KT + t - 1))
                        nc.scalar.activation(squares[:, t % 2, :], zT[:, t, :], ACT.Square).then_inc(sq_ok.sem, 1)
                    act.wait_ge(var_mm.sem, var_mm.at(l, (i + 1) * KT))
                    nc.scalar.activation(std[:, :], ps[1][:, :], ACT.Sqrt, bias=eps[:, 0:1], scale=1.0 / D)\
                        .then_inc(std_ok.sem, 1)
                    for t in range(KT):
                        act.wait_ge(scaled.sem, scaled.at(l, i * KT + t + 1))
                        g = P_LN + 2 * i * KT + t
                        nc.scalar.activation(xT[:, t, :], zT[:, t, :], ACT.Identity, bias=col(g + KT), scale=col(g))\
                            .then_inc(x_ok.sem, 1)

                act.wait_ge(par_mm.sem, par_mm.at(l, 1))
                nc.scalar.activation(par[:, :], ps[6][:, 0:NPAR], ACT.Copy).then_inc(par_ev.sem, 1)
                act.wait_ge(par_mm.sem, par_mm.at(l, 2))
                nc.scalar.activation(taps[:, :], ps[7][:, 0:TAPS * CT], ACT.Copy).then_inc(par_ev.sem, 1)
                act.wait_ge(par_ev.sem, par_ev.at(l, 2))

                for n in range(5):
                    act.wait_ge(proj_mm.sem, proj_mm.at(l, n + 1))
                    m = P if n < 4 else QK
                    dst = cqkv[:, n, :] if n < 4 else kr_raw[0:QK, :]
                    nc.scalar.activation(dst, ps[n][0:m, :], ACT.Identity, bias=col(PB_CQ + n, m)).then_inc(proj_ev.sem, 1)
                for n in range(4):
                    act.wait_ge(proj_ev.sem, proj_ev.at(l, n + 1))
                    nc.scalar.activation(mixT[:, n, :], cqkv[:, n, :], ACT.Square).then_inc(lsq.sem, 1)
                for t in range(CT):
                    act.wait_ge(proj_mm.sem, proj_mm.at(l, 7 + 2 * t))
                    if t >= 2:
                        act.wait_ge(glu.sem, glu.at(l, t - 1))
                    nc.scalar.activation(gates[:, t % 2, :], ps[(6 + 2 * t) % 8][:, :], ACT.Sigmoid, bias=col(PB_G + t))\
                        .then_inc(sig_ev.sem, 1)
                for n in range(2):
                    act.wait_ge(lsum.sem, lsum.at(l, n + 1))
                    act.wait_ge(glu.sem, glu.at(l, CT))
                    nc.scalar.activation(gates[:, n, :], ps[5 + n][:, :], ACT.Sqrt, bias=eps[:, 1:2], scale=1.0 / LORA)\
                        .then_inc(lstd.sem, 1)
                for h in range(HEADS):
                    act.wait_ge(up_mm.sem, up_mm.at(l, h + 1))
                    nc.scalar.activation(qh[0:QK, h, :], ps[h][0:QK, :], ACT.Copy).then_inc(q_ev.sem, 1)
                for h in range(HEADS):
                    act.wait_ge(up_mm.sem, up_mm.at(l, HEADS + h + 1))
                    nc.scalar.activation(kh[0:NOPE, h, :], ps[h][0:NOPE, :], ACT.Copy).then_inc(kv_ev.sem, 1)
                for t in range(ST):
                    act.wait_ge(up_mm.sem, up_mm.at(l, 2 * HEADS + t + 1))
                    nc.scalar.activation(vt[:, t, :], ps[t][:, :], ACT.Copy).then_inc(kv_ev.sem, 1)

                sc_bank = (0, 1, 6, 7)

                def exps(h):
                    for t in range(ST):
                        n = h * ST + t
                        act.wait_ge(sc_max.sem, sc_max.at(l, n + 1))
                        if h >= 2:
                            act.wait_ge(pt_mm.sem, pt_mm.at(l, (h - 1) * ST))
                        j = n % 8
                        nc.scalar.activation(probs[:, h % 2, t, 0:(t + 1) * P], ps[sc_bank[t]][:, 0:(t + 1) * P],
                                             ACT.Exp, bias=stat[:, 1, j:j + 1], scale=QK ** -0.5,
                                             accum_out=stat[:, 2, j:j + 1]).then_inc(sc_exp.sem, 1)

                def turned_probs(h):
                    for kt in range(ST):
                        n = h * ST + kt
                        act.wait_ge(pt_mm.sem, pt_mm.at(l, n + 1))
                        if h >= 1 and kt == 0:
                            act.wait_ge(pv_mm.sem, pv_mm.at(l, h))
                        nc.scalar.activation(probsT[:, kt, kt * P:S], ps[2 + n % 2][:, kt * P:S], ACT.Copy)\
                            .then_inc(pt_ev.sem, 1)

                act.wait_ge(kcopy.sem, kcopy.at(l, 1))
                act.wait_ge(qrot.sem, qrot.at(l, HEADS))
                for h in range(HEADS + 1):
                    if h < HEADS:
                        exps(h)
                    if h >= 1:
                        turned_probs(h - 1)

                for n in range(12):
                    act.wait_ge(xkv_mm.sem, xkv_mm.at(l, n + 1))
                    b = ps[sc_bank[n % 4]]
                    if n < 8:
                        nc.scalar.activation(xk[:, n, :], b[:, 0:MEM], ACT.Copy).then_inc(xkv_ev.sem, 1)
                    else:
                        t, j = (n - 8) // 2, n % 2
                        nc.scalar.activation(xv[:, t, j * 512:(j + 1) * 512], b[:, :], ACT.Copy).then_inc(xkv_ev.sem, 1)

                for t in range(CT):
                    act.wait_ge(ccen.sem, ccen.at(l, t + 1))
                    if t >= 2:
                        act.wait_ge(cvar.sem, cvar.at(l, t - 1))
                    nc.scalar.activation(squares[:, t % 2, :], mixT[:, CT + t, :], ACT.Square).then_inc(csq.sem, 1)
                act.wait_ge(cvar.sem, cvar.at(l, CT))
                nc.scalar.activation(std[:, :], ps[3][:, :], ACT.Sqrt, bias=eps[:, 0:1], scale=1.0 / CW)\
                    .then_inc(cstd.sem, 1)
                for t in range(CT):
                    act.wait_ge(cmul.sem, cmul.at(l, t + 1))
                    nc.scalar.activation(mixT[:, CT + t, :], mixT[:, CT + t, :], ACT.Silu, bias=col(P_CNB + t),
                                         scale=col(P_CNG + t)).then_inc(cout.sem, 1)
                norm(0)

                for t in range(KT):
                    act.wait_ge(xq_mm.sem, xq_mm.at(l, t + 1))
                    nc.scalar.activation(qx[:, t, :], ps[2 + t % 4][:, :], ACT.Copy).then_inc(xq_ev.sem, 1)

                def xexps(h):
                    for t in range(ST):
                        n = 2 * h + t // 2
                        act.wait_ge(xs_max.sem, xs_max.at(l, n + 1))
                        if h >= 2:
                            act.wait_ge(xt_mm.sem, xt_mm.at(l, (h - 1) * MT))
                        j = (h * ST + t) % 8
                        nc.scalar.activation(probs[:, h % 2, t, 0:MEM],
                                             ps[sc_bank[n % 4]][:, (t % 2) * MEM:(t % 2 + 1) * MEM], ACT.Exp,
                                             bias=stat[:, 1, j:j + 1], scale=XD ** -0.5,
                                             accum_out=stat[:, 2, j:j + 1]).then_inc(xs_exp.sem, 1)

                def xturned(h):
                    for kt in range(MT):
                        act.wait_ge(xt_mm.sem, xt_mm.at(l, MT * h + kt + 1))
                        if h >= 1 and kt == 0:
                            act.wait_ge(xo_mm.sem, xo_mm.at(l, 2 * h))
                        nc.scalar.activation(probsT[:, kt, :], ps[2 + kt][:, :], ACT.Copy).then_inc(xt_ev.sem, 1)

                for h in range(XH + 1):
                    if h < XH:
                        xexps(h)
                    if h >= 1:
                        xturned(h - 1)
                norm(1)
                for t in range(FT):
                    act.wait_ge(ffn_mm.sem, ffn_mm.at(l, 2 * t + 1))
                    if t >= 2:
                        act.wait_ge(ffn_ok.sem, ffn_ok.at(l, t - 1))
                    nc.scalar.activation(gates[:, t % 2, :], ps[2 * (t % 4)][:, :], ACT.Silu).then_inc(ffn_act.sem, 1)
                norm(2)

            A1 = nc.scalar.activation
            act.wait_ge(p2_mm, 1)
            A1(par2, ps[6][:, 0:NPAR2], ACT.Copy).then_inc(p2_ev, 1)
            act.wait_ge(p2_mm, 2)
            A1(taps2, ps[7][:, 0:CONV_K * 3 * DH], ACT.Copy).then_inc(p2_ev, 1)
            act.wait_ge(p2_ev, 1)
            for j, lo in enumerate((Q_C, Q_CC)):
                A1(cond[:, :, j], par2[:, lo:lo + KT], ACT.Silu).then_inc(cond_ok, 1)
            for f in range(KT):
                act.wait_ge(ctx_mm, f + 1)
                A1(ctxT[:, f, :], ps[2 + f % 4][:, 0:CTX], ACT.Copy).then_inc(ctx_ev, 1)

            def rms(m, src, dst, scale, bias, n=S, changed=None):
                for t in range(KT):
                    if changed is not None:
                        act.wait_ge(changed, t + 1)
                    if t >= 2:
                        act.wait_ge(n_mm, m * KT + t - 1)
                    A1(squares[:, t % 2, 0:n], src[:, t, :], ACT.Square).then_inc(n_sq, 1)
                act.wait_ge(n_mm, (m + 1) * KT)
                if m == 1:
                    act.wait_ge(n_mul, KT)
                A1(std[:, 0:n], ps[1 + m % 2][:, 0:n], ACT.Sqrt, bias=eps[:, 1:2], scale=1.0 / D).then_inc(n_std, 1)
                for t in range(KT):
                    act.wait_ge(n_mul, m * KT + t + 1)
                    A1(dst[:, t, :], dst[:, t, :], ACT.Identity, scale=scale(t), bias=bias(t) if bias else 0.0)\
                        .then_inc(n_out, 1)

            act.wait_ge(ctx_ev, KT)
            act.wait_ge(mod_ok, 4)
            rms(0, xT, zT, lambda t: gain[:, 0, t:t + 1], lambda t: mod[:, t, 0:1])
            rms(1, ctxT, hz, lambda t: gain[:, 1, t:t + 1], lambda t: mod[:, t, 1:2], CTX)

            def swish(c):
                act.wait_ge(cv_ok, CONV_K * (c + 1))
                t = c % DH
                if c < 2 * DH:
                    dst = (kT, vT)[c // DH]
                    A1(dst[:, t, CTX:], acc[:, c % 2, 0:S], ACT.Silu).then_inc(cv_out, 1)
                    A1(dst[:, t, 0:CTX], acc[:, c % 2, S + 3:S + 3 + CTX], ACT.Silu).then_inc(cv_out, 1)
                else:
                    A1(qT[:, t, :], acc[:, c % 2, 0:S], ACT.Silu).then_inc(cv_out, 1)

            act.wait_ge(padded, 1)
            g = 0
            for j in range(5):
                for t in range(4):
                    act.wait_ge(pj_mm, g + 1)
                    b = ps[2 * (g % 4)]
                    if j == 0:
                        A1(u[:, t, :], b, ACT.Copy).then_inc(pj_ev, 1)
                    elif j < 4:
                        c = 4 * (j - 1) + t
                        if c >= 2:
                            act.wait_ge(cv_ok, CONV_K * (c - 1))
                        if j < 3:
                            A1(pre[:, c % 2, S + 5:S + 5 + CTX], ps[2 * (g % 4) + 1][:, 0:CTX], ACT.Copy)
                        A1(pre[:, c % 2, 2:2 + S], b, ACT.Copy).then_inc(pj_ev, 1)
                        if c >= 1:
                            swish(c - 1)
                    else:
                        A1(gateT[:, t, :], b, ACT.Silu).then_inc(pj_ev, 1)
                    g += 1
                if j == 2:
                    act.wait_ge(pj_mm, g + 1)
                    src = ps[2 * (g % 4)][:, 0:16 * NT].rearrange("p (t a u) -> p t a u", a=2, u=U8)
                    A1(ab[:, :, :, 0:DH], src[:, :, :, 0:DH], ACT.Copy)
                    for step in range(NT):
                        ins = A1(ab[:, step, :, DH:], src[:, tile_of(step, 1), :, DH:], ACT.Copy)
                    ins.then_inc(pj_ev, 1)
                    g += 1
                if j == 3:
                    swish(11)

            for i in range(2 * DH + 2):
                if i < 2 * DH:
                    if i == 0:
                        act.wait_ge(cv_out, 4 * DH + DH)
                    if i >= 2:
                        act.wait_ge(l2_mm, i - 1)
                    src = kT[:, i, :] if i < DH else qT[:, i - DH, :]
                    if i < DH:
                        A1(pre[:, i % 2, 0:S], src[:, CTX:], ACT.Square)
                        A1(pre[:, i % 2, S:S + CTX], src[:, 0:CTX], ACT.Square).then_inc(l2_sq, 1)
                    else:
                        A1(pre[:, i % 2, 0:S], src, ACT.Square)
                        A1(pre[:, i % 2, S:S + CTX], src[:, 0:CTX], ACT.Square).then_inc(l2_sq, 1)
                if i >= 2:
                    m = i - 2
                    act.wait_ge(l2_mm, m + 1)
                    if m >= 2:
                        act.wait_ge(l2_ok, m - 1)
                    A1(acc[:, m % 2, 0:S], ps[2 * (m % 2)][:, :], ACT.Sqrt, bias=eps[:, 1:2])
                    A1(acc[:, m % 2, S:S + CTX], ps[2 * (m % 2) + 1][:, 0:CTX], ACT.Sqrt, bias=eps[:, 1:2]).then_inc(l2_std, 1)

            act.wait_ge(ab_v, 1)
            A1(sp_e, sp_e, ACT.Exp, scale=-1.0).then_inc(ab_a, 1)
            A1(a_log, a_log, ACT.Exp).then_inc(ab_a, 1)
            act.wait_ge(ab_a, 2)
            A1(sp_e, sp_e, ACT.Ln, bias=1.0).then_inc(ab_a, 1)
            A1(beta, ab[:, :, 1, :], ACT.Sigmoid).then_inc(ab_a, 1)
            act.wait_ge(ab_mm, 1)
            A1(gsum.rearrange("p t u -> p (t u)"), ps[4][:, 0:NT * U8], ACT.Copy).then_inc(ab_a, 1)
            A1(eg.rearrange("p t u -> p (t u)"), ps[4][:, 0:NT * U8], ACT.Exp).then_inc(ab_a, 1)
            act.wait_ge(ab_v, 5)
            A1(sdec.rearrange("p t c -> p (t c)"), ps[6][:, 0:2 * NT * U8], ACT.Exp).then_inc(ab_a, 1)
            A1(tail, tail, ACT.Exp).then_inc(ab_a, 1)

            for i in range(4):
                act.wait_ge(pl_mm, i + 1)
                A1(mix2[:, DH + i, :], ps[4 + i][:, :], ACT.Copy, scale=par2[:, Q_PS + i:Q_PS + i + 1]).then_inc(pl_ev, 1)

            for step in range(NT):
                x = step >= CTX // P

                def needs(e, name):
                    delta.wait(act, e, step, name)

                def says(name, ins):
                    delta.says("act", step, name, ins)

                needs("dve", "MIN")
                says("E", A1(E, E, ACT.Exp))
                if x:
                    says("EG", A1(EG, pair(0), ACT.Exp))
                needs("pe", "KTOK")
                says("KTOK", A1(KT1, pair(3), ACT.Copy))
                needs("pe", "VTOK")
                says("VTOK", A1(VB, pair(0), ACT.Copy))
                needs("pe", "PT")
                says("PT", A1(PTA, pair(2), ACT.Copy))
                for r in range(1, 6):
                    needs("pe", f"SQ{r}")
                    if r >= 2:
                        needs("pe", f"TT{r - 1}")
                    says(f"SQ{r}", A1((PA, PB)[r % 2], pair(3), ACT.Copy))
                needs("pe", "WT")
                says("WT", A1(PTB, pair(3), ACT.Copy))

            def head_std(h):
                act.wait_ge(l2_mm, 2 * DH + h + 1)
                A1(head_dev[:, h, :], ps[h % 2][:, :], ACT.Sqrt, bias=eps[:, 1:2], scale=1.0 / P).then_inc(l2_std, 1)

            for h in range(DH):
                if h == 0:
                    act.wait_ge(delta.sem["dve"], delta.last("dve"))
                if h >= 2:
                    act.wait_ge(l2_mm, 2 * DH + h - 1)
                A1(squares[:, h % 2, :], mix2[:, h, :], ACT.Square).then_inc(l2_sq, 1)
                if h >= 1:
                    head_std(h - 1)
            head_std(DH - 1)

            rms(2, xT, zT, lambda t: gain[:, 2, t:t + 1], lambda t: mod[:, 3 * KT + t, 0:1], changed=wo_ok)
            act.wait_ge(rt_v, 2)
            A1(aff, aff, ACT.Exp).then_inc(rt_a, 1)
            for n in range(2 * ST):
                act.wait_ge(ht_mm, n + 1)
                A1(h_tok[:, n // 2, (n % 2) * 512:(n % 2 + 1) * 512], ps[4 + n % 4][:, :], ACT.Copy).then_inc(ht_ev, 1)
            for n in range(2 * KT):
                act.wait_ge(xe_mm, n + 1)
                A1(xeT[:, n // 2, (n % 2) * 512:(n % 2 + 1) * 512], ps[4 + n % 4][:, :], ACT.Copy).then_inc(xe_ev, 1)
            for q in range(NE // 2):
                act.wait_ge(sw_mm, q + 1)
                A1(sel_wT[:, q, :], ps[q % 4][:, :], ACT.Copy).then_inc(sw_ev, 1)

            with act.Fori(0, NE // 2) as q:
                for j in range(2):
                    for hf in range(2):
                        n = 2 * j + hf
                        act.wait_ge(ex_gu.sem, ex_gu.at(q, 4 * j + 2 * hf + 1))
                        if j == 1:
                            act.wait_ge(ex_hid.sem, ex_hid.at(q, n - 1))
                        A1(gates[0:CAP, hf, :], ps[2 * hf][0:CAP, :], ACT.Silu).then_inc(ex_silu.sem, 1)
                        act.wait_ge(ex_tm.sem, ex_tm.at(q, n + 1))
                        A1(hidT[:, j, 4 * hf:4 * hf + 4, :],
                           ps[4 + 3 * hf].rearrange("p (f c) -> p f c", c=P)[:, :, 0:CAP], ACT.Copy).then_inc(ex_ht.sem, 1)
            rms(3, xT, zT, lambda t: par2[:, Q_NF + t:Q_NF + t + 1], None, changed=cb_ok)
            for n in range(2 * ST):
                t, hf = n // 2, n % 2
                act.wait_ge(fin_mm, n + 1)
                if t >= 2 and hf == 0:
                    act.wait_ge(stored[t % 2], 16 * (t // 2))
                A1(out_tok[:, t % 2, hf * 512:(hf + 1) * 512], ps[4 + n % 4][:, :], ACT.Copy).then_inc(fin_ev, 1)

        @block.gpsimd
        def _(pool):
            with pool.Fori(0, DEPTH) as l:
                pool.wait_ge(krot.sem, krot.at(l, 2))
                def every(x):
                    return x[NOPE:QK, :].rearrange("p (a n) -> p a n", a=1).broadcast_to([ROPE, HEADS, S])

                nc.gpsimd.tensor_tensor(kh[NOPE:QK, :, :], every(rope_a), every(rope_b), ALU.add).then_inc(kcopy.sem, 1)
                for h in range(HEADS):
                    q = qh[NOPE:QK, h, :]
                    pool.wait_ge(qrot_mm.sem, qrot_mm.at(l, h + 1))
                    nc.gpsimd.tensor_tensor(q, q, cosT[NOPE:QK, :], ALU.mult).then_inc(qrot_cos.sem, 1)
                    pool.wait_ge(qrot_cos.sem, qrot_cos.at(l, h + 1))
                    pool.wait_ge(qrot_sin.sem, qrot_sin.at(l, h + 1))
                    nc.gpsimd.tensor_tensor(q, q, (rope_a if h % 2 else rope_b)[NOPE:QK, :], ALU.add)\
                        .then_inc(qrot.sem, 1)

            G = nc.gpsimd
            count = [0]

            def behind(ins):
                ins.then_inc(pl_ok, 1)
                count[0] += 1
                pool.wait_ge(pl_ok, count[0])

            pool.wait_ge(small_in, 16 * 16)
            for i, win in enumerate(WINDOWS):
                buf = [pool_a, pool_b]
                W = GRID_W + win
                if i == 0:
                    pool.wait_ge(ctx_ev, KT)
                b0 = buf[0][:, 0:ROWS * W].rearrange("p (r c) -> p r c", c=W)
                behind(G.memset(b0, 0.0))
                pool.wait_ge(pj_ev, i + 1)
                ug = u[:, i, :].rearrange("p (r c) -> p r c", c=GRID_W)
                behind(G.tensor_copy(b0[:, :, win // 2:win // 2 + GRID_W], ug))
                cur, s, width = 0, 1, W
                while s < win:
                    src = buf[cur][:, 0:ROWS * W].rearrange("p (r c) -> p r c", c=W)
                    dst = buf[1 - cur][:, 0:ROWS * W].rearrange("p (r c) -> p r c", c=W)
                    width -= s
                    behind(G.tensor_tensor(dst[:, :, 0:width], src[:, :, 0:width], src[:, :, s:s + width], ALU.add))
                    cur, s = 1 - cur, 2 * s
                src = buf[cur][:, 0:ROWS * W].rearrange("p (r c) -> p r c", c=W)
                R = ROWS + win
                dst = buf[1 - cur][:, 0:R * GRID_W].rearrange("p (r c) -> p r c", c=GRID_W)
                behind(G.memset(dst, 0.0))
                behind(G.tensor_copy(dst[:, win // 2:win // 2 + ROWS, :], src[:, :, 0:GRID_W]))
                cur, s, height = 1 - cur, 1, R
                while s < win:
                    height -= s
                    src, dst = buf[cur], buf[1 - cur]
                    behind(G.tensor_tensor(dst[:, 0:height * GRID_W], src[:, 0:height * GRID_W],
                                           src[:, s * GRID_W:(s + height) * GRID_W], ALU.add))
                    cur, s = 1 - cur, 2 * s
                m = buf[cur][:, 0:S]
                behind(G.tensor_tensor(m, m, inv_cnt[:, i, :], ALU.mult))
                behind(G.tensor_tensor(u[:, i, :], m, u[:, i, :], ALU.subtract))
                assert count[0] == POOL_STEPS[i], (i, count)
            G.memset(mix2[:, 0:DH, :], 0.0)
            pool.wait_ge(pj_mm, 21)
            behind(G.memset(ST8, 0.0))
            assert count[0] == POOL_STEPS[-1], count

            for step in range(NT):
                x = step >= CTX // P

                def needs(e, name, at_step=step):
                    delta.wait(pool, e, at_step, name)

                def says(name, ins):
                    delta.says("pool", step, name, ins)

                def masked(m):
                    return [m[:, d:d + 1, :].broadcast_to([P, DH, P]) for d in range(2)]

                needs("act", "E")
                for name, dst, m in (("ETS", ETS, strict), ("ETI", ETI, tri)):
                    if step and name == "ETI":
                        needs("pe", "X" if step - 1 >= CTX // P else "SU1", step - 1)
                    for d in range(2):
                        r = slice(d * DH, (d + 1) * DH)
                        ins = G.tensor_tensor(dst[:, r, :], E[:, r, :], masked(m)[d], ALU.mult)
                    says(name, ins)
                if x:
                    needs("act", "EG")
                    for d in range(2):
                        r = slice(d * DH, (d + 1) * DH)
                        t = tile_of(step, d) - CTX // P
                        ins = G.tensor_tensor(EG[:, r, :], EG[:, r, :], qT[:, :, t * P:(t + 1) * P], ALU.mult)
                    says("QD", ins)

                def scaled(dst, src, vec8):
                    return G.tensor_tensor(dst, src, vec8.unsqueeze(2).broadcast_to([P, U8, P]), ALU.mult)

                th = tail_half[:, step * U8:(step + 1) * U8, :]
                sd = sdec[:, step * U8:(step + 1) * U8, :]
                needs("act", "KTOK")
                if step == 0:
                    pool.wait_ge(ab_v, 8)
                says("KBG", scaled(KBG, KT1, beg[:, step, :]))
                says("KT0", scaled(KT0, KT1, th[:, :, 0]))
                needs("pool", "KT0")
                says("KT1", scaled(KT1, KT1, th[:, :, 1]))
                needs("act", "VTOK")
                says("VB", scaled(VB, VB, beta[:, step, :]))
                if step:
                    needs("dve", "S1", step - 1)
                says("SD0", scaled(SD, ST8, sd[:, :, 0]))
                needs("dve", "S0")
                says("SD1", scaled(SD, ST8, sd[:, :, 1]))

            for t in range(ST):
                pool.wait_ge(se_ok, t + 1)
                G.tensor_tensor(sel_w[:, t, :].rearrange("p (e c) -> p e c", c=CAP),
                                sel[:, t, :].rearrange("p (e c) -> p e c", c=CAP),
                                aff[:, t, :].unsqueeze(2).broadcast_to([P, NE, CAP]), ALU.mult).then_inc(sw_ok, 1)

        @block.vector
        def _(dve):
            V = nc.vector
            V.memset(par_rows[:, :], 0.0).then_inc(ready, 1)
            V.memset(eps[:, 0:1], LN_EPS)
            V.memset(eps[:, 1:2], RMS_EPS)
            V.memset(hpad[:, :, 0:TAPS - 1], 0.0)
            V.memset(tap_rows[:, :], 0.0).then_inc(ready, 1)

            dve.wait_ge(const_in, 32)
            V.tensor_copy(rope_b, rope_a.bitcast(I32)).then_inc(rope_v, 1)
            dve.wait_ge(rope_v, 1)
            V.tensor_scalar(rope_b, rope_b, consts[:, K_FREQ:K_FREQ + 1], None, ALU.mult).then_inc(rope_v, 1)
            dve.wait_ge(rope_v, 2)
            V.tensor_scalar(rope_a, rope_b, 1.0 / TWO_PI, ROUND, ALU.mult, ALU.add).then_inc(rope_v, 1)
            dve.wait_ge(rope_v, 3)
            V.tensor_scalar(rope_a, rope_a, -ROUND, None, ALU.add).then_inc(rope_v, 1)
            for n, c in enumerate((PI_A, PI_B, PI_C)):
                dve.wait_ge(rope_v, 4 + n)
                V.scalar_tensor_tensor(out=rope_b, in0=rope_a, scalar=-c, in1=rope_b, op0=ALU.mult, op1=ALU.add)\
                    .then_inc(rope_v, 1)
            dve.wait_ge(rope_v, 7)
            V.tensor_scalar(rope_b, rope_b, PI_MAX, -PI_MAX, ALU.min, ALU.max).then_inc(rope_v, 1)
            dve.wait_ge(rope_v, 8)
            V.scalar_tensor_tensor(out=rope_a, in0=rope_b, scalar=-1.0, in1=rope_b, op0=ALU.mult, op1=ALU.max)\
                .then_inc(rope_v, 1)
            dve.wait_ge(rope_v, 9)
            V.tensor_scalar(kr_raw, rope_a, -1.0, np.pi / 2, ALU.mult, ALU.add).then_inc(rope_v, 1)

            with dve.Fori(0, DEPTH) as l:
                behind = [0]

                def done(ins):
                    ins.then_inc(vec.sem, 1)
                    behind[0] += 1
                    return vec.at(l, behind[0])

                def residual(i):
                    for t in range(KT):
                        dve.wait_ge(res_mm.sem, res_mm.at(l, i * KT + t + 1))
                        V.scalar_tensor_tensor(out=zT[:, t, :], in0=xT[:, t, :], scalar=ALPHA, in1=ps[4 + t % 4][:, :],
                                               op0=ALU.mult, op1=ALU.add).then_inc(z_ok.sem, 1)
                    dve.wait_ge(mean_mm.sem, mean_mm.at(l, i + 1))
                    for t in range(KT):
                        V.scalar_tensor_tensor(out=zT[:, t, :], in0=ps[0][:, :], scalar=-1.0 / D, in1=zT[:, t, :],
                                               op0=ALU.mult, op1=ALU.add).then_inc(cen.sem, 1)
                    dve.wait_ge(std_ok.sem, std_ok.at(l, i + 1))
                    n = done(V.reciprocal(std[:, :], std[:, :]))
                    dve.wait_ge(vec.sem, n)
                    for t in range(KT):
                        V.tensor_tensor(zT[:, t, :], zT[:, t, :], std[:, :], ALU.mult).then_inc(scaled.sem, 1)

                dve.wait_ge(par_ev.sem, par_ev.at(l, 2))
                for t in range(CT):
                    dve.wait_ge(sig_ev.sem, sig_ev.at(l, t + 1))
                    V.scalar_tensor_tensor(out=hpad[:, t, TAPS - 1:], in0=ps[(5 + 2 * t) % 8][:, :],
                                           scalar=par[:, PB_A + t:PB_A + t + 1], in1=gates[:, t % 2, :],
                                           op0=ALU.add, op1=ALU.mult).then_inc(glu.sem, 1)
                for n in range(2):
                    dve.wait_ge(lstd.sem, lstd.at(l, n + 1))
                    v = done(V.reciprocal(gates[:, n, :], gates[:, n, :]))
                    dve.wait_ge(vec.sem, v)
                    for k in range(2):
                        j = P_QN + 2 * n + k
                        V.scalar_tensor_tensor(out=cqkv[:, 2 * n + k, :], in0=cqkv[:, 2 * n + k, :],
                                               scalar=par[:, j:j + 1], in1=gates[:, n, :],
                                               op0=ALU.mult, op1=ALU.mult).then_inc(lnorm.sem, 1)
                r = slice(NOPE, QK)
                dve.wait_ge(krot_mm.sem, krot_mm.at(l, 1))
                V.tensor_tensor(rope_a[r, :], ps[7][r, :], sinT[r, :], ALU.mult).then_inc(krot.sem, 1)
                V.tensor_tensor(rope_b[r, :], kr_raw[r, :], cosT[r, :], ALU.mult).then_inc(krot.sem, 1)
                dve.wait_ge(kcopy.sem, kcopy.at(l, 1))
                for h in range(HEADS):
                    dve.wait_ge(qrot_mm.sem, qrot_mm.at(l, h + 1))
                    if h >= 2:
                        dve.wait_ge(qrot.sem, qrot.at(l, h - 1))
                    V.tensor_tensor((rope_a if h % 2 else rope_b)[r, :], ps[4 + h % 4][r, :], sinT[r, :], ALU.mult)\
                        .then_inc(qrot_sin.sem, 1)

                sc_bank = (0, 1, 6, 7)

                def maximum(n):
                    t, j = n % ST, n % 8
                    b = ps[sc_bank[t]]
                    dve.wait_ge(sc_mm.sem, sc_mm.at(l, n + 1))
                    v = done(V.memset(b[0:CHUNK, (t + 1) * P - CHUNK:(t + 1) * P], NEG))
                    dve.wait_ge(vec.sem, v)
                    v = done(V.tensor_reduce(stat[:, 0, j:j + 1], b[:, 0:(t + 1) * P], AX, ALU.max))
                    dve.wait_ge(vec.sem, v)
                    V.tensor_scalar(stat[:, 1, j:j + 1], stat[:, 0, j:j + 1], -QK ** -0.5, None, ALU.mult)\
                        .then_inc(sc_max.sem, 1)

                def normalise(n):
                    h, t, j = n // ST, n % ST, n % 8
                    dve.wait_ge(sc_exp.sem, sc_exp.at(l, n + 1))
                    v = done(V.reciprocal(stat[:, 3, j:j + 1], stat[:, 2, j:j + 1]))
                    dve.wait_ge(vec.sem, v)
                    p = probs[:, h % 2, t, 0:(t + 1) * P]
                    V.tensor_scalar(p, p, stat[:, 3, j:j + 1], None, ALU.mult).then_inc(sc_norm.sem, 1)

                def tap(k):
                    for t in range(CT):
                        acc, x = mixT[:, CT + t, :], hpad[:, t, k:k + S]
                        c = taps[:, k * CT + t:k * CT + t + 1]
                        if k == 0:
                            V.tensor_scalar(acc, x, c, par[:, P_DWB + t:P_DWB + t + 1], ALU.mult, ALU.add)\
                                .then_inc(conv.sem, 1)
                        else:
                            dve.wait_ge(conv.sem, conv.at(l, CT * (k - 1) + t + 1))
                            V.scalar_tensor_tensor(out=acc, in0=x, scalar=c, in1=acc, op0=ALU.mult, op1=ALU.add)\
                                .then_inc(conv.sem, 1)

                def head_out(h):
                    dve.wait_ge(pv_mm.sem, pv_mm.at(l, h + 1))
                    lo = (h % 2) * VD
                    V.tensor_copy(mixT[lo:lo + VD, h // 2, :], ps[4 + h % 2][0:VD, :]).then_inc(pv_ev.sem, 1)

                LAG = 2
                for n in range(HEADS * ST + LAG):
                    if n < HEADS * ST:
                        maximum(n)
                    if n >= LAG:
                        normalise(n - LAG)
                    if n < TAPS:
                        tap(n)
                    if n >= 2 * ST and n % ST == 3:
                        head_out(n // ST - 2)
                head_out(HEADS - 2)
                head_out(HEADS - 1)

                dve.wait_ge(cstat_mm.sem, cstat_mm.at(l, 1))
                for t in range(CT):
                    V.scalar_tensor_tensor(out=mixT[:, CT + t, :], in0=ps[2][:, :], scalar=-1.0 / CW,
                                           in1=mixT[:, CT + t, :], op0=ALU.mult, op1=ALU.add).then_inc(ccen.sem, 1)
                dve.wait_ge(cstd.sem, cstd.at(l, 1))
                v = done(V.reciprocal(std[:, :], std[:, :]))
                dve.wait_ge(vec.sem, v)
                for t in range(CT):
                    V.tensor_tensor(mixT[:, CT + t, :], mixT[:, CT + t, :], std[:, :], ALU.mult).then_inc(cmul.sem, 1)
                residual(0)

                def xmaximum(n):
                    j = (2 * n) % 8
                    dve.wait_ge(xs_mm.sem, xs_mm.at(l, n + 1))
                    v = done(V.tensor_reduce(stat[:, 0, j:j + 2],
                                             ps[sc_bank[n % 4]][:, :].rearrange("p (a m) -> p a m", a=2), AX, ALU.max))
                    dve.wait_ge(vec.sem, v)
                    V.tensor_scalar(stat[:, 1, j:j + 2], stat[:, 0, j:j + 2], -XD ** -0.5, None, ALU.mult)\
                        .then_inc(xs_max.sem, 1)

                def xnormalise(n):
                    j = (2 * n) % 8
                    dve.wait_ge(xs_exp.sem, xs_exp.at(l, 2 * n + 2))
                    v = done(V.reciprocal(stat[:, 3, j:j + 2], stat[:, 2, j:j + 2]))
                    dve.wait_ge(vec.sem, v)
                    for i in range(2):
                        p = probs[:, (n // 2) % 2, 2 * (n % 2) + i, 0:MEM]
                        V.tensor_scalar(p, p, stat[:, 3, j + i:j + i + 1], None, ALU.mult).then_inc(xs_norm.sem, 1)

                def xhead_out(h):
                    for v in range(2):
                        dve.wait_ge(xo_mm.sem, xo_mm.at(l, 2 * h + v + 1))
                        V.tensor_copy(ox[:, 2 * h + v, :], ps[4 + v][:, :]).then_inc(xo_ev.sem, 1)

                for h in range(XH + 1):
                    if h < XH:
                        for j in range(2):
                            xmaximum(2 * h + j)
                        for j in range(2):
                            xnormalise(2 * h + j)
                    if h >= 1:
                        xhead_out(h - 1)
                residual(1)
                for t in range(FT):
                    dve.wait_ge(ffn_act.sem, ffn_act.at(l, t + 1))
                    dve.wait_ge(ffn_mm.sem, ffn_mm.at(l, 2 * t + 2))
                    V.tensor_tensor(hidden[:, t, :], gates[:, t % 2, :], ps[2 * (t % 4) + 1][:, :], ALU.mult)\
                        .then_inc(ffn_ok.sem, 1)
                residual(2)
                assert behind[0] == vec.per, behind


            n2 = [0]

            def done(ins):
                ins.then_inc(vec2, 1)
                n2[0] += 1
                return n2[0]

            dve.wait_ge(p2_ev, 2)
            dve.wait_ge(mod_mm, 1)
            v = done(V.tensor_tensor(mod, ps[0][:, 0:12 * KT].rearrange("p (j w) -> p j w", w=2),
                                     par2[:, 0:6 * KT].unsqueeze(2).broadcast_to([P, 6 * KT, 2]), ALU.add))
            dve.wait_ge(vec2, v)
            for i, (which, col, norm) in enumerate(((1, 0, Q_N1), (1, 1, Q_N1), (4, 0, Q_N2))):
                V.scalar_tensor_tensor(out=gain[:, i, :], in0=mod[:, which * KT:(which + 1) * KT, col], scalar=1.0,
                                       in1=par2[:, norm:norm + KT], op0=ALU.add, op1=ALU.mult).then_inc(mod_ok, 1)
            V.tensor_copy(gain[:, 3, :], par2[:, Q_NF:Q_NF + KT]).then_inc(mod_ok, 1)

            def rms(m, src, dst, n=S):
                dve.wait_ge(n_std, m + 1)
                v = done(V.reciprocal(std[:, 0:n], std[:, 0:n]))
                dve.wait_ge(vec2, v)
                for t in range(KT):
                    V.tensor_tensor(dst[:, t, :], src[:, t, :], std[:, 0:n], ALU.mult).then_inc(n_mul, 1)

            rms(0, xT, zT)
            rms(1, ctxT, hz, CTX)
            dve.wait_ge(n_mul, 2 * KT)
            V.memset(pre[:, :, 0:2], 0.0)
            V.memset(pre[:, :, S + 2:S + 5], 0.0)
            V.memset(pre[:, :, PRE - 1:PRE], 0.0).then_inc(padded, 1)
            dve.wait_ge(n_out, 2 * KT)

            for c in range(3 * DH):
                tile = (c + DH) % (3 * DH)
                n = PRE - 3 if c < 2 * DH else S
                dve.wait_ge(pj_ev, 4 + c + 1 + (1 if c >= 2 * DH else 0))
                if c >= 2:
                    dve.wait_ge(cv_out, 2 * (c - 1) if c - 2 < 2 * DH else 4 * DH + c - 1 - 2 * DH)
                for k in range(CONV_K):
                    tap_col = taps2[:, k * 3 * DH + tile:k * 3 * DH + tile + 1]
                    x = pre[:, c % 2, k:k + n]
                    if k == 0:
                        V.tensor_scalar(acc[:, c % 2, 0:n], x, tap_col, None, ALU.mult).then_inc(cv_ok, 1)
                    else:
                        dve.wait_ge(cv_ok, CONV_K * c + k)
                        V.scalar_tensor_tensor(out=acc[:, c % 2, 0:n], in0=x, scalar=tap_col, in1=acc[:, c % 2, 0:n],
                                               op0=ALU.mult, op1=ALU.add).then_inc(cv_ok, 1)

            dve.wait_ge(small_in, 16 * 16)
            s3 = sp_s.rearrange("p (t u) -> p t u", u=U8)
            dve.wait_ge(pj_ev, 13)
            v = done(V.tensor_tensor(s3, ab[:, :, 0, :], dt_bias.unsqueeze(1).broadcast_to([P, NT, U8]), ALU.add))
            dve.wait_ge(vec2, v)
            V.scalar_tensor_tensor(out=sp_e, in0=sp_s, scalar=-1.0, in1=sp_s, op0=ALU.mult, op1=ALU.max).then_inc(ab_v, 1)

            for i in range(2 * DH):
                dve.wait_ge(l2_std, i + 1)
                n = S + CTX if i < DH else S
                v = done(V.reciprocal(acc[:, i % 2, 0:n], acc[:, i % 2, 0:n]))
                dve.wait_ge(vec2, v)
                if i < DH:
                    V.tensor_tensor(kT[:, i, CTX:], kT[:, i, CTX:], acc[:, i % 2, 0:S], ALU.mult)
                    V.tensor_tensor(kT[:, i, 0:CTX], kT[:, i, 0:CTX], acc[:, i % 2, S:S + CTX], ALU.mult).then_inc(l2_ok, 1)
                else:
                    q = qT[:, i - DH, :]
                    V.scalar_tensor_tensor(out=q, in0=q, scalar=float(P) ** -0.5, in1=acc[:, i % 2, 0:S],
                                           op0=ALU.mult, op1=ALU.mult).then_inc(l2_ok, 1)

            dve.wait_ge(ab_a, 3)
            v = done(V.scalar_tensor_tensor(out=sp_s, in0=sp_s, scalar=0.0, in1=sp_e, op0=ALU.max, op1=ALU.add))
            dve.wait_ge(vec2, v)
            V.scalar_tensor_tensor(out=la, in0=s3, scalar=-1.0, in1=a_log.unsqueeze(1).broadcast_to([P, NT, U8]),
                                   op0=ALU.mult, op1=ALU.mult).then_inc(ab_v, 1)
            dve.wait_ge(ab_v, 2)
            dve.wait_ge(ab_a, 4)
            V.tensor_scalar(nbeta, beta, -1.0, None, ALU.mult).then_inc(ab_v, 1)

            def halves(dst, src):
                for t in range(NT):
                    ins = V.tensor_tensor(dst[:, t * U8:(t + 1) * U8, :], half,
                                          src[:, t, :].unsqueeze(2).broadcast_to([P, U8, 2]), ALU.mult)
                return ins

            halves(la_half, la).then_inc(ab_v, 1)
            dve.wait_ge(ab_mm, 1)
            dve.wait_ge(ab_a, 6)
            V.tensor_tensor(tail.rearrange("p t u -> p (t u)"), ps[5][:, 0:NT * U8], gsum.rearrange("p t u -> p (t u)"),
                            ALU.subtract).then_inc(ab_v, 1)
            V.tensor_tensor(beg, beta, eg, ALU.mult).then_inc(ab_v, 1)
            dve.wait_ge(ab_a, 8)
            halves(tail_half, tail).then_inc(ab_v, 1)
            V.tensor_copy(sp_s[:, 0:1], sp_s[:, 0:1]).then_inc(ab_v, 1)

            for step in range(NT):
                x = step >= CTX // P

                def needs(e, name, at_step=step):
                    delta.wait(dve, e, at_step, name)

                def says(name, ins):
                    delta.says("dve", step, name, ins)

                def every(v8):
                    return v8.unsqueeze(2).broadcast_to([P, U8, P])

                if step:
                    needs("pool", "ETI", step - 1)
                for d in range(2):
                    r = slice(d * DH, (d + 1) * DH)
                    ins = V.tensor_tensor(E[:, r, :], tri[:, d:d + 1, :].broadcast_to([P, DH, P]),
                                          la[:, step, r].unsqueeze(2).broadcast_to([P, DH, P]), ALU.mult)
                says("TRILA", ins)
                needs("pe", "G")
                says("SUB", V.tensor_tensor(E, pair(0), every(gsum[:, step, :]), ALU.subtract))
                needs("dve", "SUB")
                says("MIN", V.tensor_scalar(E, E, 0.0, None, ALU.min))
                needs("pe", "KK")
                needs("pool", "ETS")
                says("LT", V.tensor_tensor(ETS, pair(1), ETS, ALU.mult))
                if x:
                    needs("pe", "QK")
                    needs("pool", "ETI")
                    says("QKD", V.tensor_tensor(ETI, pair(2), ETI, ALU.mult))
                needs("pe", "L")
                says("PM", V.tensor_tensor(PA, pair(1), every(nbeta[:, step, :]), ALU.mult))
                needs("act", "PT")
                says("TT0", V.tensor_tensor(TT, PTA, ident.unsqueeze(1).broadcast_to([P, U8, P]), ALU.add))
                for r in range(1, 6):
                    if r < 5:
                        needs("pe", f"SQT{r}")
                        says(f"SQT{r}", V.tensor_copy((PTA, PTB)[r % 2], pair(0)))
                    needs("pe", f"TT{r}")
                    says(f"TT{r}", V.tensor_tensor(TT, TT, pair(1 if r % 2 else 2), ALU.add))
                needs("pe", "U")
                says("U", V.tensor_copy(PA, pair(0)))
                needs("dve", "U")
                for c in range(2):
                    needs("pe", f"WS{c}")
                    for name, d, h in (("UF", 0, c), ("UB", 1, 1 - c)):
                        rows, un = slice(h * CHUNK, (h + 1) * CHUNK), slice(d * DH, (d + 1) * DH)
                        says(f"{name}{c}", V.tensor_tensor(PTA[rows, un, :], PA[rows, un, :], pair(1)[rows, un, :], ALU.subtract))
                    needs("pe", f"SU{c}")
                    needs("pool", f"SD{c}")
                    says(f"S{c}", V.tensor_tensor(ST8, SD, pair(2), ALU.add))
                if x:
                    needs("pe", "X")
                    for d in range(2):
                        t = tile_of(step, d) - CTX // P
                        o = mix2[:, 0:DH, t * P:(t + 1) * P]
                        un = slice(d * DH, (d + 1) * DH)
                        says(f"Y{d}", V.tensor_tensor(o, o, pair(3)[:, un, :], ALU.add))
                        needs("dve", f"Y{d}")
                        says(f"X{d}", V.tensor_tensor(o, o, pair(0)[:, un, :], ALU.add))

            for h in range(DH):
                dve.wait_ge(l2_std, 2 * DH + h + 1)
                r, o = head_dev[:, h, :], mix2[:, h, :]
                v = done(V.reciprocal(r, r))
                dve.wait_ge(vec2, v)
                v = done(V.scalar_tensor_tensor(out=o, in0=o, scalar=par2[:, Q_DN:Q_DN + 1], in1=r, op0=ALU.mult, op1=ALU.mult))
                dve.wait_ge(vec2, v)
                V.tensor_tensor(o, o, gateT[:, h, :], ALU.mult).then_inc(l2_ok, 1)
            for t in range(KT):
                dve.wait_ge(wo_mm, t + 1)
                V.scalar_tensor_tensor(out=xT[:, t, :], in0=ps[4 + t % 4][:, :], scalar=mod[:, 2 * KT + t, 0:1],
                                       in1=xT[:, t, :], op0=ALU.mult, op1=ALU.add).then_inc(wo_ok, 1)
            rms(2, xT, zT)

            m4, s4 = sp_s[:, 0:ST], sp_s[:, ST:2 * ST]
            logits = ps[0][:, 0:ST * NE].rearrange("p (t e) -> p t e", e=NE)
            dve.wait_ge(rt_mm, 1)
            V.tensor_reduce(m4, logits, AX, ALU.max).then_inc(rt_v, 1)
            dve.wait_ge(rt_v, 1)
            V.tensor_tensor(aff, logits, m4.unsqueeze(2).broadcast_to([P, ST, NE]), ALU.subtract).then_inc(rt_v, 1)
            dve.wait_ge(rt_a, 1)
            V.tensor_reduce(s4, aff, AX, ALU.add).then_inc(rt_v, 1)
            dve.wait_ge(rt_v, 3)
            V.reciprocal(s4, s4).then_inc(rt_v, 1)
            dve.wait_ge(rt_v, 4)
            V.tensor_tensor(aff, aff, s4.unsqueeze(2).broadcast_to([P, ST, NE]), ALU.mult).then_inc(rt_v, 1)
            rv = [5]

            def next_rt(ins):
                ins.then_inc(rt_v, 1)
                rv[0] += 1
                dve.wait_ge(rt_v, rv[0])

            work, cum, zero = squares[0:NE, 0, :], squares[0:NE, 1, :], std[0:NE, :]
            best = stat[0:NE, 0, :]
            dve.wait_ge(rt_mm, 2)
            next_rt(V.tensor_copy(work, ps[1][0:NE, :]))
            for r in range(ROUNDS):
                next_rt(V.max(best, work))
                if r == ROUNDS - 1:
                    V.memset(zero, 0.0)
                ins = V.match_replace(work, best, work, -1.0)
                next_rt(ins)
            next_rt(V.tensor_scalar(work, work, 0.0, None, ALU.is_lt))
            next_rt(V.tensor_tensor_scan(cum, zero, work, 0.0, ALU.add, ALU.add))
            next_rt(V.tensor_tensor(zero, cum, work, ALU.mult))
            assert rv[0] == POS_KNOWN, rv
            dve.wait_ge(rt_mm, 3)
            v = done(V.tensor_copy(pos, ps[2][:, 0:ST * NE].rearrange("p (t e) -> p t e", e=NE)))
            dve.wait_ge(vec2, v)
            for t in range(ST):
                V.tensor_tensor(sel[:, t, :].rearrange("p (e c) -> p e c", c=CAP),
                                iota.unsqueeze(1).broadcast_to([P, NE, CAP]),
                                pos[:, t, :].unsqueeze(2).broadcast_to([P, NE, CAP]), ALU.is_equal).then_inc(se_ok, 1)

            dve.wait_ge(xe_ev, 2 * KT)
            dve.wait_ge(sw_ev, NE // 2)
            with dve.Fori(0, NE // 2) as q:
                def tokens(j):
                    V.tensor_scalar(xs[:, j, :, :], xeT[:, :, bass.ds(q * (2 * CAP) + j * CAP, CAP)], 1.0, None, ALU.mult)\
                        .then_inc(ex_x.sem, 1)

                tokens(0)
                tokens(1)
                for j in range(2):
                    for hf in range(2):
                        n = 2 * j + hf
                        dve.wait_ge(ex_silu.sem, ex_silu.at(q, n + 1))
                        dve.wait_ge(ex_gu.sem, ex_gu.at(q, 4 * j + 2 * hf + 2))
                        V.tensor_tensor(hid[0:CAP, j, hf * 512:(hf + 1) * 512], gates[0:CAP, hf, :], ps[2 * hf + 1][0:CAP, :],
                                        ALU.mult).then_inc(ex_hid.sem, 1)
                    dve.wait_ge(used, q * (2 * EXP_CHUNKS) + C_EXP + (j + 1) * EXP_CHUNKS + NSLOT)
                    for n in range(2):
                        V.tensor_scalar(ye[j * CAP:(j + 1) * CAP, bass.ds(q, 1), n * 512:(n + 1) * 512],
                                        ps[5 + n][0:CAP, :].unsqueeze(1), 1.0, None, ALU.mult).then_inc(ex_ye.sem, 1)
            for f in range(KT):
                dve.wait_ge(cb_mm, f + 1)
                V.scalar_tensor_tensor(out=xT[:, f, :], in0=ps[f][:, :], scalar=mod[:, 5 * KT + f, 0:1], in1=xT[:, f, :],
                                       op0=ALU.mult, op1=ALU.add).then_inc(cb_ok, 1)
            rms(3, xT, zT)


def kernel(**inputs):
    import concourse.bacc as bacc
    from concourse.bass_utils import run_bass_kernel_spmd

    nc = bacc.Bacc("TRN2", target_bir_lowering=False, num_devices=1)
    arrays, aps = {}, {}
    for name, a in {**inputs, "consts": shape_constants()}.items():
        a = np.ascontiguousarray(a)
        arrays[f"in_{name}"] = a
        aps[name] = nc.dram_tensor(f"in_{name}", a.shape, mybir.dt.from_np(a.dtype), kind="ExternalInput").ap()
    out = nc.dram_tensor("out", (1, S, D), F32, kind="ExternalOutput").ap()
    build(nc, aps, out)
    r = run_bass_kernel_spmd(nc, [arrays], core_ids=[0])
    return r.results[0]["out"]
```

```python
from contextlib import ExitStack

import numpy as np

import concourse.bass as bass
from concourse import mybir

F32 = mybir.dt.float32
I32 = mybir.dt.int32
U32 = mybir.dt.uint32
F32R = mybir.dt.float32r
ACT = mybir.ActivationFunctionType
ALU = mybir.AluOpType
AX = mybir.AxisListType.X

P = 128
D = 1024
KT = D // P
S = 512
ST = S // P
MEM = 256
MT = MEM // P
DEPTH = 2
HEADS, NOPE, ROPE, VD = 8, 64, 32, 64
QK = NOPE + ROPE
LORA = 256
CW = 512
CT = CW // P
TAPS = 31
CONV0 = 2 * LORA + ROPE
IN_COLS = CONV0 + 2 * CW
XH, XD = 4, 256
FFN = 2816
FT = FFN // P
ALPHA = (2.0 * DEPTH) ** 0.25
LN_EPS = 1e-5
RMS_EPS = 1e-6
CHUNK = 64
NEG = -1e30
CTX = 256
DH = 4
CONV_K = 4
Q_BMOD, Q_N1, Q_N2, Q_NF, Q_C, Q_CC, Q_PS, Q_DN = 0, 48, 56, 64, 72, 80, 88, 92
NPAR2 = 93
NE, CAP = 16, 64
GRID_W = 64
ROWS = S // GRID_W
WINDOWS = (2, 4, 8, 16)

TWO_PI = 2.0 * np.pi
PI_A = 6.28125
PI_B = float(np.float32(int((TWO_PI - PI_A) * 2 ** 19)) / 2 ** 19)
PI_C = float(TWO_PI - PI_A - PI_B)
ROUND = 1.5 * 2.0 ** 23
PI_MAX = 3.1415925

SLOT = 4352
NSLOT = 3
LAYER_CHUNKS = 15
SLOT_CHUNKS = (5, 5, 4)
C_QKV, C_A, C_G, C_UP = 0, 1, 2, 3
C_XKV, C_MO, C_XQ, C_XO, C_FFN = 4, 8, 10, 12, 14
HALF = FT // 2
FFN_CHUNKS = 2 * (HALF + KT)
RAW = KT * 2 * P

PB_CQ, PB_KR, PB_A, PB_G, P_QN, P_KVN = 0, 4, 5, 9, 13, 15
P_DWB, P_CNG, P_CNB, P_LN = 17, 21, 25, 29
NPAR = P_LN + 6 * KT

K_ID, K_ONE, K_SWAP = 0, P, 2 * P
K_FREQ = 3 * P
N_FIRST = K_FREQ + 1
K_TRI, K_STRICT = N_FIRST, N_FIRST + 2 * P
K_SAME = K_STRICT + 2 * P
K_HALF = K_SAME + P
K_IOTA = K_HALF + 2 * 2 * DH
K_CNT = K_IOTA + CAP
NCONST = K_CNT + 4 * S
ARENA = 26744


def shape_constants():
    c = np.zeros((P, NCONST), np.float32)
    i = np.arange(P)
    same = (i[:, None] // CHUNK) == (i[None, :] // CHUNK)
    c[:, K_ID:K_ID + P] = np.eye(P)
    c[:, K_ONE:K_ONE + P] = 1.0
    h = ROPE // 2
    for j in range(h):
        c[NOPE + h + j, K_SWAP + NOPE + j] = -1.0
        c[NOPE + j, K_SWAP + NOPE + h + j] = 1.0
    before = i[:, None] <= i[None, :]
    for d, m in enumerate((before, before.T)):
        c[:, K_TRI + d * P:K_TRI + (d + 1) * P] = m & same
        c[:, K_STRICT + d * P:K_STRICT + (d + 1) * P] = m & same & (i[:, None] != i[None, :])
    c[:, K_SAME:K_SAME + P] = same
    for u in range(2 * DH):
        for n in range(2):
            c[:, K_HALF + 2 * u + n] = (i // CHUNK) == (n if u < DH else 1 - n)
    c[:, K_IOTA:K_IOTA + CAP] = np.arange(CAP) + 1
    freq = np.float32(10000.0) ** (-np.arange(0, ROPE, 2, dtype=np.float32) / np.float32(ROPE))
    c[:, K_FREQ] = freq[i % h]
    for g, w in enumerate(WINDOWS):
        def span(n):
            p = np.arange(n)
            return np.clip(p - w // 2 + w, 0, n) - np.clip(p - w // 2, 0, n)
        cnt = (span(ROWS)[:, None] * span(GRID_W)[None, :]).astype(np.float32)
        c[:, K_CNT + g * S:K_CNT + (g + 1) * S] = (np.float32(1.0) / cnt).reshape(1, S)
    return c


class Signal:

    def __init__(self, sem, per):
        self.sem, self.per = sem, per

    def at(self, layer, n):
        return layer * self.per + n


def build(nc, A, out, debug=None):
    with ExitStack() as ctx:
        def sb(name, shape, dt=F32):
            return ctx.enter_context(nc.sbuf_tensor(name, shape, dt))

        def sem(name):
            return ctx.enter_context(nc.semaphore(name))

        def signal(name, per):
            return Signal(sem(name), per)

        def place():
            return -(-nc.sbuf_base // 32) * 32

        banks = ctx.enter_context(nc.psum_tensor("banks", [P, 8, 512], F32))
        ps = [banks[:, i, :] for i in range(8)]
        ring_at = place()
        ring = sb("ring", [P, NSLOT, SLOT])
        xT = sb("xT", [P, KT, S])
        zT = sb("zT", [P, KT, S])
        arena_at = place()
        arena = sb("arena", [P, ARENA])
        consts = sb("consts", [P, N_FIRST])
        cos_at = place()
        cosT = sb("cosT", [P, S])
        sinT = sb("sinT", [P, S])
        squares = sb("squares", [P, 2, S])
        std = sb("std", [P, S])
        gates = sb("gates", [P, 2, S])
        par_rows = sb("par_rows", [P, P])
        tap_rows = sb("tap_rows", [P, P])
        par = sb("par", [P, NPAR])
        taps = sb("taps", [P, TAPS * CT])
        stat = sb("stat", [P, 4, 8])
        eps = sb("eps", [P, 2])

        def view(lo, *shape, of=None):
            n = int(np.prod(shape))
            v = (arena if of is None else of)[:, lo:lo + n]
            if len(shape) == 2:
                return v.rearrange("p (a b) -> p a b", a=shape[0])
            if len(shape) == 3:
                return v.rearrange("p (a b c) -> p a b c", a=shape[0], b=shape[1])
            return v

        BIG = 0
        memT = view(24 * S, KT, MEM)
        hpad = view(24 * S + KT * MEM, CT, TAPS - 1 + S)
        MIX = 24 * S + KT * MEM + CT * (TAPS - 1 + S)
        mixT = view(MIX, KT, S)
        probsT = view(MIX + KT * S, ST, S)
        xk = view(MIX + (KT + ST) * S, KT, MEM)
        xv = view(MIX + (KT + ST) * S + KT * MEM, MT, D)

        ident = consts[:, K_ID:K_ID + P]
        ones = consts[:, K_ONE:K_ONE + P]
        swap = consts[0:QK, K_SWAP:K_SWAP + QK]

        cqkv = view(0, 4, S)
        qh = view(4 * S, HEADS, S)
        kh = view(12 * S, HEADS, S)
        vt = view(20 * S, ST, HEADS * VD)
        xload = view(0, ST, D)
        memload = view(ST * D, MT, D)
        qx = view(0, KT, S)
        ox = view(KT * S, KT, S)

        def split(name, base, lo, n):
            return [nc.alloc_sbuf_tensor_at(f"{name}_{part}", [P, n], F32R, offset=base + 4 * (lo + i * n)).ap()
                    for i, part in enumerate(("hi", "lo"))]

        def tiles(pair, n):
            return [x.rearrange("p (t n) -> p t n", n=n) for x in pair]

        raw = [ring[:, NSLOT - 1, i * RAW:(i + 1) * RAW] for i in range(2)]
        w_split = [split(f"ffn_w{i}", ring_at, i * SLOT, RAW) for i in range(2)]
        x_split = tiles(split("ffn_x", arena_at, MIX, KT * S), S)
        h_split = tiles(split("ffn_hidden", arena_at, 0, HALF * S), S)
        kr_raw = probsT[:, 0, :]
        rope_a = probsT[:, 2, :]
        rope_b = probsT[:, 3, :]
        probs = zT[:, :, :].rearrange("p (b t) n -> p b t n", b=2)

        loaded = [sem(f"slot{i}_loaded") for i in range(NSLOT)]
        used = sem("chunks_used")
        const_in = sem("const_in")
        x_in = sem("x_in")
        rows_in = sem("rows_in")
        rows_used = sem("rows_used")
        ready = sem("fills_ready")
        turned = sem("inputs_turned")
        turned_out = sem("inputs_turned_out")
        rope_v = sem("rope_angles")
        rope_s = sem("rope_sines")
        par_mm = signal("par_turned", 2)
        par_ev = signal("par_copied", 2)
        proj_mm = signal("proj_mm", 13)
        proj_ev = signal("proj_ev", 5)
        sig_ev = signal("gate_sigmoid", 4)
        glu = signal("glu", 4)
        lsq = signal("lora_squares", 4)
        lsum = signal("lora_sums", 2)
        lstd = signal("lora_std", 2)
        lnorm = signal("lora_normed", 4)
        krot_mm = signal("krot_mm", 1)
        krot = signal("krot_parts", 2)
        kcopy = signal("kr_in_heads", 1)
        up_mm = signal("up_mm", 20)
        q_ev = signal("q_ev", 8)
        kv_ev = signal("kv_ev", 12)
        qrot_mm = signal("qrot_mm", 8)
        qrot_sin = signal("qrot_sin", 8)
        qrot_cos = signal("qrot_cos", 8)
        qrot = signal("qrot", 8)
        sc_mm = signal("scores_mm", 32)
        sc_max = signal("scores_max", 32)
        sc_exp = signal("scores_exp", 32)
        sc_norm = signal("scores_norm", 32)
        pt_mm = signal("probsT_mm", 32)
        pt_ev = signal("probsT_ev", 32)
        pv_mm = signal("pv_mm", 8)
        pv_ev = signal("pv_ev", 8)
        xkv_mm = signal("xkv_mm", 12)
        xkv_ev = signal("xkv_ev", 12)
        conv = signal("conv", CT * TAPS)
        cstat_mm = signal("conv_stat_mm", 1)
        ccen = signal("conv_centred", CT)
        csq = signal("conv_squares", CT)
        cvar = signal("conv_var_mm", CT)
        cstd = signal("conv_std", 1)
        cmul = signal("conv_scaled", CT)
        cout = signal("conv_out", CT)
        res_mm = signal("residual_mm", 4 * KT + 1)
        z_ok = signal("z_summed", 4 * KT + 1)
        mean_mm = signal("mean_mm", 3)
        cen = signal("centred", 3 * KT)
        sq_ok = signal("squared", 3 * KT)
        var_mm = signal("var_mm", 3 * KT)
        std_ok = signal("std_ok", 3)
        scaled = signal("scaled", 3 * KT)
        x_ok = signal("x_normed", 3 * KT)
        xq_mm = signal("xq_mm", KT)
        xq_ev = signal("xq_ev", KT)
        xs_mm = signal("xscores_mm", 8)
        xs_max = signal("xscores_max", 8)
        xs_exp = signal("xscores_exp", 16)
        xs_norm = signal("xscores_norm", 16)
        xt_mm = signal("xprobsT_mm", 8)
        xt_ev = signal("xprobsT_ev", 8)
        xo_mm = signal("xpv_mm", 8)
        xo_ev = signal("xpv_ev", 8)
        ffn_mm = signal("ffn_mm", 2 * FT)
        ffn_act = signal("ffn_silu", FT)
        ffn_ok = signal("ffn_hidden", FT)
        raw_in = [sem(f"ffn_chunk{i}_in") for i in range(2)]
        f_hi = signal("ffn_chunk_hi", FFN_CHUNKS)
        f_lo = signal("ffn_chunk_lo", FFN_CHUNKS)
        x_part = signal("ffn_x_split", 2 * KT)
        h_part = signal("ffn_hidden_split", 2 * FT)
        vec = signal("vector_order", 118)
        stored = [sem(f"stored{i}") for i in range(2)]

        at = [0]

        def take(*shape):
            lo = at[0]
            at[0] += int(np.prod(shape))
            return view(lo, *shape)

        NC2 = K_CNT - K_TRI
        c2 = take(NC2)
        tri = c2[:, 0:2 * P].rearrange("p (d n) -> p d n", d=2)
        strict = c2[:, K_STRICT - K_TRI:K_STRICT - K_TRI + 2 * P].rearrange("p (d n) -> p d n", d=2)
        same = c2[:, K_SAME - K_TRI:K_SAME - K_TRI + P]
        half = c2[:, K_HALF - K_TRI:K_HALF - K_TRI + 4 * DH].rearrange("p (u c) -> p u c", c=2)
        iota = c2[:, K_IOTA - K_TRI:K_IOTA - K_TRI + CAP]
        par2 = take(NPAR2)
        taps2 = take(CONV_K * 3 * DH)
        mod = take(6 * KT, 2)
        cond = take(KT, 2)
        gain = take(4, KT)
        a_log = take(2 * DH)
        dt_bias = take(2 * DH)
        w_rt = take(KT, NE)
        NT = (CTX + S) // P
        U8 = 2 * DH
        ab = take(NT, 2, U8)
        sp_s = take(NT * U8)
        sp_e = take(NT * U8)
        la = take(NT, U8)
        la_half = take(NT * U8, 2)
        beta = take(NT, U8)
        nbeta = take(NT, U8)
        eg = take(NT, U8)
        gsum = take(NT, U8)
        beg = take(NT, U8)
        tail = take(NT, U8)
        tail_half = take(NT * U8, 2)
        sdec = take(NT * U8, 2)
        at[0] = -(-at[0] // 8) * 8
        PHASE = at[0]
        kT = take(DH, NT * P)
        vT = take(DH, NT * P)
        qT = take(DH, S)
        gateT = take(DH, S)
        mix2 = take(KT, S)
        SCRATCH = at[0]
        hz = take(KT, CTX)
        ctx_in = take(CTX // P, D)
        PRE = S + CTX + 2 * (CONV_K - 1)
        pre = take(2, PRE)
        acc = take(2, PRE)
        pool_w = take(4, P)
        u = take(4, S)
        assert at[0] <= ARENA
        ctxT = view(SCRATCH + 2 * KT * CTX, KT, CTX)
        pool_a = mix2[:, 0:DH, :].rearrange("p a n -> p (a n)")
        pool_b = ctx_in.rearrange("p a n -> p (a n)")
        inv_cnt = mix2[:, DH:, :]
        at[0] = SCRATCH
        E, ETS, ETI, EG, KBG, KT0, KT1, VB, PA, PB = [take(U8, P) for _ in range(10)]
        assert at[0] <= ARENA
        zf = zT.rearrange("p a n -> p (a n)")
        PTA, PTB, TT, ST8 = [view(i * U8 * P, U8, P, of=zf) for i in range(4)]
        SD = squares.rearrange("p a (u n) -> p (a u) n", n=P)
        head_dev = view(SCRATCH, DH, S)
        at[0] = PHASE
        ye = take(NE // 2, D)
        h_tok = view(PHASE, ST, D)
        sel = view(PHASE + ST * D, ST, NE * CAP)
        at[0] = PHASE + 2 * ST * D
        sel_w = view(at[0], ST, NE * CAP)
        EC = 4 * 512
        EXP_CHUNKS = 3 * KT * D // EC
        E_RAW, E_SPLIT = 4, 3
        e_raw = [zT.rearrange("p a n -> p (a n)")[:, i * EC:(i + 1) * EC] for i in range(2)]
        e_raw += [nc.alloc_sbuf_tensor_at("expert_raw2", [P, EC], F32, offset=cos_at).ap(), view(at[0], EC)]
        e_split = [split(f"expert_w{i}", ring_at, 2 * i * EC, EC) for i in range(E_SPLIT)]
        xs, hidT = [nc.alloc_sbuf_tensor_at(name, [P, KT, 2 * CAP], F32R,
                                            offset=arena_at + 4 * (at[0] + EC + i * KT * 2 * CAP)).ap()
                    for i, name in enumerate(("expert_tokens_split", "expert_hidden_split"))]
        hid = ring.rearrange("p a n -> p (a n)")[:, 2 * E_SPLIT * EC:2 * E_SPLIT * EC + 512]
        HI, LO = slice(0, CAP), slice(CAP, 2 * CAP)
        at[0] += ST * D
        xeT = take(KT, NE * CAP)
        sel_wT = take(NE // 2, S)
        assert at[0] <= ARENA
        aff = gates[:, 0, 0:ST * NE].rearrange("p (t e) -> p t e", e=NE)
        pos = gates[:, 1, 0:ST * NE].rearrange("p (t e) -> p t e", e=NE)
        out_tok = view(PHASE, 2, D)

        def pair(i):
            return banks[:, 2 * i:2 * i + 2, :].rearrange("p b (h n) -> p (b h) n", n=P)

        def tile_of(step, d):
            n0, n1 = CTX // P, NT
            if d == 0:
                return step
            return n0 - 1 - step if step < n0 else n0 + n1 - 1 - step

        small_in = sem("small_in")
        p2_mm, p2_ev = sem("params2_turned"), sem("params2_copied")
        ctx_mm, ctx_ev = sem("ctx_turned"), sem("ctx_copied")
        cond_ok, mod_mm, mod_ok = sem("cond_silu"), sem("mod_mm"), sem("mod_ok")
        n_sq, n_mm, n_std, n_mul, n_out = (sem(f"rms_{x}") for x in ("squared", "summed", "std", "scaled", "out"))
        pj_mm, pj_ev = sem("in_proj_mm"), sem("in_proj_out")
        cv_ok, cv_out = sem("short_conv"), sem("short_conv_silu")
        l2_sq, l2_mm, l2_std, l2_ok = (sem(f"l2_{x}") for x in ("squared", "summed", "std", "ok"))
        ab_a, ab_v, ab_mm = sem("decay_act"), sem("decay_vec"), sem("decay_mm")
        pl_ok, pl_mm, pl_ev = sem("pool_step"), sem("pool_mm"), sem("pool_out")
        vec2 = sem("vector_order2")
        padded = sem("short_conv_padded")
        wo_mm, wo_ok = sem("out_proj_mm"), sem("out_proj_ok")
        rt_mm, rt_v, rt_a = sem("router_mm"), sem("router_vec"), sem("router_act")
        ht_mm, ht_ev = sem("h_turned"), sem("h_copied")
        se_ok, sw_ok = sem("slots_known"), sem("slots_weighted")
        xe_mm, xe_ev = sem("gathered_mm"), sem("gathered")
        sw_mm, sw_ev = sem("slots_turned"), sem("slots_copied")
        e_lo = Signal(sem("expert_chunk_lo"), 2 * EXP_CHUNKS)
        e_used = Signal(sem("expert_chunk_used"), 2 * EXP_CHUNKS)
        e_hi = Signal(sem("expert_chunk_hi"), 2 * EXP_CHUNKS)
        e_in = [sem(f"expert_chunk{i}_in") for i in range(E_RAW)]
        ex_x = Signal(sem("expert_tokens"), 4)
        ex_silu = Signal(sem("expert_silu"), 4)
        ex_hid = Signal(sem("expert_hidden"), 4)
        ex_tm = Signal(sem("expert_hidden_turned"), 4)
        ex_ht = Signal(sem("expert_hidden_hi"), 4)
        ex_hl = Signal(sem("expert_hidden_lo"), 4)
        ex_yb = Signal(sem("expert_out_lo"), 4)
        ex_ye = Signal(sem("expert_out"), 4)
        cb_mm, cb_ok = sem("combine_mm"), sem("combine_ok")
        fin_mm, fin_ev = sem("out_turned"), sem("out_copied")

        def events(step):
            x = step >= CTX // P
            r5 = range(1, 6)
            return {
                "pe": ["G", "KK"] + x * ["QK"] + ["KTOK", "VTOK", "L", "PT"]
                + [f"{n}{r}" for r in r5 for n in (("SQ", "SQT", "TT") if r < 5 else ("SQ", "TT"))]
                + ["WT", "U", "WS0"] + x * ["Y0"] + ["SU0", "WS1"] + x * ["Y1"] + ["SU1"] + x * ["X"],
                "dve": ["TRILA", "SUB", "MIN", "LT"] + x * ["QKD"] + ["PM", "TT0"]
                + [f"{n}{r}" for r in r5 for n in (("SQT", "TT") if r < 5 else ("TT",))]
                + ["U"] + [f"{n}{c}" for c in (0, 1) for n in ("UF", "UB", "S")] + x * ["Y0", "X0", "Y1", "X1"],
                "act": ["E"] + x * ["EG"] + ["KTOK", "VTOK", "PT"] + [f"SQ{r}" for r in r5] + ["WT"],
                "pool": ["ETS", "ETI"] + x * ["QD"] + ["KBG", "KT0", "KT1", "VB", "SD0", "SD1"],
            }

        class Delta:

            def __init__(self):
                self.sem = {e: sem(f"delta_{e}") for e in ("pe", "dve", "act", "pool")}
                self.value = {}
                n = {e: 0 for e in self.sem}
                for step in range(NT):
                    for e, names in events(step).items():
                        for name in names:
                            n[e] += 1
                            self.value[e, step, name] = n[e]
                self.said = {e: 0 for e in self.sem}

            def says(self, e, step, name, ins):
                self.said[e] += 1
                assert self.value[e, step, name] == self.said[e], (e, step, name)
                ins.then_inc(self.sem[e], 1)

            def wait(self, eng, e, step, name):
                eng.wait_ge(self.sem[e], self.value[e, step, name])

            def last(self, e):
                return max(v for (x, _, _), v in self.value.items() if x == e)

        delta = Delta()
        POOL_STEPS = list(np.cumsum([6 + 2 * int(np.log2(win)) for win in WINDOWS]))
        POOL_STEPS = [int(n) for n in POOL_STEPS] + [int(POOL_STEPS[-1]) + 1]
        ROUNDS = CAP // 8
        POS_KNOWN = 5 + 1 + 2 * ROUNDS + 3
        LAYERS_DONE = DEPTH * x_ok.per
        C2 = DEPTH * LAYER_CHUNKS
        C_MOD, C_IN, C_OUT2 = C2, C2 + 12, C2 + 17
        DW = DH * P
        IN_RANGES = ((3 * DW + 16 + DW, 4 * DW + 16 + DW), (DW, 2 * DW), (2 * DW, 3 * DW + 16), (0, DW),
                     (3 * DW + 16, 4 * DW + 16))

        def slot(c):
            return c % NSLOT

        def arrivals(c):
            return 32 * (DEPTH * SLOT_CHUNKS[slot(c)] + (c - C2) // NSLOT + 1)

        def ffn_chunk(n):
            half_no, i = n // (HALF + KT), n % (HALF + KT)
            return (half_no, half_no * HALF + i, True) if i < HALF else (half_no, i - HALF, False)

        def ffn_floats(n):
            return RAW if ffn_chunk(n)[2] else HALF * P

        def ffn_used(eng, l, n):
            half_no, t, hidden_tile = ffn_chunk(n)
            if hidden_tile:
                eng.wait_ge(ffn_mm.sem, ffn_mm.at(l, 2 * t + 2))
            else:
                eng.wait_ge(res_mm.sem, res_mm.at(l, (2 + half_no) * KT + t + 1))

        def w(c, lo, *shape):
            n = int(np.prod(shape))
            v = ring[:, slot(c), lo:lo + n]
            if len(shape) == 2:
                return v.rearrange("p (a b) -> p a b", a=shape[0])
            return v.rearrange("p (a b c) -> p a b c", a=shape[0], b=shape[1])

        block = ctx.enter_context(nc.Block())

        @block.sync
        def _(sp):
            sp.dma_start(consts[:, :], A["consts"][:, 0:N_FIRST]).then_inc(const_in, 16)
            sp.dma_start(rope_a.bitcast(I32), A["positions"].broadcast_to([P, S])).then_inc(const_in, 16)
            sp.dma_start(xload, A["x"][0].rearrange("(t p) d -> p t d", p=P)).then_inc(x_in, 16)
            sp.dma_start(memload, A["mem"][0].rearrange("(t p) d -> p t d", p=P)).then_inc(x_in, 16)
            sp.wait_ge(ready, 2)

            with sp.Fori(0, DEPTH) as l:
                def layer(name):
                    return A[name][bass.ds(l, 1)]

                def row(dst, name, lo, n):
                    src = layer(name)[:, lo:lo + n * P].rearrange("a (r c) -> (a r) c", c=P)
                    sp.dma_start(par_rows[dst:dst + n, :], src).then_inc(rows_in, 16)

                def load(c, halves):
                    sp.wait_ge(used, l * LAYER_CHUNKS + c + 1)
                    for dst, src in halves:
                        sp.dma_start(dst, src).then_inc(loaded[slot(c)], 16)

                def matrix(c, name, lo, n, lo2=None):
                    src = layer(name).rearrange("a (k p) n -> p (a k) n", p=P)
                    m = KT // 2
                    if lo2 is None:
                        dst = w(c, 0, KT, n)
                        load(c, [(dst[:, h * m:(h + 1) * m], src[:, h * m:(h + 1) * m, lo:lo + n])
                                 for h in range(2)])
                    else:
                        load(c, [(w(c, h * KT * n, KT, n), src[:, :, at:at + n])
                                 for h, at in enumerate((lo, lo2))])

                matrix(C_QKV, "mix_w_in", 0, CONV0)
                sp.wait_ge(rows_used, l + 1)
                row(PB_CQ, "mix_b_in", 0, 4)
                sp.dma_start(par_rows[PB_KR:PB_KR + 1, 0:QK],
                             layer("mix_b_in")[:, CONV0 - QK:CONV0]).then_inc(rows_in, 16)
                row(PB_A, "mix_b_in", CONV0, 2 * CT)
                row(P_QN, "mla_q_norm", 0, 2)
                row(P_KVN, "mla_kv_norm", 0, 2)
                row(P_DWB, "conv_dw_b", 0, CT)
                row(P_CNG, "conv_norm_g", 0, CT)
                row(P_CNB, "conv_norm_b", 0, CT)
                for j, name in enumerate(("ln1_g", "ln1_b", "ln2_g", "ln2_b", "ln3_g", "ln3_b")):
                    row(P_LN + j * KT, name, 0, KT)
                sp.dma_start(tap_rows[0:TAPS * CT, :],
                             layer("conv_dw_w").rearrange("a k (t p) -> (a k t) p", p=P)).then_inc(rows_in, 16)
                matrix(C_A, "mix_w_in", CONV0, CW)
                matrix(C_G, "mix_w_in", CONV0 + CW, CW)
                nq, nkv = HEADS * QK, HEADS * (NOPE + VD)
                load(C_UP, [(w(C_UP, 0, 2, nq), layer("mla_w_uq").rearrange("a (k p) n -> p (a k) n", p=P)),
                            (w(C_UP, 2 * nq, 2, nkv), layer("mla_w_ukv").rearrange("a (k p) n -> p (a k) n", p=P))])
                for j in range(4):
                    matrix(C_XKV + j, "xa_w_kv", j * 512, 512)
                for j in range(2):
                    matrix(C_MO + j, "mix_w_o", j * 512, 512)
                for j in range(2):
                    matrix(C_XQ + j, "xa_w_q", j * 512, 512)
                for j in range(2):
                    matrix(C_XO + j, "xa_w_o", j * 512, 512)
                gate_up = layer("ffn_w_in").rearrange("a (k p) n -> p (a k) n", p=P)
                down = layer("ffn_w_down").rearrange("a (k p) n -> p (a k) n", p=P)
                for n in range(FFN_CHUNKS):
                    half_no, t, hidden_tile = ffn_chunk(n)
                    if n == 0:
                        sp.wait_ge(used, l * LAYER_CHUNKS + C_FFN + 1)
                    if n >= 2:
                        sp.wait_ge(f_lo.sem, f_lo.at(l, n - 1))
                    if hidden_tile:
                        dst = raw[n % 2].rearrange("p (j k c) -> p j k c", j=2, k=KT)
                        for j in range(2):
                            lo = j * FFN + t * P
                            sp.dma_start(dst[:, j], gate_up[:, :, lo:lo + P]).then_inc(raw_in[n % 2], 16)
                    else:
                        dst = raw[n % 2][:, 0:HALF * P].rearrange("p (k c) -> p k c", c=P)
                        for a, b in ((0, HALF // 2), (HALF // 2, HALF)):
                            k0 = half_no * HALF
                            sp.dma_start(dst[:, a:b], down[:, k0 + a:k0 + b, t * P:(t + 1) * P]).then_inc(raw_in[n % 2], 16)
            sp.wait_ge(rows_used, DEPTH + 1)
            for dst, name, n in ((Q_BMOD, "b_mod_2", 6 * KT), (Q_N1, "norm1_2", KT), (Q_N2, "norm2_2", KT),
                                 (Q_C, "c_2", KT), (Q_PS, "pool_scale_2", 4), (Q_DN, "dn_norm_2", 1)):
                sp.dma_start(par_rows[dst:dst + n, :], A[name].rearrange("a (r c) -> (a r) c", c=P)).then_inc(small_in, 16)
            for dst, name in ((Q_NF, "norm_f_2"), (Q_CC, "c_ctx_2")):
                sp.dma_start(par_rows[dst:dst + KT, :], A[name].rearrange("(r c) -> r c", c=P)).then_inc(small_in, 16)
            sp.dma_start(tap_rows[0:CONV_K * 3 * DH, :],
                         A["conv_w_2"].rearrange("a k (t p) -> (a k t) p", p=P)).then_inc(small_in, 16)

            def load2(c, halves):
                sp.wait_ge(used, c + 1)
                for dst, src in halves:
                    sp.dma_start(dst, src).then_inc(loaded[slot(c)], 16)

            def matrix2(c, src, lo, hi):
                src = src.rearrange("(k p) n -> p k n", p=P)
                dst, m = w(c, 0, KT, hi - lo), KT // 2
                load2(c, [(dst[:, h * m:(h + 1) * m], src[:, h * m:(h + 1) * m, lo:hi]) for h in range(2)])

            for j in range(NSLOT):
                matrix2(C_MOD + j, A["w_mod_2"][0], j * 512, (j + 1) * 512)
            sp.wait_ge(x_ok.sem, LAYERS_DONE)
            sp.dma_start(c2, A["consts"][:, K_TRI:K_CNT]).then_inc(small_in, 16)
            sp.dma_start(inv_cnt, A["consts"][:, K_CNT:].rearrange("p (g n) -> p g n", g=4)).then_inc(small_in, 16)
            sp.dma_start(a_log, A["a_log_2"].rearrange("a d h -> a (d h)").broadcast_to([P, U8])).then_inc(small_in, 16)
            sp.dma_start(dt_bias, A["dt_bias_2"].rearrange("a d h -> a (d h)").broadcast_to([P, U8])).then_inc(small_in, 16)
            sp.dma_start(w_rt, A["w_router_2"][0].rearrange("(k p) n -> p k n", p=P)).then_inc(small_in, 16)
            sp.dma_start(pool_w, A["pool_w_2"][0].rearrange("g c d -> c g d")).then_inc(small_in, 16)
            sp.dma_start(ctx_in, A["ctx_2"][0].rearrange("(t p) d -> p t d", p=P)).then_inc(small_in, 16)
            for j in range(NSLOT, 12):
                matrix2(C_MOD + j, A["w_mod_2"][0], j * 512, (j + 1) * 512)
            for j, (lo, hi) in enumerate(IN_RANGES):
                matrix2(C_IN + j, A["w_in_2"][0], lo, hi)
            for j in range(2):
                matrix2(C_OUT2 + j, A["w_out_2"][0], j * 512, (j + 1) * 512)
            with sp.Fori(0, NE) as e:
                for c in range(EXP_CHUNKS):
                    sp.wait_ge(e_lo.sem, e * EXP_CHUNKS + c + 1)
                    name = ("w_gate_2", "w_up_2")[c // 2 % 2] if c < 8 else "w_down_2"
                    src = A[name][0][bass.ds(e, 1)].rearrange("a (k p) n -> p (a k) n", p=P)
                    if c < 8:
                        k0, n0 = 4 * (c % 2), 512 * (c // 4)
                        src = src[:, k0:k0 + 4, n0:n0 + 512]
                    else:
                        src = src[:, 2 * (c - 8):2 * (c - 8) + 2, :]
                    dst = e_raw[c % E_RAW].rearrange("p (k n) -> p k n", k=4 if c < 8 else 2)
                    sp.dma_start(dst, src).then_inc(e_in[c % E_RAW], 16)
            for t in range(ST):
                sp.wait_ge(fin_ev, 2 * (t + 1))
                sp.dma_start(out[0, t * P:(t + 1) * P, :], out_tok[:, t % 2, :]).then_inc(stored[t % 2], 16)
            for i in range(2):
                sp.wait_ge(stored[i], 16 * ST // 2)

        @block.tensor
        def _(pe):
            pe.sem_inc(used, NSLOT)
            pe.sem_inc(rows_used, 1)
            pe.wait_ge(const_in, 32)
            pe.wait_ge(x_in, 32)
            for f in range(2 * KT):
                if f >= 4:
                    pe.wait_ge(turned_out, f - 3)
                src, n = (xload, ST) if f < KT else (memload, MT)
                for t in range(n):
                    mm = pe.transpose(ps[f % 4][:, t * P:(t + 1) * P],
                                      src[:, t, (f % KT) * P:(f % KT + 1) * P], ident)
                mm.then_inc(turned, 1)
            pe.wait_ge(turned_out, 2 * KT)

            with pe.Fori(0, DEPTH) as l:
                def arrived(c):
                    pe.wait_ge(loaded[slot(c)], l * (32 * SLOT_CHUNKS[slot(c)]) + 32 * (c // NSLOT + 1))

                spent = [0]

                def give_back(n):
                    spent[0] += n

                def say_spent(mm):
                    if spent[0]:
                        mm.then_inc(used, spent[0])
                        spent[0] = 0

                def product(bank, weights, rhs, n=KT, width=S, m=P):
                    for k in range(n):
                        mm = pe.matmul(bank[0:m, 0:width], weights(k), rhs(k), start=(k == 0), stop=(k == n - 1))
                        if k == 0:
                            say_spent(mm)
                    return mm

                def residual(i, weights, rhs, n, chunk, per_chunk, keep=False):
                    for t in range(KT):
                        if t % per_chunk == 0:
                            arrived(chunk + t // per_chunk)
                        if t >= 4:
                            pe.wait_ge(z_ok.sem, z_ok.at(l, i * KT + t - 3))
                        mm = product(ps[4 + t % 4], lambda k: weights(t, k), rhs, n)
                        mm.then_inc(res_mm.sem, 1)
                        if t % per_chunk == per_chunk - 1 and not keep:
                            give_back(1)

                def norm_sums(i, z0, bank):
                    for t in range(KT):
                        pe.wait_ge(z_ok.sem, z_ok.at(l, z0 + t + 1))
                        mm = pe.matmul(ps[bank][:, :], ones, zT[:, t, :], start=(t == 0), stop=(t == KT - 1))
                        if t == 0:
                            say_spent(mm)
                    mm.then_inc(mean_mm.sem, 1)
                    for t in range(KT):
                        pe.wait_ge(sq_ok.sem, sq_ok.at(l, i * KT + t + 1))
                        mm = pe.matmul(ps[bank + 1][:, :], ones, squares[:, t % 2, :], start=(t == 0), stop=(t == KT - 1))
                        mm.then_inc(var_mm.sem, 1)

                def split_product(bank, weights, rhs, n, need):
                    for k in range(n):
                        need(k)
                        for wp, rp in ((0, 0), (0, 1), (1, 0)):
                            mm = pe.matmul(bank[:, :], weights(wp, k), rhs(rp, k), start=(k == 0 and wp == rp),
                                           stop=(k == n - 1 and wp == 1))
                    return mm

                pe.wait_ge(rows_in, l * (15 * 16) + 15 * 16)
                pe.transpose(ps[6][:, 0:P], par_rows[:, :], ident).then_inc(par_mm.sem, 1)
                pe.transpose(ps[7][:, 0:P], tap_rows[:, :], ident).then_inc(par_mm.sem, 1)
                pe.wait_ge(par_ev.sem, par_ev.at(l, 2))
                pe.sem_inc(rows_used, 1)

                arrived(C_QKV)
                wq = w(C_QKV, 0, KT, CONV0)
                for n in range(5):
                    lo, m = (n * P, P) if n < 4 else (CONV0 - QK, QK)
                    mm = product(ps[n], lambda k: wq[:, k, lo:lo + m], lambda k: xT[:, k, :], m=m)
                    mm.then_inc(proj_mm.sem, 1)
                give_back(1)
                arrived(C_A)
                arrived(C_G)
                for t in range(CT):
                    for j in range(2):
                        n = 5 + 2 * t + j
                        if n >= 8:
                            pe.wait_ge(proj_ev.sem, proj_ev.at(l, n - 7))
                        wc = w(C_A + j, 0, KT, CW)
                        mm = product(ps[n % 8], lambda k: wc[:, k, t * P:(t + 1) * P], lambda k: xT[:, k, :])
                        mm.then_inc(proj_mm.sem, 1)
                give_back(2)

                pe.wait_ge(glu.sem, glu.at(l, 2))
                for n in range(2):
                    for k in range(2):
                        pe.wait_ge(lsq.sem, lsq.at(l, 2 * n + k + 1))
                        mm = pe.matmul(ps[5 + n][:, :], ones, mixT[:, 2 * n + k, :], start=(k == 0), stop=(k == 1))
                    mm.then_inc(lsum.sem, 1)
                pe.wait_ge(proj_ev.sem, proj_ev.at(l, 5))
                pe.matmul(ps[7][0:QK, :], swap, kr_raw[0:QK, :], start=True, stop=True).then_inc(krot_mm.sem, 1)

                arrived(C_UP)
                wuq = w(C_UP, 0, 2, HEADS * QK)
                wukv = w(C_UP, 2 * HEADS * QK, 2, HEADS * (NOPE + VD))
                wv = w(C_UP, 2 * HEADS * QK, 2, HEADS, NOPE + VD)
                pe.wait_ge(glu.sem, glu.at(l, CT))
                pe.wait_ge(lnorm.sem, lnorm.at(l, 2))
                for h in range(HEADS):
                    if h == 7:
                        pe.wait_ge(krot.sem, krot.at(l, 2))
                    if h == 5:
                        pe.wait_ge(lnorm.sem, lnorm.at(l, 4))
                    mm = product(ps[h], lambda k: wuq[:, k, h * QK:(h + 1) * QK], lambda k: cqkv[:, k, :], 2, m=QK)
                    mm.then_inc(up_mm.sem, 1)
                for h in range(HEADS):
                    pe.wait_ge(q_ev.sem, q_ev.at(l, h + 1))
                    lo = h * (NOPE + VD)
                    mm = product(ps[h], lambda k: wukv[:, k, lo:lo + NOPE], lambda k: cqkv[:, 2 + k, :], 2, m=NOPE)
                    mm.then_inc(up_mm.sem, 1)
                for t in range(ST):
                    pe.wait_ge(kv_ev.sem, kv_ev.at(l, t + 1))
                    mm = product(ps[t], lambda k: cqkv[:, 2 + k, t * P:(t + 1) * P], lambda k: wv[:, k, :, NOPE:], 2)
                    mm.then_inc(up_mm.sem, 1)
                give_back(1)
                for h in range(HEADS):
                    b = 4 + h % 4
                    pe.wait_ge(kv_ev.sem, kv_ev.at(l, 5 + h % 4))
                    if h >= 4:
                        pe.wait_ge(qrot_sin.sem, qrot_sin.at(l, h - 3))
                    pe.matmul(ps[b][0:QK, :], swap, qh[0:QK, h, :], start=True, stop=True).then_inc(qrot_mm.sem, 1)

                sc_bank = (0, 1, 6, 7)

                def scores(h):
                    pe.wait_ge(qrot.sem, qrot.at(l, h + 1))
                    for t in range(ST):
                        n = h * ST + t
                        if n == 0:
                            pe.wait_ge(kv_ev.sem, kv_ev.at(l, 12))
                            pe.wait_ge(kcopy.sem, kcopy.at(l, 1))
                            pe.wait_ge(qrot_sin.sem, qrot_sin.at(l, HEADS))
                        if n >= 4:
                            pe.wait_ge(sc_exp.sem, sc_exp.at(l, n - 3))
                        pe.matmul(ps[sc_bank[t]][:, 0:(t + 1) * P], qh[0:QK, h, t * P:(t + 1) * P],
                                  kh[0:QK, h, 0:(t + 1) * P], start=True, stop=True).then_inc(sc_mm.sem, 1)

                def values(h):
                    for kt in range(ST):
                        n = h * ST + kt
                        if n >= 2:
                            pe.wait_ge(pt_ev.sem, pt_ev.at(l, n - 1))
                        for t in range(kt, ST):
                            if kt == 0:
                                pe.wait_ge(sc_norm.sem, sc_norm.at(l, h * ST + t + 1))
                            mm = pe.transpose(ps[2 + n % 2][:, t * P:(t + 1) * P],
                                              probs[:, h % 2, t, kt * P:(kt + 1) * P], ident)
                        mm.then_inc(pt_mm.sem, 1)
                    if h >= 2:
                        pe.wait_ge(pv_ev.sem, pv_ev.at(l, h - 1))
                    for kt in range(ST):
                        pe.wait_ge(pt_ev.sem, pt_ev.at(l, h * ST + kt + 1))
                        mm = pe.matmul(ps[4 + h % 2][0:VD, kt * P:S], vt[:, kt, h * VD:(h + 1) * VD],
                                       probsT[:, kt, kt * P:S], start=(kt == 0), stop=(kt == ST - 1))
                    mm.then_inc(pv_mm.sem, 1)

                for h in range(HEADS + 1):
                    if h < HEADS:
                        scores(h)
                    if h >= 1:
                        values(h - 1)

                pe.wait_ge(sc_exp.sem, sc_exp.at(l, 32))
                for n in range(12):
                    b = sc_bank[n % 4]
                    c = C_XKV + (n // 4 if n < 8 else 2 + (n - 8) % 2)
                    if n in (0, 4, 8, 9):
                        arrived(c)
                    if n >= 4:
                        pe.wait_ge(xkv_ev.sem, xkv_ev.at(l, n - 3))
                    wkv = w(c, 0, KT, 512)
                    if n < 8:
                        mm = product(ps[b], lambda k: wkv[:, k, (n % 4) * P:(n % 4 + 1) * P],
                                     lambda k: memT[:, k, :], width=MEM)
                    else:
                        t = (n - 8) // 2
                        mm = product(ps[b], lambda k: memT[:, k, t * P:(t + 1) * P], lambda k: wkv[:, k, :])
                    mm.then_inc(xkv_mm.sem, 1)
                    if n in (3, 7):
                        give_back(1)
                give_back(2)

                pe.wait_ge(pt_ev.sem, pt_ev.at(l, 32))
                for t in range(CT):
                    pe.wait_ge(conv.sem, conv.at(l, CT * (TAPS - 1) + t + 1))
                    mm = pe.matmul(ps[2][:, :], ones, mixT[:, CT + t, :], start=(t == 0), stop=(t == CT - 1))
                mm.then_inc(cstat_mm.sem, 1)
                for t in range(CT):
                    pe.wait_ge(csq.sem, csq.at(l, t + 1))
                    mm = pe.matmul(ps[3][:, :], ones, squares[:, t % 2, :], start=(t == 0), stop=(t == CT - 1))
                    mm.then_inc(cvar.sem, 1)

                pe.wait_ge(pv_ev.sem, pv_ev.at(l, HEADS))
                pe.wait_ge(xkv_ev.sem, xkv_ev.at(l, 12))
                pe.wait_ge(cout.sem, cout.at(l, CT))
                residual(0, lambda t, k: w(C_MO + t // 4, 0, KT, 512)[:, k, (t % 4) * P:(t % 4 + 1) * P],
                         lambda k: mixT[:, k, :], KT, C_MO, 4)
                norm_sums(0, 0, 0)

                pe.wait_ge(x_ok.sem, x_ok.at(l, KT))
                for t in range(KT):
                    if t % 4 == 0:
                        arrived(C_XQ + t // 4)
                    if t >= 4:
                        pe.wait_ge(xq_ev.sem, xq_ev.at(l, t - 3))
                    wx = w(C_XQ + t // 4, 0, KT, 512)
                    mm = product(ps[2 + t % 4], lambda k: wx[:, k, (t % 4) * P:(t % 4 + 1) * P], lambda k: xT[:, k, :])
                    mm.then_inc(xq_mm.sem, 1)
                    if t % 4 == 3:
                        give_back(1)

                def xscores(h):
                    pe.wait_ge(xq_ev.sem, xq_ev.at(l, min(2 * h + 2, KT)))
                    for j in range(2):
                        n = 2 * h + j
                        if n >= 4:
                            pe.wait_ge(xs_exp.sem, xs_exp.at(l, 2 * (n - 3)))
                        for i in range(2):
                            t = 2 * j + i
                            for k in range(2):
                                mm = pe.matmul(ps[sc_bank[n % 4]][:, i * MEM:(i + 1) * MEM],
                                               qx[:, 2 * h + k, t * P:(t + 1) * P], xk[:, 2 * h + k, :],
                                               start=(k == 0), stop=(k == 1))
                        mm.then_inc(xs_mm.sem, 1)

                def xvalues(h):
                    for kt in range(MT):
                        n = 2 * h + kt
                        if n >= 2:
                            pe.wait_ge(xt_ev.sem, xt_ev.at(l, n - 1))
                        else:
                            pe.wait_ge(xq_ev.sem, xq_ev.at(l, KT))
                        for t in range(ST):
                            if kt == 0:
                                pe.wait_ge(xs_norm.sem, xs_norm.at(l, ST * h + t + 1))
                            mm = pe.transpose(ps[2 + kt][:, t * P:(t + 1) * P],
                                              probs[:, h % 2, t, kt * P:(kt + 1) * P], ident)
                        mm.then_inc(xt_mm.sem, 1)
                    for v in range(2):
                        n = 2 * h + v
                        if n >= 2:
                            pe.wait_ge(xo_ev.sem, xo_ev.at(l, n - 1))
                        for kt in range(MT):
                            pe.wait_ge(xt_ev.sem, xt_ev.at(l, 2 * h + kt + 1))
                            mm = pe.matmul(ps[4 + v][:, :], xv[:, kt, h * XD + v * P:h * XD + (v + 1) * P],
                                           probsT[:, kt, :], start=(kt == 0), stop=(kt == MT - 1))
                        mm.then_inc(xo_mm.sem, 1)

                for h in range(XH + 1):
                    if h < XH:
                        xscores(h)
                    if h >= 1:
                        xvalues(h - 1)
                pe.wait_ge(xo_ev.sem, xo_ev.at(l, KT))
                residual(1, lambda t, k: w(C_XO + t // 4, 0, KT, 512)[:, k, (t % 4) * P:(t % 4 + 1) * P],
                         lambda k: ox[:, k, :], KT, C_XO, 4, keep=True)
                norm_sums(1, KT, 0)

                out_bank = (6, 7, 0, 1)
                for n in range(FFN_CHUNKS):
                    half_no, t, hidden_tile = ffn_chunk(n)
                    pe.wait_ge(f_lo.sem, f_lo.at(l, n + 1))
                    if hidden_tile:
                        if t >= 4:
                            pe.wait_ge(ffn_ok.sem, ffn_ok.at(l, t - 3))
                        if t in (HALF, HALF + 1):
                            pe.wait_ge(z_ok.sem, z_ok.at(l, 2 * KT + (6 if t == HALF else KT)))

                        def x_ready(k):
                            if t == 0:
                                pe.wait_ge(x_part.sem, x_part.at(l, min(2 * k + 3, 2 * KT)))

                        for j in range(2):
                            wf = [x.rearrange("p (j k c) -> p j k c", j=2, k=KT) for x in w_split[n % 2]]
                            mm = split_product(ps[2 * (t % 4) + j], lambda i, k: wf[i][:, j, k, :],
                                               lambda i, k: x_split[i][:, k, :], KT, x_ready)
                            mm.then_inc(ffn_mm.sem, 1)
                    else:
                        if t == 0:
                            pe.wait_ge(ffn_ok.sem, ffn_ok.at(l, half_no * HALF + HALF - 2))
                        if t >= 4:
                            pe.wait_ge(z_ok.sem, z_ok.at(l, (2 + half_no) * KT + t - 3))

                        def hidden_ready(k):
                            if t == 0:
                                pe.wait_ge(h_part.sem, h_part.at(l, 2 * (half_no * HALF + k) + 2))

                        wd = [x[:, 0:HALF * P].rearrange("p (k c) -> p k c", c=P) for x in w_split[n % 2]]
                        mm = split_product(ps[out_bank[t % 4]], lambda i, k: wd[i][:, k, :],
                                           lambda i, k: h_split[i][:, k, :], HALF, hidden_ready)
                        mm.then_inc(res_mm.sem, 2 if n == FFN_CHUNKS - 1 else 1)
                give_back(LAYER_CHUNKS - C_XO)
                norm_sums(2, 3 * KT, 2)
                pe.wait_ge(x_ok.sem, x_ok.at(l, 3 * KT))

            def arrived2(c):
                pe.wait_ge(loaded[slot(c)], arrivals(c))

            spent = [0]

            def give_back(n):
                spent[0] += n

            def say_spent(mm):
                if spent[0]:
                    mm.then_inc(used, spent[0])
                    spent[0] = 0

            def product(out, weights, rhs, n=KT):
                for k in range(n):
                    mm = pe.matmul(out, weights(k), rhs(k), start=(k == 0), stop=(k == n - 1))
                    if k == 0:
                        say_spent(mm)
                return mm

            pe.wait_ge(small_in, 16 * 16)
            pe.transpose(ps[6][:, 0:P], par_rows[:, :], ident).then_inc(p2_mm, 1)
            pe.transpose(ps[7][:, 0:P], tap_rows[:, :], ident).then_inc(p2_mm, 1)
            for f in range(KT):
                if f >= 4:
                    pe.wait_ge(ctx_ev, f - 3)
                for t in range(CTX // P):
                    mm = pe.transpose(ps[2 + f % 4][:, t * P:(t + 1) * P], ctx_in[:, t, f * P:(f + 1) * P], ident)
                mm.then_inc(ctx_mm, 1)

            pe.wait_ge(cond_ok, 2)
            for j in range(6 * KT):
                if j % 4 == 0:
                    arrived2(C_MOD + j // 4)
                wm = w(C_MOD + j // 4, 0, KT, 512)
                mm = product(ps[0][:, 2 * j:2 * j + 2], lambda k: wm[:, k, (j % 4) * P:(j % 4 + 1) * P], lambda k: cond[:, k, :])
                if j % 4 == 3 and j + 1 < 6 * KT:
                    give_back(1)
            mm.then_inc(mod_mm, 1)
            give_back(1)

            def rms_sums(m, n=S):
                for t in range(KT):
                    pe.wait_ge(n_sq, m * KT + t + 1)
                    mm = pe.matmul(ps[1 + m % 2][:, 0:n], ones, squares[:, t % 2, 0:n], start=(t == 0), stop=(t == KT - 1))
                    mm.then_inc(n_mm, 1)

            rms_sums(0)
            rms_sums(1, CTX)

            pe.wait_ge(mod_ok, 4)
            pe.wait_ge(n_out, 2 * KT)
            g = 0
            for j in range(5):
                c = C_IN + j
                arrived2(c)
                lo, hi = IN_RANGES[j]
                wi = w(c, 0, KT, hi - lo)
                for t in range(4):
                    if g >= 4:
                        pe.wait_ge(pj_ev, g - 3)
                    wt = lambda k: wi[:, k, t * P:(t + 1) * P]
                    mm = product(ps[2 * (g % 4)], wt, lambda k: zT[:, k, :])
                    if j in (1, 2):
                        mm = product(ps[2 * (g % 4) + 1][:, 0:CTX], wt, lambda k: hz[:, k, :])
                    mm.then_inc(pj_mm, 1)
                    g += 1
                if j == 2:
                    pe.wait_ge(pj_ev, g - 3)
                    for t in range(NT):
                        src, t0 = (hz, t) if t < CTX // P else (zT, t - CTX // P)
                        mm = product(ps[2 * (g % 4)][:, 16 * t:16 * t + 16], lambda k: src[:, k, t0 * P:(t0 + 1) * P],
                                     lambda k: wi[:, k, 4 * P:4 * P + 16])
                    mm.then_inc(pj_mm, 1)
                    g += 1
                give_back(1)

            for i in range(2 * DH):
                b = 2 * (i % 2)
                if i < 2:
                    pe.wait_ge(pj_ev, g - 2 + i)
                if i >= 2:
                    pe.wait_ge(l2_std, i - 1)
                pe.wait_ge(l2_sq, i + 1)
                mm = pe.matmul(ps[b][:, :], ones, pre[:, i % 2, 0:S], start=True, stop=True)
                say_spent(mm)
                mm = pe.matmul(ps[b + 1][:, 0:CTX], ones, pre[:, i % 2, S:S + CTX], start=True, stop=True)
                mm.then_inc(l2_mm, 1)

            pe.wait_ge(pj_ev, g)
            pe.wait_ge(ab_v, 4)
            gs = ps[4][:, 0:NT * U8].rearrange("p (t u) -> p t u", u=U8)
            for d in range(2):
                pe.matmul(gs[:, :, d * DH:(d + 1) * DH], tri[:, d, :], la[:, :, d * DH:(d + 1) * DH], start=True, stop=True)
            pe.matmul(ps[5][:, 0:NT * U8], same, la.rearrange("p t u -> p (t u)"), start=True, stop=True)
            pe.matmul(ps[6][:, 0:2 * NT * U8], ones, la_half.rearrange("p t c -> p (t c)"), start=True, stop=True)\
                .then_inc(ab_mm, 1)

            for i in range(4):
                pe.wait_ge(pl_ok, POOL_STEPS[i])
                if i == 0:
                    pe.wait_ge(ab_a, 7)
                pe.matmul(ps[4 + i][:, :], pool_w[:, i, :], u[:, i, :], start=True, stop=True).then_inc(pl_mm, 1)
            pe.wait_ge(pl_ev, 4)
            pe.wait_ge(l2_std, 2 * DH)

            for step in range(NT):
                x = step >= CTX // P

                def needs(e, name, at_step=step):
                    delta.wait(pe, e, at_step, name)

                def says(name, mm):
                    delta.says("pe", step, name, mm)

                def cols(un):
                    t = tile_of(step, un // DH)
                    return slice(t * P, (t + 1) * P)

                def xcols(un):
                    t = tile_of(step, un // DH) - CTX // P
                    return slice(t * P, (t + 1) * P)

                def each(i, lhsT, rhs, turn=False):
                    for un in range(U8):
                        o = pair(i)[:, un, :]
                        mm = pe.transpose(o, lhsT(un), ident) if turn else \
                            pe.matmul(o, lhsT(un), rhs(un), start=True, stop=True)
                    return mm

                needs("dve", "TRILA")
                if step == 0:
                    pe.wait_ge(l2_ok, 2 * DH)
                for d in range(2):
                    mm = pe.matmul(ps[d][:, :], ones, E[:, d * DH:(d + 1) * DH, :].rearrange("p u n -> p (u n)"),
                                   start=True, stop=True)
                says("G", mm)
                key = lambda un: kT[:, un % DH, cols(un)]
                says("KK", each(1, key, key))
                if x:
                    says("QK", each(2, key, lambda un: qT[:, un % DH, xcols(un)]))
                says("KTOK", each(3, key, None, True))
                needs("dve", "SUB")
                if x:
                    needs("act", "EG")
                says("VTOK", each(0, lambda un: vT[:, un % DH, cols(un)], None, True))
                needs("dve", "LT")
                says("L", each(1, lambda un: ETS[:, un, :], None, True))
                needs("dve", "PM")
                says("PT", each(2, lambda un: PA[:, un, :], None, True))
                needs("act", "PT")
                Ps, PTs = (PA, PB), (PTA, PTB)
                for r in range(1, 6):
                    p0, pt0, p1 = Ps[(r - 1) % 2], PTs[(r - 1) % 2], Ps[r % 2]
                    if r == 1:
                        needs("act", "VTOK")
                    else:
                        needs("dve", f"SQT{r - 1}")
                    says(f"SQ{r}", each(3, lambda un: pt0[:, un, :], lambda un: p0[:, un, :]))
                    if r < 5:
                        says(f"SQT{r}", each(0, lambda un: p0[:, un, :], lambda un: pt0[:, un, :]))
                    needs("act", f"SQ{r}")
                    needs("dve", f"TT{r - 1}")
                    says(f"TT{r}", each(1 if r % 2 else 2, lambda un: p1[:, un, :], lambda un: TT[:, un, :]))
                needs("dve", "TT5")
                needs("pool", "VB")
                says("WT", each(3, lambda un: KBG[:, un, :], lambda un: TT[:, un, :]))
                says("U", each(0, lambda un: TT[:, un, :], lambda un: VB[:, un, :]))
                needs("act", "WT")
                for c in range(2):
                    if c == 0:
                        if step == 0:
                            pe.wait_ge(pl_ok, POOL_STEPS[-1])
                        else:
                            needs("dve", "S1", step - 1)
                    else:
                        needs("dve", "S0")
                    says(f"WS{c}", each(1, lambda un: PTB[:, un, :], lambda un: ST8[:, un, :]))
                    if x:
                        for un in range(U8):
                            h = c if un < DH else 1 - c
                            part = slice(h * CHUNK, (h + 1) * CHUNK)
                            mm = pe.matmul(pair(3)[:, un, part], ST8[:, un, :], EG[:, un, part], start=True, stop=True)
                        says(f"Y{c}", mm)
                    needs("dve", f"UB{c}")
                    says(f"SU{c}", each(2, lambda un: (KT0 if c == 0 else KT1)[:, un, :], lambda un: PTA[:, un, :]))
                if x:
                    says("X", each(0, lambda un: PTA[:, un, :], lambda un: ETI[:, un, :]))

            for h in range(DH):
                pe.wait_ge(l2_sq, 2 * DH + h + 1)
                if h == 0:
                    pe.wait_ge(delta.sem["dve"], delta.last("dve"))
                if h >= 2:
                    pe.wait_ge(l2_std, 2 * DH + h - 1)
                pe.matmul(ps[h % 2][:, :], ones, squares[:, h % 2, :], start=True, stop=True).then_inc(l2_mm, 1)
            pe.wait_ge(l2_ok, 2 * DH + DH)
            for t in range(KT):
                c = C_OUT2 + t // 4
                if t % 4 == 0:
                    arrived2(c)
                if t >= 4:
                    pe.wait_ge(wo_ok, t - 3)
                wo = w(c, 0, KT, 512)
                mm = product(ps[4 + t % 4], lambda k: wo[:, k, (t % 4) * P:(t % 4 + 1) * P], lambda k: mix2[:, k, :])
                mm.then_inc(wo_mm, 1)
                if t % 4 == 3:
                    give_back(1)

            pe.wait_ge(wo_ok, KT)
            pe.sem_inc(e_used.sem, E_SPLIT)
            rms_sums(2)
            pe.wait_ge(n_out, 3 * KT)
            for t in range(ST):
                mm = product(ps[0][:, t * NE:(t + 1) * NE], lambda k: zT[:, k, t * P:(t + 1) * P], lambda k: w_rt[:, k, :])
            mm.then_inc(rt_mm, 1)
            for t in range(ST):
                for hf in range(2):
                    n = 2 * t + hf
                    if n >= 4:
                        pe.wait_ge(ht_ev, n - 3)
                    for f in range(4):
                        mm = pe.transpose(ps[4 + n % 4][:, f * P:(f + 1) * P],
                                          zT[:, 4 * hf + f, t * P:(t + 1) * P], ident)
                    mm.then_inc(ht_mm, 1)
            pe.wait_ge(rt_v, 5)
            for t in range(ST):
                mm = pe.transpose(ps[1][0:NE, t * P:(t + 1) * P], aff[:, t, :], ident)
            mm.then_inc(rt_mm, 1)
            pe.wait_ge(rt_v, POS_KNOWN)
            slot_rows = std[0:NE, :]
            for t in range(ST):
                mm = pe.transpose(ps[2][:, t * NE:(t + 1) * NE], slot_rows[:, t * P:(t + 1) * P], ident[0:NE, 0:NE])
            mm.then_inc(rt_mm, 1)
            pe.wait_ge(se_ok, ST)
            pe.wait_ge(ht_ev, 2 * ST)
            for f in range(KT):
                for hf in range(2):
                    n = 2 * f + hf
                    if n >= 4:
                        pe.wait_ge(xe_ev, n - 3)
                    mm = product(ps[4 + n % 4], lambda t: h_tok[:, t, f * P:(f + 1) * P],
                                 lambda t: sel[:, t, hf * 512:(hf + 1) * 512], ST)
                    mm.then_inc(xe_mm, 1)
            pe.wait_ge(sw_ok, ST)
            for q in range(NE // 2):
                if q >= 4:
                    pe.wait_ge(sw_ev, q - 3)
                for t in range(ST):
                    mm = pe.transpose(ps[q % 4][:, t * P:(t + 1) * P], sel_w[:, t, q * P:(q + 1) * P], ident)
                mm.then_inc(sw_mm, 1)
            pe.wait_ge(sw_ev, NE // 2)
            pe.wait_ge(xe_ev, 2 * KT)

            with pe.Fori(0, NE // 2) as q:
                for j in range(2):
                    def turn(hf):
                        pe.wait_ge(ex_hid.sem, ex_hid.at(q, 2 * j + hf + 1))
                        for f in range(4):
                            mm = pe.transpose(ps[4 + 3 * hf][:, f * P:(f + 1) * P], hid[:, f * P:(f + 1) * P], ident)
                        mm.then_inc(ex_tm.sem, 1)

                    pe.wait_ge(ex_x.sem, ex_x.at(q, 2 * j + 2))
                    for c in range(EXP_CHUNKS):
                        if c == 7:
                            turn(0)
                        if c == 10:
                            turn(1)
                        if c == 8 and j == 1:
                            pe.wait_ge(ex_ye.sem, ex_ye.at(q, 2))
                        if c in (8, 10):
                            pe.wait_ge(ex_hl.sem, ex_hl.at(q, 2 * j + (c - 8) // 2 + 1))
                        pe.wait_ge(e_lo.sem, e_lo.at(q, E_RAW + EXP_CHUNKS * j + c + 1))
                        if c < 8:
                            wg = tiles(e_split[c % E_SPLIT], 512)
                            for i in range(4):
                                k = 4 * (c % 2) + i
                                for wp, part in ((0, HI), (1, HI), (0, LO)):
                                    mm = pe.matmul(ps[c // 2][0:CAP, :], xs[:, k, part], wg[wp][:, i, :],
                                                   start=(k == 0 and wp == 0 and part is HI),
                                                   stop=(k == KT - 1 and part is LO))
                        else:
                            wd = tiles(e_split[c % E_SPLIT], D)
                            for i in range(2):
                                f = 2 * (c - 8) + i
                                for n in range(2):
                                    for wp in range(2):
                                        mm = pe.matmul(ps[5 + n][:, :], hidT[:, f, :], wd[wp][:, i, n * 512:(n + 1) * 512],
                                                       start=(f == 0 and wp == 0), stop=(f == KT - 1 and wp == 1))
                        mm.then_inc(e_used.sem, 1)

            pe.wait_ge(ex_ye.sem, ex_ye.per * NE // 2)
            for f in range(KT):
                mm = product(ps[f], lambda q: ye[:, q, f * P:(f + 1) * P], lambda q: sel_wT[:, q, :], NE // 2)
                mm.then_inc(cb_mm, 1)
            pe.wait_ge(cb_ok, KT)
            rms_sums(3)
            for t in range(ST):
                for hf in range(2):
                    n = 2 * t + hf
                    if n == 0:
                        pe.wait_ge(n_out, 4 * KT)
                    if n >= 4:
                        pe.wait_ge(fin_ev, n - 3)
                    for f in range(4):
                        mm = pe.transpose(ps[4 + n % 4][:, f * P:(f + 1) * P], zT[:, 4 * hf + f, t * P:(t + 1) * P], ident)
                    mm.then_inc(fin_mm, 1)

        @block.scalar
        def _(act):
            act.wait_ge(const_in, 32)
            act.wait_ge(ready, 1)
            act.wait_ge(rope_v, 8)
            nc.scalar.activation(sinT[:, :], rope_b, ACT.Sin).then_inc(rope_s, 1)
            act.wait_ge(rope_v, 10)
            nc.scalar.activation(cosT[:, :], kr_raw, ACT.Sin).then_inc(rope_s, 1)
            for f in range(2 * KT):
                act.wait_ge(turned, f + 1)
                dst = xT[:, f, :] if f < KT else memT[:, f - KT, :]
                nc.scalar.activation(dst, ps[f % 4][:, 0:S if f < KT else MEM], ACT.Copy).then_inc(turned_out, 1)

            with act.Fori(0, DEPTH) as l:
                def col(j, m=P):
                    return par[0:m, j:j + 1]

                def norm(i, bank=1):
                    for t in range(KT):
                        act.wait_ge(cen.sem, cen.at(l, i * KT + t + 1))
                        if t >= 2:
                            act.wait_ge(var_mm.sem, var_mm.at(l, i * KT + t - 1))
                        nc.scalar.activation(squares[:, t % 2, :], zT[:, t, :], ACT.Square).then_inc(sq_ok.sem, 1)
                    act.wait_ge(var_mm.sem, var_mm.at(l, (i + 1) * KT))
                    nc.scalar.activation(std[:, :], ps[bank][:, :], ACT.Sqrt, bias=eps[:, 0:1], scale=1.0 / D)\
                        .then_inc(std_ok.sem, 1)
                    for t in range(KT):
                        act.wait_ge(scaled.sem, scaled.at(l, i * KT + t + 1))
                        g = P_LN + 2 * i * KT + t
                        nc.scalar.activation(xT[:, t, :], zT[:, t, :], ACT.Identity, bias=col(g + KT), scale=col(g))\
                            .then_inc(x_ok.sem, 1)

                act.wait_ge(par_mm.sem, par_mm.at(l, 1))
                nc.scalar.activation(par[:, :], ps[6][:, 0:NPAR], ACT.Copy).then_inc(par_ev.sem, 1)
                act.wait_ge(par_mm.sem, par_mm.at(l, 2))
                nc.scalar.activation(taps[:, :], ps[7][:, 0:TAPS * CT], ACT.Copy).then_inc(par_ev.sem, 1)
                act.wait_ge(par_ev.sem, par_ev.at(l, 2))

                for n in range(5):
                    act.wait_ge(proj_mm.sem, proj_mm.at(l, n + 1))
                    m = P if n < 4 else QK
                    dst = cqkv[:, n, :] if n < 4 else kr_raw[0:QK, :]
                    nc.scalar.activation(dst, ps[n][0:m, :], ACT.Identity, bias=col(PB_CQ + n, m)).then_inc(proj_ev.sem, 1)
                for n in range(4):
                    act.wait_ge(proj_ev.sem, proj_ev.at(l, n + 1))
                    nc.scalar.activation(mixT[:, n, :], cqkv[:, n, :], ACT.Square).then_inc(lsq.sem, 1)
                for t in range(CT):
                    act.wait_ge(proj_mm.sem, proj_mm.at(l, 7 + 2 * t))
                    if t >= 2:
                        act.wait_ge(glu.sem, glu.at(l, t - 1))
                    nc.scalar.activation(gates[:, t % 2, :], ps[(6 + 2 * t) % 8][:, :], ACT.Sigmoid, bias=col(PB_G + t))\
                        .then_inc(sig_ev.sem, 1)
                for n in range(2):
                    act.wait_ge(lsum.sem, lsum.at(l, n + 1))
                    act.wait_ge(glu.sem, glu.at(l, CT))
                    nc.scalar.activation(gates[:, n, :], ps[5 + n][:, :], ACT.Sqrt, bias=eps[:, 1:2], scale=1.0 / LORA)\
                        .then_inc(lstd.sem, 1)
                for h in range(HEADS):
                    act.wait_ge(up_mm.sem, up_mm.at(l, h + 1))
                    nc.scalar.activation(qh[0:QK, h, :], ps[h][0:QK, :], ACT.Copy).then_inc(q_ev.sem, 1)
                for h in range(HEADS):
                    act.wait_ge(up_mm.sem, up_mm.at(l, HEADS + h + 1))
                    nc.scalar.activation(kh[0:NOPE, h, :], ps[h][0:NOPE, :], ACT.Copy).then_inc(kv_ev.sem, 1)
                for t in range(ST):
                    act.wait_ge(up_mm.sem, up_mm.at(l, 2 * HEADS + t + 1))
                    nc.scalar.activation(vt[:, t, :], ps[t][:, :], ACT.Copy).then_inc(kv_ev.sem, 1)

                sc_bank = (0, 1, 6, 7)

                def exps(h):
                    for t in range(ST):
                        n = h * ST + t
                        act.wait_ge(sc_max.sem, sc_max.at(l, n + 1))
                        if h >= 2:
                            act.wait_ge(pt_mm.sem, pt_mm.at(l, (h - 1) * ST))
                        j = n % 8
                        nc.scalar.activation(probs[:, h % 2, t, 0:(t + 1) * P], ps[sc_bank[t]][:, 0:(t + 1) * P],
                                             ACT.Exp, bias=stat[:, 1, j:j + 1], scale=QK ** -0.5,
                                             accum_out=stat[:, 2, j:j + 1]).then_inc(sc_exp.sem, 1)

                def turned_probs(h):
                    for kt in range(ST):
                        n = h * ST + kt
                        act.wait_ge(pt_mm.sem, pt_mm.at(l, n + 1))
                        if h >= 1 and kt == 0:
                            act.wait_ge(pv_mm.sem, pv_mm.at(l, h))
                        nc.scalar.activation(probsT[:, kt, kt * P:S], ps[2 + n % 2][:, kt * P:S], ACT.Copy)\
                            .then_inc(pt_ev.sem, 1)

                act.wait_ge(kcopy.sem, kcopy.at(l, 1))
                act.wait_ge(qrot.sem, qrot.at(l, HEADS))
                for h in range(HEADS + 1):
                    if h < HEADS:
                        exps(h)
                    if h >= 1:
                        turned_probs(h - 1)

                for n in range(12):
                    act.wait_ge(xkv_mm.sem, xkv_mm.at(l, n + 1))
                    b = ps[sc_bank[n % 4]]
                    if n < 8:
                        nc.scalar.activation(xk[:, n, :], b[:, 0:MEM], ACT.Copy).then_inc(xkv_ev.sem, 1)
                    else:
                        t, j = (n - 8) // 2, n % 2
                        nc.scalar.activation(xv[:, t, j * 512:(j + 1) * 512], b[:, :], ACT.Copy).then_inc(xkv_ev.sem, 1)

                for t in range(CT):
                    act.wait_ge(ccen.sem, ccen.at(l, t + 1))
                    if t >= 2:
                        act.wait_ge(cvar.sem, cvar.at(l, t - 1))
                    nc.scalar.activation(squares[:, t % 2, :], mixT[:, CT + t, :], ACT.Square).then_inc(csq.sem, 1)
                act.wait_ge(cvar.sem, cvar.at(l, CT))
                nc.scalar.activation(std[:, :], ps[3][:, :], ACT.Sqrt, bias=eps[:, 0:1], scale=1.0 / CW)\
                    .then_inc(cstd.sem, 1)
                for t in range(CT):
                    act.wait_ge(cmul.sem, cmul.at(l, t + 1))
                    nc.scalar.activation(mixT[:, CT + t, :], mixT[:, CT + t, :], ACT.Silu, bias=col(P_CNB + t),
                                         scale=col(P_CNG + t)).then_inc(cout.sem, 1)
                norm(0)

                for t in range(KT):
                    act.wait_ge(xq_mm.sem, xq_mm.at(l, t + 1))
                    nc.scalar.activation(qx[:, t, :], ps[2 + t % 4][:, :], ACT.Copy).then_inc(xq_ev.sem, 1)

                def xexps(h):
                    for t in range(ST):
                        n = 2 * h + t // 2
                        act.wait_ge(xs_max.sem, xs_max.at(l, n + 1))
                        if h >= 2:
                            act.wait_ge(xt_mm.sem, xt_mm.at(l, (h - 1) * MT))
                        j = (h * ST + t) % 8
                        nc.scalar.activation(probs[:, h % 2, t, 0:MEM],
                                             ps[sc_bank[n % 4]][:, (t % 2) * MEM:(t % 2 + 1) * MEM], ACT.Exp,
                                             bias=stat[:, 1, j:j + 1], scale=XD ** -0.5,
                                             accum_out=stat[:, 2, j:j + 1]).then_inc(xs_exp.sem, 1)

                def xturned(h):
                    for kt in range(MT):
                        act.wait_ge(xt_mm.sem, xt_mm.at(l, MT * h + kt + 1))
                        if h >= 1 and kt == 0:
                            act.wait_ge(xo_mm.sem, xo_mm.at(l, 2 * h))
                        nc.scalar.activation(probsT[:, kt, :], ps[2 + kt][:, :], ACT.Copy).then_inc(xt_ev.sem, 1)

                for h in range(XH + 1):
                    if h < XH:
                        xexps(h)
                    if h >= 1:
                        xturned(h - 1)

                def high(n):
                    if n < 2:
                        act.wait_ge(res_mm.sem, res_mm.at(l, KT + 4 * (n + 1)))
                    else:
                        ffn_used(act, l, n - 2)
                    act.wait_ge(raw_in[n % 2], l * (16 * FFN_CHUNKS) + 32 * (n // 2 + 1))
                    m = ffn_floats(n)
                    nc.scalar.activation(w_split[n % 2][0][:, 0:m], raw[n % 2][:, 0:m], ACT.Copy).then_inc(f_hi.sem, 1)

                high(0)
                high(1)
                norm(1)
                for n in range(FFN_CHUNKS):
                    half_no, t, hidden_tile = ffn_chunk(n)
                    if hidden_tile:
                        act.wait_ge(ffn_mm.sem, ffn_mm.at(l, 2 * t + 1))
                        if t >= 2:
                            act.wait_ge(ffn_ok.sem, ffn_ok.at(l, t - 1))
                        nc.scalar.activation(gates[:, t % 2, :], ps[2 * (t % 4)][:, :], ACT.Silu).then_inc(ffn_act.sem, 1)
                    if n + 2 < FFN_CHUNKS:
                        high(n + 2)
                norm(2, 3)

            A1 = nc.scalar.activation
            act.wait_ge(p2_mm, 1)
            A1(par2, ps[6][:, 0:NPAR2], ACT.Copy).then_inc(p2_ev, 1)
            act.wait_ge(p2_mm, 2)
            A1(taps2, ps[7][:, 0:CONV_K * 3 * DH], ACT.Copy).then_inc(p2_ev, 1)
            act.wait_ge(p2_ev, 1)
            for j, lo in enumerate((Q_C, Q_CC)):
                A1(cond[:, :, j], par2[:, lo:lo + KT], ACT.Silu).then_inc(cond_ok, 1)
            for f in range(KT):
                act.wait_ge(ctx_mm, f + 1)
                A1(ctxT[:, f, :], ps[2 + f % 4][:, 0:CTX], ACT.Copy).then_inc(ctx_ev, 1)

            def rms(m, src, dst, scale, bias, n=S, changed=None):
                for t in range(KT):
                    if changed is not None:
                        act.wait_ge(changed, t + 1)
                    if t >= 2:
                        act.wait_ge(n_mm, m * KT + t - 1)
                    A1(squares[:, t % 2, 0:n], src[:, t, :], ACT.Square).then_inc(n_sq, 1)
                act.wait_ge(n_mm, (m + 1) * KT)
                if m == 1:
                    act.wait_ge(n_mul, KT)
                A1(std[:, 0:n], ps[1 + m % 2][:, 0:n], ACT.Sqrt, bias=eps[:, 1:2], scale=1.0 / D).then_inc(n_std, 1)
                for t in range(KT):
                    act.wait_ge(n_mul, m * KT + t + 1)
                    A1(dst[:, t, :], dst[:, t, :], ACT.Identity, scale=scale(t), bias=bias(t) if bias else 0.0)\
                        .then_inc(n_out, 1)

            act.wait_ge(ctx_ev, KT)
            act.wait_ge(mod_ok, 4)
            rms(0, xT, zT, lambda t: gain[:, 0, t:t + 1], lambda t: mod[:, t, 0:1])
            rms(1, ctxT, hz, lambda t: gain[:, 1, t:t + 1], lambda t: mod[:, t, 1:2], CTX)

            def swish(c):
                act.wait_ge(cv_ok, CONV_K * (c + 1))
                t = c % DH
                if c < 2 * DH:
                    dst = (kT, vT)[c // DH]
                    A1(dst[:, t, CTX:], acc[:, c % 2, 0:S], ACT.Silu).then_inc(cv_out, 1)
                    A1(dst[:, t, 0:CTX], acc[:, c % 2, S + 3:S + 3 + CTX], ACT.Silu).then_inc(cv_out, 1)
                else:
                    A1(qT[:, t, :], acc[:, c % 2, 0:S], ACT.Silu).then_inc(cv_out, 1)

            act.wait_ge(padded, 1)
            g = 0
            for j in range(5):
                for t in range(4):
                    act.wait_ge(pj_mm, g + 1)
                    b = ps[2 * (g % 4)]
                    if j == 0:
                        A1(u[:, t, :], b, ACT.Copy).then_inc(pj_ev, 1)
                    elif j < 4:
                        c = 4 * (j - 1) + t
                        if c >= 2:
                            act.wait_ge(cv_ok, CONV_K * (c - 1))
                        if j < 3:
                            A1(pre[:, c % 2, S + 5:S + 5 + CTX], ps[2 * (g % 4) + 1][:, 0:CTX], ACT.Copy)
                        A1(pre[:, c % 2, 2:2 + S], b, ACT.Copy).then_inc(pj_ev, 1)
                        if c >= 1:
                            swish(c - 1)
                    else:
                        A1(gateT[:, t, :], b, ACT.Silu).then_inc(pj_ev, 1)
                    g += 1
                if j == 2:
                    act.wait_ge(pj_mm, g + 1)
                    src = ps[2 * (g % 4)][:, 0:16 * NT].rearrange("p (t a u) -> p t a u", a=2, u=U8)
                    A1(ab[:, :, :, 0:DH], src[:, :, :, 0:DH], ACT.Copy)
                    for step in range(NT):
                        ins = A1(ab[:, step, :, DH:], src[:, tile_of(step, 1), :, DH:], ACT.Copy)
                    ins.then_inc(pj_ev, 1)
                    g += 1
                if j == 3:
                    swish(11)

            for i in range(2 * DH + 2):
                if i < 2 * DH:
                    if i == 0:
                        act.wait_ge(cv_out, 4 * DH + DH)
                    if i >= 2:
                        act.wait_ge(l2_mm, i - 1)
                    src = kT[:, i, :] if i < DH else qT[:, i - DH, :]
                    if i < DH:
                        A1(pre[:, i % 2, 0:S], src[:, CTX:], ACT.Square)
                        A1(pre[:, i % 2, S:S + CTX], src[:, 0:CTX], ACT.Square).then_inc(l2_sq, 1)
                    else:
                        A1(pre[:, i % 2, 0:S], src, ACT.Square)
                        A1(pre[:, i % 2, S:S + CTX], src[:, 0:CTX], ACT.Square).then_inc(l2_sq, 1)
                if i >= 2:
                    m = i - 2
                    act.wait_ge(l2_mm, m + 1)
                    if m >= 2:
                        act.wait_ge(l2_ok, m - 1)
                    A1(acc[:, m % 2, 0:S], ps[2 * (m % 2)][:, :], ACT.Sqrt, bias=eps[:, 1:2])
                    A1(acc[:, m % 2, S:S + CTX], ps[2 * (m % 2) + 1][:, 0:CTX], ACT.Sqrt, bias=eps[:, 1:2]).then_inc(l2_std, 1)

            act.wait_ge(ab_v, 1)
            A1(sp_e, sp_e, ACT.Exp, scale=-1.0).then_inc(ab_a, 1)
            A1(a_log, a_log, ACT.Exp).then_inc(ab_a, 1)
            act.wait_ge(ab_a, 2)
            A1(sp_e, sp_e, ACT.Ln, bias=1.0).then_inc(ab_a, 1)
            A1(beta, ab[:, :, 1, :], ACT.Sigmoid).then_inc(ab_a, 1)
            act.wait_ge(ab_mm, 1)
            A1(gsum.rearrange("p t u -> p (t u)"), ps[4][:, 0:NT * U8], ACT.Copy).then_inc(ab_a, 1)
            A1(eg.rearrange("p t u -> p (t u)"), ps[4][:, 0:NT * U8], ACT.Exp).then_inc(ab_a, 1)
            act.wait_ge(ab_v, 5)
            A1(sdec.rearrange("p t c -> p (t c)"), ps[6][:, 0:2 * NT * U8], ACT.Exp).then_inc(ab_a, 1)
            A1(tail, tail, ACT.Exp).then_inc(ab_a, 1)

            for i in range(4):
                act.wait_ge(pl_mm, i + 1)
                A1(mix2[:, DH + i, :], ps[4 + i][:, :], ACT.Copy, scale=par2[:, Q_PS + i:Q_PS + i + 1]).then_inc(pl_ev, 1)

            for step in range(NT):
                x = step >= CTX // P

                def needs(e, name):
                    delta.wait(act, e, step, name)

                def says(name, ins):
                    delta.says("act", step, name, ins)

                needs("dve", "MIN")
                says("E", A1(E, E, ACT.Exp))
                if x:
                    says("EG", A1(EG, pair(0), ACT.Exp))
                needs("pe", "KTOK")
                says("KTOK", A1(KT1, pair(3), ACT.Copy))
                needs("pe", "VTOK")
                says("VTOK", A1(VB, pair(0), ACT.Copy))
                needs("pe", "PT")
                says("PT", A1(PTA, pair(2), ACT.Copy))
                for r in range(1, 6):
                    needs("pe", f"SQ{r}")
                    if r >= 2:
                        needs("pe", f"TT{r - 1}")
                    says(f"SQ{r}", A1((PA, PB)[r % 2], pair(3), ACT.Copy))
                needs("pe", "WT")
                says("WT", A1(PTB, pair(3), ACT.Copy))

            def head_std(h):
                act.wait_ge(l2_mm, 2 * DH + h + 1)
                A1(head_dev[:, h, :], ps[h % 2][:, :], ACT.Sqrt, bias=eps[:, 1:2], scale=1.0 / P).then_inc(l2_std, 1)

            for h in range(DH):
                if h == 0:
                    act.wait_ge(delta.sem["dve"], delta.last("dve"))
                if h >= 2:
                    act.wait_ge(l2_mm, 2 * DH + h - 1)
                A1(squares[:, h % 2, :], mix2[:, h, :], ACT.Square).then_inc(l2_sq, 1)
                if h >= 1:
                    head_std(h - 1)
            head_std(DH - 1)

            rms(2, xT, zT, lambda t: gain[:, 2, t:t + 1], lambda t: mod[:, 3 * KT + t, 0:1], changed=wo_ok)
            act.wait_ge(rt_v, 2)
            A1(aff, aff, ACT.Exp).then_inc(rt_a, 1)
            for n in range(2 * ST):
                act.wait_ge(ht_mm, n + 1)
                A1(h_tok[:, n // 2, (n % 2) * 512:(n % 2 + 1) * 512], ps[4 + n % 4][:, :], ACT.Copy).then_inc(ht_ev, 1)
            for n in range(2 * KT):
                act.wait_ge(xe_mm, n + 1)
                A1(xeT[:, n // 2, (n % 2) * 512:(n % 2 + 1) * 512], ps[4 + n % 4][:, :], ACT.Copy).then_inc(xe_ev, 1)
            for q in range(NE // 2):
                act.wait_ge(sw_mm, q + 1)
                A1(sel_wT[:, q, :], ps[q % 4][:, :], ACT.Copy).then_inc(sw_ev, 1)

            with act.Fori(0, NE // 2) as q:
                def used_up(j, c):
                    act.wait_ge(e_used.sem, e_used.at(q, E_SPLIT + EXP_CHUNKS * j + c + 1))

                def high(j, lo, hi):
                    for c in range(lo, hi):
                        act.wait_ge(e_in[c % E_RAW], q * (32 * EXP_CHUNKS // E_RAW)
                                    + 16 * (EXP_CHUNKS // E_RAW * j + c // E_RAW + 1))
                        act.wait_ge(e_used.sem, e_used.at(q, EXP_CHUNKS * j + c + 1))
                        A1(e_split[c % E_SPLIT][0], e_raw[c % E_RAW], ACT.Copy).then_inc(e_hi.sem, 1)

                def silu(j, hf):
                    used_up(j, 4 * hf + 1)
                    if 2 * j + hf:
                        act.wait_ge(ex_hid.sem, ex_hid.at(q, 2 * j + hf))
                    A1(gates[0:CAP, 0, :], ps[2 * hf][0:CAP, :], ACT.Silu).then_inc(ex_silu.sem, 1)

                def hidden_high(j, hf):
                    act.wait_ge(ex_tm.sem, ex_tm.at(q, 2 * j + hf + 1))
                    A1(hidT[:, 4 * hf:4 * hf + 4, HI], ps[4 + 3 * hf].rearrange("p (f c) -> p f c", c=P)[:, :, 0:CAP],
                       ACT.Copy).then_inc(ex_ht.sem, 1)

                def out_low(j):
                    used_up(j, EXP_CHUNKS - 1)
                    for n in range(2):
                        A1(std[0:CAP, :] if n else gates[0:CAP, 1, :], ps[5 + n][LO, :], ACT.Copy).then_inc(ex_yb.sem, 1)

                for j in range(2):
                    high(j, 0, 2)
                    if j == 1:
                        out_low(0)
                    high(j, 2, 5)
                    silu(j, 0)
                    high(j, 5, 9)
                    silu(j, 1)
                    high(j, 9, 10)
                    hidden_high(j, 0)
                    high(j, 10, 12)
                    hidden_high(j, 1)
                out_low(1)
            rms(3, xT, zT, lambda t: par2[:, Q_NF + t:Q_NF + t + 1], None, changed=cb_ok)
            for n in range(2 * ST):
                t, hf = n // 2, n % 2
                act.wait_ge(fin_mm, n + 1)
                if t >= 2 and hf == 0:
                    act.wait_ge(stored[t % 2], 16 * (t // 2))
                A1(out_tok[:, t % 2, hf * 512:(hf + 1) * 512], ps[4 + n % 4][:, :], ACT.Copy).then_inc(fin_ev, 1)

        @block.gpsimd
        def _(pool):
            with pool.Fori(0, DEPTH) as l:
                pool.wait_ge(krot.sem, krot.at(l, 2))
                def every(x):
                    return x[NOPE:QK, :].rearrange("p (a n) -> p a n", a=1).broadcast_to([ROPE, HEADS, S])

                nc.gpsimd.tensor_tensor(kh[NOPE:QK, :, :], every(rope_a), every(rope_b), ALU.add).then_inc(kcopy.sem, 1)
                for h in range(HEADS):
                    q = qh[NOPE:QK, h, :]
                    pool.wait_ge(qrot_mm.sem, qrot_mm.at(l, h + 1))
                    nc.gpsimd.tensor_tensor(q, q, cosT[NOPE:QK, :], ALU.mult).then_inc(qrot_cos.sem, 1)
                    pool.wait_ge(qrot_cos.sem, qrot_cos.at(l, h + 1))
                    pool.wait_ge(qrot_sin.sem, qrot_sin.at(l, h + 1))
                    nc.gpsimd.tensor_tensor(q, q, (rope_a if h % 2 else rope_b)[NOPE:QK, :], ALU.add)\
                        .then_inc(qrot.sem, 1)

            G = nc.gpsimd
            count = [0]

            def behind(ins):
                ins.then_inc(pl_ok, 1)
                count[0] += 1
                pool.wait_ge(pl_ok, count[0])

            pool.wait_ge(small_in, 16 * 16)
            for i, win in enumerate(WINDOWS):
                buf = [pool_a, pool_b]
                W = GRID_W + win
                if i == 0:
                    pool.wait_ge(ctx_ev, KT)
                b0 = buf[0][:, 0:ROWS * W].rearrange("p (r c) -> p r c", c=W)
                behind(G.memset(b0, 0.0))
                pool.wait_ge(pj_ev, i + 1)
                ug = u[:, i, :].rearrange("p (r c) -> p r c", c=GRID_W)
                behind(G.tensor_copy(b0[:, :, win // 2:win // 2 + GRID_W], ug))
                cur, s, width = 0, 1, W
                while s < win:
                    src = buf[cur][:, 0:ROWS * W].rearrange("p (r c) -> p r c", c=W)
                    dst = buf[1 - cur][:, 0:ROWS * W].rearrange("p (r c) -> p r c", c=W)
                    width -= s
                    behind(G.tensor_tensor(dst[:, :, 0:width], src[:, :, 0:width], src[:, :, s:s + width], ALU.add))
                    cur, s = 1 - cur, 2 * s
                src = buf[cur][:, 0:ROWS * W].rearrange("p (r c) -> p r c", c=W)
                R = ROWS + win
                dst = buf[1 - cur][:, 0:R * GRID_W].rearrange("p (r c) -> p r c", c=GRID_W)
                behind(G.memset(dst, 0.0))
                behind(G.tensor_copy(dst[:, win // 2:win // 2 + ROWS, :], src[:, :, 0:GRID_W]))
                cur, s, height = 1 - cur, 1, R
                while s < win:
                    height -= s
                    src, dst = buf[cur], buf[1 - cur]
                    behind(G.tensor_tensor(dst[:, 0:height * GRID_W], src[:, 0:height * GRID_W],
                                           src[:, s * GRID_W:(s + height) * GRID_W], ALU.add))
                    cur, s = 1 - cur, 2 * s
                m = buf[cur][:, 0:S]
                behind(G.tensor_tensor(m, m, inv_cnt[:, i, :], ALU.mult))
                behind(G.tensor_tensor(u[:, i, :], m, u[:, i, :], ALU.subtract))
                assert count[0] == POOL_STEPS[i], (i, count)
            G.memset(mix2[:, 0:DH, :], 0.0)
            pool.wait_ge(pj_mm, 21)
            behind(G.memset(ST8, 0.0))
            assert count[0] == POOL_STEPS[-1], count

            for step in range(NT):
                x = step >= CTX // P

                def needs(e, name, at_step=step):
                    delta.wait(pool, e, at_step, name)

                def says(name, ins):
                    delta.says("pool", step, name, ins)

                def masked(m):
                    return [m[:, d:d + 1, :].broadcast_to([P, DH, P]) for d in range(2)]

                needs("act", "E")
                for name, dst, m in (("ETS", ETS, strict), ("ETI", ETI, tri)):
                    if step and name == "ETI":
                        needs("pe", "X" if step - 1 >= CTX // P else "SU1", step - 1)
                    for d in range(2):
                        r = slice(d * DH, (d + 1) * DH)
                        ins = G.tensor_tensor(dst[:, r, :], E[:, r, :], masked(m)[d], ALU.mult)
                    says(name, ins)
                if x:
                    needs("act", "EG")
                    for d in range(2):
                        r = slice(d * DH, (d + 1) * DH)
                        t = tile_of(step, d) - CTX // P
                        ins = G.tensor_tensor(EG[:, r, :], EG[:, r, :], qT[:, :, t * P:(t + 1) * P], ALU.mult)
                    says("QD", ins)

                def scaled(dst, src, vec8):
                    return G.tensor_tensor(dst, src, vec8.unsqueeze(2).broadcast_to([P, U8, P]), ALU.mult)

                th = tail_half[:, step * U8:(step + 1) * U8, :]
                sd = sdec[:, step * U8:(step + 1) * U8, :]
                needs("act", "KTOK")
                if step == 0:
                    pool.wait_ge(ab_v, 8)
                says("KBG", scaled(KBG, KT1, beg[:, step, :]))
                says("KT0", scaled(KT0, KT1, th[:, :, 0]))
                needs("pool", "KT0")
                says("KT1", scaled(KT1, KT1, th[:, :, 1]))
                needs("act", "VTOK")
                says("VB", scaled(VB, VB, beta[:, step, :]))
                if step:
                    needs("dve", "S1", step - 1)
                says("SD0", scaled(SD, ST8, sd[:, :, 0]))
                needs("dve", "S0")
                says("SD1", scaled(SD, ST8, sd[:, :, 1]))

            for t in range(ST):
                pool.wait_ge(se_ok, t + 1)
                G.tensor_tensor(sel_w[:, t, :].rearrange("p (e c) -> p e c", c=CAP),
                                sel[:, t, :].rearrange("p (e c) -> p e c", c=CAP),
                                aff[:, t, :].unsqueeze(2).broadcast_to([P, NE, CAP]), ALU.mult).then_inc(sw_ok, 1)

        @block.vector
        def _(dve):
            V = nc.vector
            V.memset(par_rows[:, :], 0.0).then_inc(ready, 1)
            V.memset(eps[:, 0:1], LN_EPS)
            V.memset(eps[:, 1:2], RMS_EPS)
            V.memset(hpad[:, :, 0:TAPS - 1], 0.0)
            V.memset(tap_rows[:, :], 0.0).then_inc(ready, 1)

            dve.wait_ge(const_in, 32)
            V.tensor_copy(rope_b, rope_a.bitcast(I32)).then_inc(rope_v, 1)
            dve.wait_ge(rope_v, 1)
            V.tensor_scalar(rope_b, rope_b, consts[:, K_FREQ:K_FREQ + 1], None, ALU.mult).then_inc(rope_v, 1)
            dve.wait_ge(rope_v, 2)
            V.tensor_scalar(rope_a, rope_b, 1.0 / TWO_PI, ROUND, ALU.mult, ALU.add).then_inc(rope_v, 1)
            dve.wait_ge(rope_v, 3)
            V.tensor_scalar(rope_a, rope_a, -ROUND, None, ALU.add).then_inc(rope_v, 1)
            for n, c in enumerate((PI_A, PI_B, PI_C)):
                dve.wait_ge(rope_v, 4 + n)
                V.scalar_tensor_tensor(out=rope_b, in0=rope_a, scalar=-c, in1=rope_b, op0=ALU.mult, op1=ALU.add)\
                    .then_inc(rope_v, 1)
            dve.wait_ge(rope_v, 7)
            V.tensor_scalar(rope_b, rope_b, PI_MAX, -PI_MAX, ALU.min, ALU.max).then_inc(rope_v, 1)
            dve.wait_ge(rope_v, 8)
            V.scalar_tensor_tensor(out=rope_a, in0=rope_b, scalar=-1.0, in1=rope_b, op0=ALU.mult, op1=ALU.max)\
                .then_inc(rope_v, 1)
            dve.wait_ge(rope_v, 9)
            V.tensor_scalar(kr_raw, rope_a, -1.0, np.pi / 2, ALU.mult, ALU.add).then_inc(rope_v, 1)

            with dve.Fori(0, DEPTH) as l:
                behind = [0]

                def done(ins):
                    ins.then_inc(vec.sem, 1)
                    behind[0] += 1
                    return vec.at(l, behind[0])

                def low(n):
                    dve.wait_ge(f_hi.sem, f_hi.at(l, n + 1))
                    m, (hi, lo) = ffn_floats(n), w_split[n % 2]
                    V.tensor_tensor(lo[:, 0:m], raw[n % 2][:, 0:m], hi[:, 0:m].bitcast(F32), ALU.subtract).then_inc(f_lo.sem, 1)

                def add_in(i, t):
                    dve.wait_ge(res_mm.sem, res_mm.at(l, i * KT + t + 1))
                    V.scalar_tensor_tensor(out=zT[:, t, :], in0=xT[:, t, :], scalar=ALPHA,
                                           in1=ps[(6, 7, 0, 1)[t % 4] if i == 2 else 4 + t % 4][:, :],
                                           op0=ALU.mult, op1=ALU.add).then_inc(z_ok.sem, 1)

                def norm(i):
                    dve.wait_ge(mean_mm.sem, mean_mm.at(l, i + 1))
                    for t in range(KT):
                        V.scalar_tensor_tensor(out=zT[:, t, :], in0=ps[2 if i == 2 else 0][:, :], scalar=-1.0 / D,
                                               in1=zT[:, t, :], op0=ALU.mult, op1=ALU.add).then_inc(cen.sem, 1)
                    if i == 1:
                        low(1)
                    dve.wait_ge(std_ok.sem, std_ok.at(l, i + 1))
                    n = done(V.reciprocal(std[:, :], std[:, :]))
                    dve.wait_ge(vec.sem, n)
                    for t in range(KT + 3):
                        if t < KT:
                            V.tensor_tensor(zT[:, t, :], zT[:, t, :], std[:, :], ALU.mult).then_inc(scaled.sem, 1)
                        if i == 1 and t >= 2:
                            k = t - 2
                            if k < KT:
                                dve.wait_ge(x_ok.sem, x_ok.at(l, i * KT + k + 1))
                                V.tensor_copy(x_split[0][:, k, :], xT[:, k, :]).then_inc(x_part.sem, 1)
                            if k >= 1:
                                dve.wait_ge(x_part.sem, x_part.at(l, max(1, 2 * (k - 1))))
                                V.tensor_tensor(x_split[1][:, k - 1, :], xT[:, k - 1, :],
                                                x_split[0][:, k - 1, :].bitcast(F32), ALU.subtract).then_inc(x_part.sem, 1)

                dve.wait_ge(par_ev.sem, par_ev.at(l, 2))
                for t in range(CT):
                    dve.wait_ge(sig_ev.sem, sig_ev.at(l, t + 1))
                    V.scalar_tensor_tensor(out=hpad[:, t, TAPS - 1:], in0=ps[(5 + 2 * t) % 8][:, :],
                                           scalar=par[:, PB_A + t:PB_A + t + 1], in1=gates[:, t % 2, :],
                                           op0=ALU.add, op1=ALU.mult).then_inc(glu.sem, 1)
                for n in range(2):
                    dve.wait_ge(lstd.sem, lstd.at(l, n + 1))
                    v = done(V.reciprocal(gates[:, n, :], gates[:, n, :]))
                    dve.wait_ge(vec.sem, v)
                    for k in range(2):
                        j = P_QN + 2 * n + k
                        V.scalar_tensor_tensor(out=cqkv[:, 2 * n + k, :], in0=cqkv[:, 2 * n + k, :],
                                               scalar=par[:, j:j + 1], in1=gates[:, n, :],
                                               op0=ALU.mult, op1=ALU.mult).then_inc(lnorm.sem, 1)
                r = slice(NOPE, QK)
                dve.wait_ge(krot_mm.sem, krot_mm.at(l, 1))
                V.tensor_tensor(rope_a[r, :], ps[7][r, :], sinT[r, :], ALU.mult).then_inc(krot.sem, 1)
                V.tensor_tensor(rope_b[r, :], kr_raw[r, :], cosT[r, :], ALU.mult).then_inc(krot.sem, 1)
                dve.wait_ge(kcopy.sem, kcopy.at(l, 1))
                for h in range(HEADS):
                    dve.wait_ge(qrot_mm.sem, qrot_mm.at(l, h + 1))
                    if h >= 2:
                        dve.wait_ge(qrot.sem, qrot.at(l, h - 1))
                    V.tensor_tensor((rope_a if h % 2 else rope_b)[r, :], ps[4 + h % 4][r, :], sinT[r, :], ALU.mult)\
                        .then_inc(qrot_sin.sem, 1)

                sc_bank = (0, 1, 6, 7)

                def maximum(n):
                    t, j = n % ST, n % 8
                    b = ps[sc_bank[t]]
                    dve.wait_ge(sc_mm.sem, sc_mm.at(l, n + 1))
                    v = done(V.memset(b[0:CHUNK, (t + 1) * P - CHUNK:(t + 1) * P], NEG))
                    dve.wait_ge(vec.sem, v)
                    v = done(V.tensor_reduce(stat[:, 0, j:j + 1], b[:, 0:(t + 1) * P], AX, ALU.max))
                    dve.wait_ge(vec.sem, v)
                    V.tensor_scalar(stat[:, 1, j:j + 1], stat[:, 0, j:j + 1], -QK ** -0.5, None, ALU.mult)\
                        .then_inc(sc_max.sem, 1)

                def normalise(n):
                    h, t, j = n // ST, n % ST, n % 8
                    dve.wait_ge(sc_exp.sem, sc_exp.at(l, n + 1))
                    v = done(V.reciprocal(stat[:, 3, j:j + 1], stat[:, 2, j:j + 1]))
                    dve.wait_ge(vec.sem, v)
                    p = probs[:, h % 2, t, 0:(t + 1) * P]
                    V.tensor_scalar(p, p, stat[:, 3, j:j + 1], None, ALU.mult).then_inc(sc_norm.sem, 1)

                def tap(k):
                    for t in range(CT):
                        acc, x = mixT[:, CT + t, :], hpad[:, t, k:k + S]
                        c = taps[:, k * CT + t:k * CT + t + 1]
                        if k == 0:
                            V.tensor_scalar(acc, x, c, par[:, P_DWB + t:P_DWB + t + 1], ALU.mult, ALU.add)\
                                .then_inc(conv.sem, 1)
                        else:
                            dve.wait_ge(conv.sem, conv.at(l, CT * (k - 1) + t + 1))
                            V.scalar_tensor_tensor(out=acc, in0=x, scalar=c, in1=acc, op0=ALU.mult, op1=ALU.add)\
                                .then_inc(conv.sem, 1)

                def head_out(h):
                    dve.wait_ge(pv_mm.sem, pv_mm.at(l, h + 1))
                    lo = (h % 2) * VD
                    V.tensor_copy(mixT[lo:lo + VD, h // 2, :], ps[4 + h % 2][0:VD, :]).then_inc(pv_ev.sem, 1)

                LAG = 2
                for n in range(HEADS * ST + LAG):
                    if n < HEADS * ST:
                        maximum(n)
                    if n >= LAG:
                        normalise(n - LAG)
                    if n < TAPS:
                        tap(n)
                    if n >= 2 * ST and n % ST == 3:
                        head_out(n // ST - 2)
                head_out(HEADS - 2)
                head_out(HEADS - 1)

                dve.wait_ge(cstat_mm.sem, cstat_mm.at(l, 1))
                for t in range(CT):
                    V.scalar_tensor_tensor(out=mixT[:, CT + t, :], in0=ps[2][:, :], scalar=-1.0 / CW,
                                           in1=mixT[:, CT + t, :], op0=ALU.mult, op1=ALU.add).then_inc(ccen.sem, 1)
                dve.wait_ge(cstd.sem, cstd.at(l, 1))
                v = done(V.reciprocal(std[:, :], std[:, :]))
                dve.wait_ge(vec.sem, v)
                for t in range(CT):
                    V.tensor_tensor(mixT[:, CT + t, :], mixT[:, CT + t, :], std[:, :], ALU.mult).then_inc(cmul.sem, 1)
                for t in range(KT):
                    add_in(0, t)
                norm(0)

                def xmaximum(n):
                    j = (2 * n) % 8
                    dve.wait_ge(xs_mm.sem, xs_mm.at(l, n + 1))
                    v = done(V.tensor_reduce(stat[:, 0, j:j + 2],
                                             ps[sc_bank[n % 4]][:, :].rearrange("p (a m) -> p a m", a=2), AX, ALU.max))
                    dve.wait_ge(vec.sem, v)
                    V.tensor_scalar(stat[:, 1, j:j + 2], stat[:, 0, j:j + 2], -XD ** -0.5, None, ALU.mult)\
                        .then_inc(xs_max.sem, 1)

                def xnormalise(n):
                    j = (2 * n) % 8
                    dve.wait_ge(xs_exp.sem, xs_exp.at(l, 2 * n + 2))
                    v = done(V.reciprocal(stat[:, 3, j:j + 2], stat[:, 2, j:j + 2]))
                    dve.wait_ge(vec.sem, v)
                    for i in range(2):
                        p = probs[:, (n // 2) % 2, 2 * (n % 2) + i, 0:MEM]
                        V.tensor_scalar(p, p, stat[:, 3, j + i:j + i + 1], None, ALU.mult).then_inc(xs_norm.sem, 1)

                def xhead_out(h):
                    for v in range(2):
                        dve.wait_ge(xo_mm.sem, xo_mm.at(l, 2 * h + v + 1))
                        V.tensor_copy(ox[:, 2 * h + v, :], ps[4 + v][:, :]).then_inc(xo_ev.sem, 1)

                for h in range(XH + 1):
                    if h < XH:
                        for j in range(2):
                            xmaximum(2 * h + j)
                        for j in range(2):
                            xnormalise(2 * h + j)
                    if h >= 1:
                        xhead_out(h - 1)
                for t in range(KT):
                    add_in(1, t)
                    if t == KT - 3:
                        low(0)
                norm(1)
                for n in range(FFN_CHUNKS):
                    half_no, t, hidden_tile = ffn_chunk(n)
                    if hidden_tile:
                        dve.wait_ge(ffn_act.sem, ffn_act.at(l, t + 1))
                        dve.wait_ge(ffn_mm.sem, ffn_mm.at(l, 2 * t + 2))
                        whole, i = squares[:, t % 2, :], t % HALF
                        V.tensor_tensor(whole, gates[:, t % 2, :], ps[2 * (t % 4) + 1][:, :], ALU.mult)\
                            .then_inc(ffn_ok.sem, 1)
                        dve.wait_ge(ffn_ok.sem, ffn_ok.at(l, t + 1))
                        V.tensor_copy(h_split[0][:, i, :], whole).then_inc(h_part.sem, 1)
                        dve.wait_ge(h_part.sem, h_part.at(l, 2 * t + 1))
                        V.tensor_tensor(h_split[1][:, i, :], whole, h_split[0][:, i, :].bitcast(F32), ALU.subtract)\
                            .then_inc(h_part.sem, 1)
                    elif half_no == 0:
                        add_in(2, t)
                    else:
                        dve.wait_ge(res_mm.sem, res_mm.at(l, 3 * KT + t + 1))
                        V.tensor_tensor(zT[:, t, :], zT[:, t, :], ps[(6, 7, 0, 1)[t % 4]][:, :], ALU.add)\
                            .then_inc(z_ok.sem, 2 if t == KT - 1 else 1)
                    if n + 2 < FFN_CHUNKS:
                        low(n + 2)
                norm(2)
                assert behind[0] == vec.per, behind


            n2 = [0]

            def done(ins):
                ins.then_inc(vec2, 1)
                n2[0] += 1
                return n2[0]

            dve.wait_ge(p2_ev, 2)
            dve.wait_ge(mod_mm, 1)
            v = done(V.tensor_tensor(mod, ps[0][:, 0:12 * KT].rearrange("p (j w) -> p j w", w=2),
                                     par2[:, 0:6 * KT].unsqueeze(2).broadcast_to([P, 6 * KT, 2]), ALU.add))
            dve.wait_ge(vec2, v)
            for i, (which, col, norm) in enumerate(((1, 0, Q_N1), (1, 1, Q_N1), (4, 0, Q_N2))):
                V.scalar_tensor_tensor(out=gain[:, i, :], in0=mod[:, which * KT:(which + 1) * KT, col], scalar=1.0,
                                       in1=par2[:, norm:norm + KT], op0=ALU.add, op1=ALU.mult).then_inc(mod_ok, 1)
            V.tensor_copy(gain[:, 3, :], par2[:, Q_NF:Q_NF + KT]).then_inc(mod_ok, 1)

            def rms(m, src, dst, n=S):
                dve.wait_ge(n_std, m + 1)
                v = done(V.reciprocal(std[:, 0:n], std[:, 0:n]))
                dve.wait_ge(vec2, v)
                for t in range(KT):
                    V.tensor_tensor(dst[:, t, :], src[:, t, :], std[:, 0:n], ALU.mult).then_inc(n_mul, 1)

            rms(0, xT, zT)
            rms(1, ctxT, hz, CTX)
            dve.wait_ge(n_mul, 2 * KT)
            V.memset(pre[:, :, 0:2], 0.0)
            V.memset(pre[:, :, S + 2:S + 5], 0.0)
            V.memset(pre[:, :, PRE - 1:PRE], 0.0).then_inc(padded, 1)
            dve.wait_ge(n_out, 2 * KT)

            for c in range(3 * DH):
                tile = (c + DH) % (3 * DH)
                n = PRE - 3 if c < 2 * DH else S
                dve.wait_ge(pj_ev, 4 + c + 1 + (1 if c >= 2 * DH else 0))
                if c >= 2:
                    dve.wait_ge(cv_out, 2 * (c - 1) if c - 2 < 2 * DH else 4 * DH + c - 1 - 2 * DH)
                for k in range(CONV_K):
                    tap_col = taps2[:, k * 3 * DH + tile:k * 3 * DH + tile + 1]
                    x = pre[:, c % 2, k:k + n]
                    if k == 0:
                        V.tensor_scalar(acc[:, c % 2, 0:n], x, tap_col, None, ALU.mult).then_inc(cv_ok, 1)
                    else:
                        dve.wait_ge(cv_ok, CONV_K * c + k)
                        V.scalar_tensor_tensor(out=acc[:, c % 2, 0:n], in0=x, scalar=tap_col, in1=acc[:, c % 2, 0:n],
                                               op0=ALU.mult, op1=ALU.add).then_inc(cv_ok, 1)

            dve.wait_ge(small_in, 16 * 16)
            s3 = sp_s.rearrange("p (t u) -> p t u", u=U8)
            dve.wait_ge(pj_ev, 13)
            v = done(V.tensor_tensor(s3, ab[:, :, 0, :], dt_bias.unsqueeze(1).broadcast_to([P, NT, U8]), ALU.add))
            dve.wait_ge(vec2, v)
            V.scalar_tensor_tensor(out=sp_e, in0=sp_s, scalar=-1.0, in1=sp_s, op0=ALU.mult, op1=ALU.max).then_inc(ab_v, 1)

            for i in range(2 * DH):
                dve.wait_ge(l2_std, i + 1)
                n = S + CTX if i < DH else S
                v = done(V.reciprocal(acc[:, i % 2, 0:n], acc[:, i % 2, 0:n]))
                dve.wait_ge(vec2, v)
                if i < DH:
                    V.tensor_tensor(kT[:, i, CTX:], kT[:, i, CTX:], acc[:, i % 2, 0:S], ALU.mult)
                    V.tensor_tensor(kT[:, i, 0:CTX], kT[:, i, 0:CTX], acc[:, i % 2, S:S + CTX], ALU.mult).then_inc(l2_ok, 1)
                else:
                    q = qT[:, i - DH, :]
                    V.scalar_tensor_tensor(out=q, in0=q, scalar=float(P) ** -0.5, in1=acc[:, i % 2, 0:S],
                                           op0=ALU.mult, op1=ALU.mult).then_inc(l2_ok, 1)

            dve.wait_ge(ab_a, 3)
            v = done(V.scalar_tensor_tensor(out=sp_s, in0=sp_s, scalar=0.0, in1=sp_e, op0=ALU.max, op1=ALU.add))
            dve.wait_ge(vec2, v)
            V.scalar_tensor_tensor(out=la, in0=s3, scalar=-1.0, in1=a_log.unsqueeze(1).broadcast_to([P, NT, U8]),
                                   op0=ALU.mult, op1=ALU.mult).then_inc(ab_v, 1)
            dve.wait_ge(ab_v, 2)
            dve.wait_ge(ab_a, 4)
            V.tensor_scalar(nbeta, beta, -1.0, None, ALU.mult).then_inc(ab_v, 1)

            def halves(dst, src):
                for t in range(NT):
                    ins = V.tensor_tensor(dst[:, t * U8:(t + 1) * U8, :], half,
                                          src[:, t, :].unsqueeze(2).broadcast_to([P, U8, 2]), ALU.mult)
                return ins

            halves(la_half, la).then_inc(ab_v, 1)
            dve.wait_ge(ab_mm, 1)
            dve.wait_ge(ab_a, 6)
            V.tensor_tensor(tail.rearrange("p t u -> p (t u)"), ps[5][:, 0:NT * U8], gsum.rearrange("p t u -> p (t u)"),
                            ALU.subtract).then_inc(ab_v, 1)
            V.tensor_tensor(beg, beta, eg, ALU.mult).then_inc(ab_v, 1)
            dve.wait_ge(ab_a, 8)
            halves(tail_half, tail).then_inc(ab_v, 1)
            V.tensor_copy(sp_s[:, 0:1], sp_s[:, 0:1]).then_inc(ab_v, 1)

            for step in range(NT):
                x = step >= CTX // P

                def needs(e, name, at_step=step):
                    delta.wait(dve, e, at_step, name)

                def says(name, ins):
                    delta.says("dve", step, name, ins)

                def every(v8):
                    return v8.unsqueeze(2).broadcast_to([P, U8, P])

                if step:
                    needs("pool", "ETI", step - 1)
                for d in range(2):
                    r = slice(d * DH, (d + 1) * DH)
                    ins = V.tensor_tensor(E[:, r, :], tri[:, d:d + 1, :].broadcast_to([P, DH, P]),
                                          la[:, step, r].unsqueeze(2).broadcast_to([P, DH, P]), ALU.mult)
                says("TRILA", ins)
                needs("pe", "G")
                says("SUB", V.tensor_tensor(E, pair(0), every(gsum[:, step, :]), ALU.subtract))
                needs("dve", "SUB")
                says("MIN", V.tensor_scalar(E, E, 0.0, None, ALU.min))
                needs("pe", "KK")
                needs("pool", "ETS")
                says("LT", V.tensor_tensor(ETS, pair(1), ETS, ALU.mult))
                if x:
                    needs("pe", "QK")
                    needs("pool", "ETI")
                    says("QKD", V.tensor_tensor(ETI, pair(2), ETI, ALU.mult))
                needs("pe", "L")
                says("PM", V.tensor_tensor(PA, pair(1), every(nbeta[:, step, :]), ALU.mult))
                needs("act", "PT")
                says("TT0", V.tensor_tensor(TT, PTA, ident.unsqueeze(1).broadcast_to([P, U8, P]), ALU.add))
                for r in range(1, 6):
                    if r < 5:
                        needs("pe", f"SQT{r}")
                        says(f"SQT{r}", V.tensor_copy((PTA, PTB)[r % 2], pair(0)))
                    needs("pe", f"TT{r}")
                    says(f"TT{r}", V.tensor_tensor(TT, TT, pair(1 if r % 2 else 2), ALU.add))
                needs("pe", "U")
                says("U", V.tensor_copy(PA, pair(0)))
                needs("dve", "U")
                for c in range(2):
                    needs("pe", f"WS{c}")
                    for name, d, h in (("UF", 0, c), ("UB", 1, 1 - c)):
                        rows, un = slice(h * CHUNK, (h + 1) * CHUNK), slice(d * DH, (d + 1) * DH)
                        says(f"{name}{c}", V.tensor_tensor(PTA[rows, un, :], PA[rows, un, :], pair(1)[rows, un, :], ALU.subtract))
                    needs("pe", f"SU{c}")
                    needs("pool", f"SD{c}")
                    says(f"S{c}", V.tensor_tensor(ST8, SD, pair(2), ALU.add))
                if x:
                    needs("pe", "X")
                    for d in range(2):
                        t = tile_of(step, d) - CTX // P
                        o = mix2[:, 0:DH, t * P:(t + 1) * P]
                        un = slice(d * DH, (d + 1) * DH)
                        says(f"Y{d}", V.tensor_tensor(o, o, pair(3)[:, un, :], ALU.add))
                        needs("dve", f"Y{d}")
                        says(f"X{d}", V.tensor_tensor(o, o, pair(0)[:, un, :], ALU.add))

            for h in range(DH):
                dve.wait_ge(l2_std, 2 * DH + h + 1)
                r, o = head_dev[:, h, :], mix2[:, h, :]
                v = done(V.reciprocal(r, r))
                dve.wait_ge(vec2, v)
                v = done(V.scalar_tensor_tensor(out=o, in0=o, scalar=par2[:, Q_DN:Q_DN + 1], in1=r, op0=ALU.mult, op1=ALU.mult))
                dve.wait_ge(vec2, v)
                V.tensor_tensor(o, o, gateT[:, h, :], ALU.mult).then_inc(l2_ok, 1)
            for t in range(KT):
                dve.wait_ge(wo_mm, t + 1)
                V.scalar_tensor_tensor(out=xT[:, t, :], in0=ps[4 + t % 4][:, :], scalar=mod[:, 2 * KT + t, 0:1],
                                       in1=xT[:, t, :], op0=ALU.mult, op1=ALU.add).then_inc(wo_ok, 1)
            rms(2, xT, zT)

            m4, s4 = sp_s[:, 0:ST], sp_s[:, ST:2 * ST]
            logits = ps[0][:, 0:ST * NE].rearrange("p (t e) -> p t e", e=NE)
            dve.wait_ge(rt_mm, 1)
            V.tensor_reduce(m4, logits, AX, ALU.max).then_inc(rt_v, 1)
            dve.wait_ge(rt_v, 1)
            V.tensor_tensor(aff, logits, m4.unsqueeze(2).broadcast_to([P, ST, NE]), ALU.subtract).then_inc(rt_v, 1)
            dve.wait_ge(rt_a, 1)
            V.tensor_reduce(s4, aff, AX, ALU.add).then_inc(rt_v, 1)
            dve.wait_ge(rt_v, 3)
            V.reciprocal(s4, s4).then_inc(rt_v, 1)
            dve.wait_ge(rt_v, 4)
            V.tensor_tensor(aff, aff, s4.unsqueeze(2).broadcast_to([P, ST, NE]), ALU.mult).then_inc(rt_v, 1)
            rv = [5]

            def next_rt(ins):
                ins.then_inc(rt_v, 1)
                rv[0] += 1
                dve.wait_ge(rt_v, rv[0])

            work, cum, zero = squares[0:NE, 0, :], squares[0:NE, 1, :], std[0:NE, :]
            best = stat[0:NE, 0, :]
            dve.wait_ge(rt_mm, 2)
            dve.sem_inc(e_lo.sem, 2)
            next_rt(V.tensor_copy(work, ps[1][0:NE, :]))
            for r in range(ROUNDS):
                next_rt(V.max(best, work))
                if r == ROUNDS - 1:
                    V.memset(zero, 0.0)
                ins = V.match_replace(work, best, work, -1.0)
                next_rt(ins)
            next_rt(V.tensor_scalar(work, work, 0.0, None, ALU.is_lt))
            next_rt(V.tensor_tensor_scan(cum, zero, work, 0.0, ALU.add, ALU.add))
            next_rt(V.tensor_tensor(zero, cum, work, ALU.mult))
            assert rv[0] == POS_KNOWN, rv
            dve.sem_inc(e_lo.sem, 1)
            dve.wait_ge(rt_mm, 3)
            v = done(V.tensor_copy(pos, ps[2][:, 0:ST * NE].rearrange("p (t e) -> p t e", e=NE)))
            dve.wait_ge(vec2, v)
            for t in range(ST):
                V.tensor_tensor(sel[:, t, :].rearrange("p (e c) -> p e c", c=CAP),
                                iota.unsqueeze(1).broadcast_to([P, NE, CAP]),
                                pos[:, t, :].unsqueeze(2).broadcast_to([P, NE, CAP]), ALU.is_equal).then_inc(se_ok, 1)

            dve.wait_ge(xe_ev, 2 * KT)
            dve.wait_ge(sw_ev, NE // 2)
            dve.sem_inc(e_lo.sem, 1)
            with dve.Fori(0, NE // 2) as q:
                def tokens(j):
                    x = xeT[:, :, bass.ds(q * (2 * CAP) + j * CAP, CAP)]
                    V.tensor_scalar(xs[:, :, HI], x, 1.0, None, ALU.mult).then_inc(ex_x.sem, 1)
                    dve.wait_ge(ex_x.sem, ex_x.at(q, 2 * j + 1))
                    V.tensor_tensor(xs[:, :, LO], x, xs[:, :, HI].bitcast(F32), ALU.subtract).then_inc(ex_x.sem, 1)

                def low(j, lo, hi):
                    for c in range(lo, hi):
                        dve.wait_ge(e_hi.sem, e_hi.at(q, EXP_CHUNKS * j + c + 1))
                        high_part, low_part = e_split[c % E_SPLIT]
                        V.tensor_tensor(low_part, e_raw[c % E_RAW], high_part.bitcast(F32), ALU.subtract).then_inc(e_lo.sem, 1)

                def hidden_values(j, hf):
                    dve.wait_ge(ex_silu.sem, ex_silu.at(q, 2 * j + hf + 1))
                    dve.wait_ge(e_used.sem, e_used.at(q, E_SPLIT + EXP_CHUNKS * j + 4 * hf + 4))
                    V.tensor_tensor(hid[0:CAP, :], gates[0:CAP, 0, :], ps[2 * hf + 1][0:CAP, :], ALU.mult).then_inc(ex_hid.sem, 1)

                def hidden_low(j, hf):
                    dve.wait_ge(ex_ht.sem, ex_ht.at(q, 2 * j + hf + 1))
                    f = slice(4 * hf, 4 * hf + 4)
                    V.tensor_tensor(hidT[:, f, LO], ps[4 + 3 * hf].rearrange("p (f c) -> p f c", c=P)[:, :, 0:CAP],
                                    hidT[:, f, HI].bitcast(F32), ALU.subtract).then_inc(ex_hl.sem, 1)

                def out_sum(j):
                    for n in range(2):
                        dve.wait_ge(ex_yb.sem, ex_yb.at(q, 2 * j + n + 1))
                        V.tensor_tensor(ye[j * CAP:(j + 1) * CAP, bass.ds(q, 1), n * 512:(n + 1) * 512],
                                        ps[5 + n][0:CAP, :].unsqueeze(1),
                                        (std[0:CAP, :] if n else gates[0:CAP, 1, :]).unsqueeze(1), ALU.add).then_inc(ex_ye.sem, 1)

                tokens(0)
                for j in range(2):
                    low(j, 0, 2)
                    if j == 1:
                        out_sum(0)
                    low(j, 2, 6)
                    hidden_values(j, 0)
                    low(j, 6, 9)
                    hidden_low(j, 0)
                    low(j, 9, 10)
                    hidden_values(j, 1)
                    if j == 0:
                        tokens(1)
                    low(j, 10, 12)
                    hidden_low(j, 1)
                out_sum(1)
            for f in range(KT):
                dve.wait_ge(cb_mm, f + 1)
                V.scalar_tensor_tensor(out=xT[:, f, :], in0=ps[f][:, :], scalar=mod[:, 5 * KT + f, 0:1], in1=xT[:, f, :],
                                       op0=ALU.mult, op1=ALU.add).then_inc(cb_ok, 1)
            rms(3, xT, zT)


def kernel(**inputs):
    import concourse.bacc as bacc
    from concourse.bass_utils import run_bass_kernel_spmd

    nc = bacc.Bacc("TRN2", target_bir_lowering=False, num_devices=1)
    arrays, aps = {}, {}
    for name, a in {**inputs, "consts": shape_constants()}.items():
        a = np.ascontiguousarray(a)
        arrays[f"in_{name}"] = a
        aps[name] = nc.dram_tensor(f"in_{name}", a.shape, mybir.dt.from_np(a.dtype), kind="ExternalInput").ap()
    out = nc.dram_tensor("out", (1, S, D), F32, kind="ExternalOutput").ap()
    build(nc, aps, out)
    r = run_bass_kernel_spmd(nc, [arrays], core_ids=[0])
    return r.results[0]["out"]
```

```python
from contextlib import ExitStack

import numpy as np

import concourse.bass as bass
from concourse import mybir

F32 = mybir.dt.float32
I32 = mybir.dt.int32
U32 = mybir.dt.uint32
F32R = mybir.dt.float32r
ACT = mybir.ActivationFunctionType
ALU = mybir.AluOpType
AX = mybir.AxisListType.X

P = 128
D = 1024
KT = D // P
S = 512
ST = S // P
MEM = 256
MT = MEM // P
DEPTH = 2
HEADS, NOPE, ROPE, VD = 8, 64, 32, 64
QK = NOPE + ROPE
LORA = 256
CW = 512
CT = CW // P
TAPS = 31
CONV0 = 2 * LORA + ROPE
IN_COLS = CONV0 + 2 * CW
XH, XD = 4, 256
FFN = 2816
FT = FFN // P
ALPHA = (2.0 * DEPTH) ** 0.25
LN_EPS = 1e-5
RMS_EPS = 1e-6
CHUNK = 64
NEG = -1e30
CTX = 256
DH = 4
CONV_K = 4
Q_BMOD, Q_N1, Q_N2, Q_NF, Q_C, Q_CC, Q_PS, Q_DN = 0, 48, 56, 64, 72, 80, 88, 92
NPAR2 = 93
NE, CAP = 16, 64
GRID_W = 64
ROWS = S // GRID_W
WINDOWS = (2, 4, 8, 16)

TWO_PI = 2.0 * np.pi
PI_A = 6.28125
PI_B = float(np.float32(int((TWO_PI - PI_A) * 2 ** 19)) / 2 ** 19)
PI_C = float(TWO_PI - PI_A - PI_B)
ROUND = 1.5 * 2.0 ** 23
PI_MAX = 3.1415925

SLOT = 4352
NSLOT = 3
LAYER_CHUNKS = 15
SLOT_CHUNKS = (5, 5, 4)
C_QKV, C_A, C_G, C_UP = 0, 1, 2, 3
MOD_CHUNKS = 6 * D // 512 // DEPTH
C_MOD = 4
C_XKV, C_SPLIT = 10, 14
HALF = FT // 2
N_MO, N_XQ, N_XO, N_FFN = 0, KT // 2, KT, 3 * KT // 2
SPLIT_CHUNKS = N_FFN + 2 * (HALF + KT)
RAW = KT * 2 * P

PB_CQ, PB_KR, PB_A, PB_G, P_QN, P_KVN = 0, 4, 5, 9, 13, 15
P_DWB, P_CNG, P_CNB, P_LN = 17, 21, 25, 29
NPAR = P_LN + 6 * KT

K_ID, K_ONE, K_SWAP = 0, P, 2 * P
K_FREQ = 3 * P
N_FIRST = K_FREQ + 1
K_TRI, K_STRICT = N_FIRST, N_FIRST + 2 * P
K_SAME = K_STRICT + 2 * P
K_HALF = K_SAME + P
K_IOTA = K_HALF + 2 * 2 * DH
K_CNT = K_IOTA + CAP
NCONST = K_CNT + 4 * S
ARENA = 26744


def shape_constants():
    c = np.zeros((P, NCONST), np.float32)
    i = np.arange(P)
    same = (i[:, None] // CHUNK) == (i[None, :] // CHUNK)
    c[:, K_ID:K_ID + P] = np.eye(P)
    c[:, K_ONE:K_ONE + P] = 1.0
    h = ROPE // 2
    for j in range(h):
        c[NOPE + h + j, K_SWAP + NOPE + j] = -1.0
        c[NOPE + j, K_SWAP + NOPE + h + j] = 1.0
    before = i[:, None] <= i[None, :]
    for d, m in enumerate((before, before.T)):
        c[:, K_TRI + d * P:K_TRI + (d + 1) * P] = m & same
        c[:, K_STRICT + d * P:K_STRICT + (d + 1) * P] = m & same & (i[:, None] != i[None, :])
    c[:, K_SAME:K_SAME + P] = same
    for u in range(2 * DH):
        for n in range(2):
            c[:, K_HALF + 2 * u + n] = (i // CHUNK) == (n if u < DH else 1 - n)
    c[:, K_IOTA:K_IOTA + CAP] = np.arange(CAP) + 1
    freq = np.float32(10000.0) ** (-np.arange(0, ROPE, 2, dtype=np.float32) / np.float32(ROPE))
    c[:, K_FREQ] = freq[i % h]
    for g, w in enumerate(WINDOWS):
        def span(n):
            p = np.arange(n)
            return np.clip(p - w // 2 + w, 0, n) - np.clip(p - w // 2, 0, n)
        cnt = (span(ROWS)[:, None] * span(GRID_W)[None, :]).astype(np.float32)
        c[:, K_CNT + g * S:K_CNT + (g + 1) * S] = (np.float32(1.0) / cnt).reshape(1, S)
    return c


class Signal:

    def __init__(self, sem, per):
        self.sem, self.per = sem, per

    def at(self, layer, n):
        return layer * self.per + n


def build(nc, A, out, debug=None):
    with ExitStack() as ctx:
        def sb(name, shape, dt=F32):
            return ctx.enter_context(nc.sbuf_tensor(name, shape, dt))

        def sem(name):
            return ctx.enter_context(nc.semaphore(name))

        def signal(name, per):
            return Signal(sem(name), per)

        def place():
            return -(-nc.sbuf_base // 32) * 32

        banks = ctx.enter_context(nc.psum_tensor("banks", [P, 8, 512], F32))
        ps = [banks[:, i, :] for i in range(8)]
        ring_at = place()
        ring = sb("ring", [P, NSLOT, SLOT])
        xT = sb("xT", [P, KT, S])
        zT = sb("zT", [P, KT, S])
        arena_at = place()
        arena = sb("arena", [P, ARENA])
        consts = sb("consts", [P, N_FIRST])
        cos_at = place()
        cosT = sb("cosT", [P, S])
        sinT = sb("sinT", [P, S])
        squares = sb("squares", [P, 2, S])
        std = sb("std", [P, S])
        gates = sb("gates", [P, 2, S])
        par_rows = sb("par_rows", [P, P])
        tap_rows = sb("tap_rows", [P, P])
        par = sb("par", [P, NPAR])
        taps = sb("taps", [P, TAPS * CT])
        stat = sb("stat", [P, 4, 8])
        eps = sb("eps", [P, 2])
        par2 = sb("par2", [P, NPAR2])[:, :]
        taps2 = sb("taps2", [P, CONV_K * 3 * DH])[:, :]
        cond = sb("cond", [P, KT, 2])[:, :, :]
        mod = sb("mod", [P, 6 * KT, 2])[:, :, :]

        def view(lo, *shape, of=None):
            n = int(np.prod(shape))
            v = (arena if of is None else of)[:, lo:lo + n]
            if len(shape) == 2:
                return v.rearrange("p (a b) -> p a b", a=shape[0])
            if len(shape) == 3:
                return v.rearrange("p (a b c) -> p a b c", a=shape[0], b=shape[1])
            return v

        BIG = 0
        memT = view(24 * S, KT, MEM)
        hpad = view(24 * S + KT * MEM, CT, TAPS - 1 + S)
        MIX = 24 * S + KT * MEM + CT * (TAPS - 1 + S)
        mixT = view(MIX, KT, S)
        probsT = view(MIX + KT * S, ST, S)
        xk = view(MIX + (KT + ST) * S, KT, MEM)
        xv = view(MIX + (KT + ST) * S + KT * MEM, MT, D)

        ident = consts[:, K_ID:K_ID + P]
        ones = consts[:, K_ONE:K_ONE + P]
        swap = consts[0:QK, K_SWAP:K_SWAP + QK]

        cqkv = view(0, 4, S)
        qh = view(4 * S, HEADS, S)
        kh = view(12 * S, HEADS, S)
        vt = view(20 * S, ST, HEADS * VD)
        xload = view(0, ST, D)
        memload = view(ST * D, MT, D)
        qx = view(0, KT, S)

        def split(name, base, lo, n):
            return [nc.alloc_sbuf_tensor_at(f"{name}_{part}", [P, n], F32R, offset=base + 4 * (lo + i * n)).ap()
                    for i, part in enumerate(("hi", "lo"))]

        def tiles(pair, n):
            return [x.rearrange("p (t n) -> p t n", n=n) for x in pair]

        raw = [ring[:, NSLOT - 1, i * RAW:(i + 1) * RAW] for i in range(2)]
        w_split = [split(f"w{i}", ring_at, i * SLOT, RAW) for i in range(2)]
        m_split = tiles(split("mixed", arena_at, 0, KT * S), S)
        xq_split = tiles([split("xq_hi", arena_at, MIX, KT * S)[0], split("xq_lo", arena_at, 2 * KT * S, KT * S)[0]], S)
        o_split = tiles(split("cross", arena_at, KT * S, KT * S), S)
        x_split = tiles(split("ffn_x", arena_at, MIX, KT * S), S)
        h_split = tiles(split("ffn_hidden", arena_at, 0, HALF * S), S)
        kr_raw = probsT[:, 0, :]
        rope_a = probsT[:, 2, :]
        rope_b = probsT[:, 3, :]
        probs = zT[:, :, :].rearrange("p (b t) n -> p b t n", b=2)

        loaded = [sem(f"slot{i}_loaded") for i in range(NSLOT)]
        used = sem("chunks_used")
        const_in = sem("const_in")
        x_in = sem("x_in")
        rows_in = sem("rows_in")
        rows_used = sem("rows_used")
        ready = sem("fills_ready")
        turned = sem("inputs_turned")
        turned_out = sem("inputs_turned_out")
        rope_v = sem("rope_angles")
        rope_s = sem("rope_sines")
        par_mm = signal("par_turned", 2)
        par_ev = signal("par_copied", 2)
        proj_mm = signal("proj_mm", 13)
        proj_ev = signal("proj_ev", 5)
        sig_ev = signal("gate_sigmoid", 4)
        glu = signal("glu", 4)
        lsq = signal("lora_squares", 4)
        lsum = signal("lora_sums", 2)
        lstd = signal("lora_std", 2)
        lnorm = signal("lora_normed", 4)
        krot_mm = signal("krot_mm", 1)
        krot = signal("krot_parts", 2)
        kcopy = signal("kr_in_heads", 1)
        up_mm = signal("up_mm", 20)
        q_ev = signal("q_ev", 8)
        kv_ev = signal("kv_ev", 12)
        qrot_mm = signal("qrot_mm", 8)
        qrot_sin = signal("qrot_sin", 8)
        qrot_cos = signal("qrot_cos", 8)
        qrot = signal("qrot", 8)
        sc_mm = signal("scores_mm", 32)
        sc_max = signal("scores_max", 32)
        sc_exp = signal("scores_exp", 32)
        sc_rec = signal("scores_reciprocal", 32)
        sc_norm = signal("scores_norm", 32)
        pt_mm = signal("probsT_mm", 32)
        pt_ev = signal("probsT_ev", 32)
        pv_mm = signal("pv_mm", 8)
        pv_ev = signal("pv_ev", 8)
        xkv_mm = signal("xkv_mm", 12)
        xkv_ev = signal("xkv_ev", 12)
        DT = CT - 1
        conv = signal("conv", DT * TAPS)
        conv_p = signal("conv_pool", 2 * TAPS)
        cstat_mm = signal("conv_stat_mm", 1)
        ccen = signal("conv_centred", CT)
        csq = signal("conv_squares", CT)
        cvar = signal("conv_var_mm", CT)
        cstd = signal("conv_std", 1)
        cmul = signal("conv_scaled", CT)
        cout = signal("conv_out", CT)
        res_mm = signal("residual_mm", 4 * KT + 1)
        z_ok = signal("z_summed", 4 * KT + 1)
        mean_mm = signal("mean_mm", 3)
        cen = signal("centred", 3 * KT)
        sq_ok = signal("squared", 3 * KT)
        var_mm = signal("var_mm", 3 * KT)
        std_ok = signal("std_ok", 3)
        scaled = signal("scaled", 3 * KT)
        x_ok = signal("x_normed", 3 * KT)
        xq_mm = signal("xq_mm", KT)
        xq_ev = signal("xq_ev", KT)
        xs_mm = signal("xscores_mm", 8)
        xs_max = signal("xscores_max", 8)
        xs_exp = signal("xscores_exp", 16)
        xs_norm = signal("xscores_norm", 16)
        xt_mm = signal("xprobsT_mm", 8)
        xt_ev = signal("xprobsT_ev", 8)
        xo_mm = signal("xpv_mm", 8)
        xo_ev = signal("xpv_ev", 8)
        ffn_mm = signal("ffn_mm", 2 * FT)
        ffn_act = signal("ffn_silu", FT)
        ffn_ok = signal("ffn_hidden", FT)
        raw_in = [sem(f"split_chunk{i}_in") for i in range(2)]
        f_hi = signal("split_chunk_hi", SPLIT_CHUNKS)
        f_lo = signal("split_chunk_lo", SPLIT_CHUNKS)
        x_part = signal("x_split", 4 * KT)
        m_part = signal("mixed_split", 2 * KT)
        h_part = signal("ffn_hidden_split", 2 * FT)
        vec = signal("vector_order", 94)
        stored = [sem(f"stored{i}") for i in range(2)]

        at = [0]

        def take(*shape):
            lo = at[0]
            at[0] += int(np.prod(shape))
            return view(lo, *shape)

        NC2 = K_CNT - K_TRI
        c2 = take(NC2)
        tri = c2[:, 0:2 * P].rearrange("p (d n) -> p d n", d=2)
        strict = c2[:, K_STRICT - K_TRI:K_STRICT - K_TRI + 2 * P].rearrange("p (d n) -> p d n", d=2)
        same = c2[:, K_SAME - K_TRI:K_SAME - K_TRI + P]
        half = c2[:, K_HALF - K_TRI:K_HALF - K_TRI + 4 * DH].rearrange("p (u c) -> p u c", c=2)
        iota = c2[:, K_IOTA - K_TRI:K_IOTA - K_TRI + CAP]
        gain = take(4, KT)
        a_log = take(2 * DH)
        dt_bias = take(2 * DH)
        w_rt = take(KT, NE)
        NT = (CTX + S) // P
        U8 = 2 * DH
        ab = take(NT, 2, U8)
        sp_s = take(NT * U8)
        sp_e = take(NT * U8)
        la = take(NT, U8)
        la_half = take(NT * U8, 2)
        beta = take(NT, U8)
        nbeta = take(NT, U8)
        eg = take(NT, U8)
        gsum = take(NT, U8)
        beg = take(NT, U8)
        tail = take(NT, U8)
        tail_half = take(NT * U8, 2)
        sdec = take(NT * U8, 2)
        at[0] = -(-at[0] // 8) * 8
        PHASE = at[0]
        kT = take(DH, NT * P)
        vT = take(DH, NT * P)
        qT = take(DH, S)
        gateT = take(DH, S)
        mix2 = take(KT, S)
        SCRATCH = at[0]
        hz = take(KT, CTX)
        ctx_in = take(CTX // P, D)
        PRE = S + CTX + 2 * (CONV_K - 1)
        pre = take(2, PRE)
        acc = take(2, PRE)
        pool_w = take(4, P)
        u = take(4, S)
        assert at[0] <= ARENA
        ctxT = view(SCRATCH + 2 * KT * CTX, KT, CTX)
        pool_a = mix2[:, 0:DH, :].rearrange("p a n -> p (a n)")
        pool_b = ctx_in.rearrange("p a n -> p (a n)")
        inv_cnt = mix2[:, DH:, :]
        at[0] = SCRATCH
        E, ETS, ETI, EG, KBG, KT0, KT1, VB, PA, PB = [take(U8, P) for _ in range(10)]
        assert at[0] <= ARENA
        zf = zT.rearrange("p a n -> p (a n)")
        PTA, PTB, TT, ST8 = [view(i * U8 * P, U8, P, of=zf) for i in range(4)]
        SD = squares.rearrange("p a (u n) -> p (a u) n", n=P)
        head_dev = view(SCRATCH, DH, S)
        at[0] = PHASE
        ye = take(NE // 2, D)
        h_tok = [nc.alloc_sbuf_tensor_at(f"h_tok_{part}", [P, ST, D], F32R, offset=offset).ap()
                 for part, offset in (("hi", arena_at + 4 * PHASE), ("lo", ring_at + 4 * 2 * ST * D))]
        sel = nc.alloc_sbuf_tensor_at("selection", [P, ST, NE * CAP], F32R, offset=arena_at + 4 * (PHASE + ST * D)).ap()
        at[0] = PHASE + 2 * ST * D
        sel_w = view(at[0], ST, NE * CAP)
        EC = 4 * 512
        EXP_CHUNKS = 3 * KT * D // EC
        E_RAW, E_SPLIT = 4, 3
        TURN = 4
        e_raw = [zT.rearrange("p a n -> p (a n)")[:, i * EC:(i + 1) * EC] for i in range(2)]
        e_raw += [nc.alloc_sbuf_tensor_at("expert_raw2", [P, EC], F32, offset=cos_at).ap(), view(at[0], EC)]
        e_split = [split(f"expert_w{i}", ring_at, 2 * i * EC, EC) for i in range(E_SPLIT)]
        xs, hidT = [nc.alloc_sbuf_tensor_at(name, [P, KT, 2 * CAP], F32R,
                                            offset=arena_at + 4 * (at[0] + EC + i * KT * 2 * CAP)).ap()
                    for i, name in enumerate(("expert_tokens_split", "expert_hidden_split"))]
        hid = ring.rearrange("p a n -> p (a n)")[:, 2 * E_SPLIT * EC:2 * E_SPLIT * EC + 512]
        HI, LO = slice(0, CAP), slice(CAP, 2 * CAP)
        at[0] += ST * D
        xeT = take(KT, NE * CAP)
        sel_wT = take(NE // 2, S)
        assert at[0] <= ARENA
        aff = gates[:, 0, 0:ST * NE].rearrange("p (t e) -> p t e", e=NE)
        pos = gates[:, 1, 0:ST * NE].rearrange("p (t e) -> p t e", e=NE)
        out_tok = view(PHASE, 2, D)

        def pair(i):
            return banks[:, 2 * i:2 * i + 2, :].rearrange("p b (h n) -> p (b h) n", n=P)

        def tile_of(step, d):
            n0, n1 = CTX // P, NT
            if d == 0:
                return step
            return n0 - 1 - step if step < n0 else n0 + n1 - 1 - step

        small_in = sem("small_in")
        p2_mm, p2_ev = sem("params2_turned"), sem("params2_copied")
        ctx_mm, ctx_ev = sem("ctx_turned"), sem("ctx_copied")
        cond_ok, mod_ok = sem("cond_silu"), sem("mod_ok")
        mod_rows, mod_row_ev = signal("mod_rows_mm", MOD_CHUNKS), signal("mod_rows_out", MOD_CHUNKS)
        mod_mm, mod_in = signal("mod_turned", MOD_CHUNKS), signal("mod_in", 1)
        n_sq, n_mm, n_std, n_mul, n_out = (sem(f"rms_{x}") for x in ("squared", "summed", "std", "scaled", "out"))
        pj_mm, pj_ev = sem("in_proj_mm"), sem("in_proj_out")
        cv_ok, cv_out = sem("short_conv"), sem("short_conv_silu")
        l2_sq, l2_mm, l2_std, l2_ok = (sem(f"l2_{x}") for x in ("squared", "summed", "std", "ok"))
        ab_a, ab_v, ab_mm = sem("decay_act"), sem("decay_vec"), sem("decay_mm")
        pl_ok, pl_mm, pl_ev = sem("pool_step"), sem("pool_mm"), sem("pool_out")
        vec2 = sem("vector_order2")
        padded = sem("short_conv_padded")
        wo_mm, wo_ok = sem("out_proj_mm"), sem("out_proj_ok")
        rt_mm, rt_v, rt_a = sem("router_mm"), sem("router_vec"), sem("router_act")
        ht_mm, ht_ev, ht_lo = sem("h_turned"), sem("h_high"), sem("h_low")
        se_ok, sw_ok = sem("slots_known"), sem("slots_weighted")
        xe_mm, xe_ev = sem("gathered_mm"), sem("gathered")
        sw_mm, sw_ev = sem("slots_turned"), sem("slots_copied")
        e_lo = Signal(sem("expert_chunk_lo"), TURN * EXP_CHUNKS)
        e_used = Signal(sem("expert_chunk_used"), TURN * EXP_CHUNKS)
        e_hi = Signal(sem("expert_chunk_hi"), TURN * EXP_CHUNKS)
        e_in = [sem(f"expert_chunk{i}_in") for i in range(E_RAW)]
        ex_x = Signal(sem("expert_tokens"), 2 * TURN)
        ex_silu = Signal(sem("expert_silu"), 2 * TURN)
        ex_hid = Signal(sem("expert_hidden"), 2 * TURN)
        ex_tm = Signal(sem("expert_hidden_turned"), 2 * TURN)
        ex_ht = Signal(sem("expert_hidden_hi"), 2 * TURN)
        ex_hl = Signal(sem("expert_hidden_lo"), 2 * TURN)
        ex_yb = Signal(sem("expert_out_lo"), 2 * TURN)
        ex_ye = Signal(sem("expert_out"), 2 * TURN)
        cb_mm, cb_ok = sem("combine_mm"), sem("combine_ok")
        fin_mm, fin_ev = sem("out_turned"), sem("out_copied")

        DIRS = {"f": slice(0, DH), "b": slice(DH, U8)}

        def events(step):
            x = step >= CTX // P
            r5 = range(1, 6)
            return {
                "pe": ["G", "KK"] + x * ["QK"] + ["KTOK", "VTOK", "L", "PT"]
                + [f"{n}{r}{d}" for r in r5 for n in (("SQ", "SQT", "TT") if r < 5 else ("SQ", "TT")) for d in "fb"]
                + ["WT", "U", "WS0f", "WS0b"] + x * ["Y0"] + ["SU0f", "SU0b", "WS1f", "WS1b"] + x * ["Y1"]
                + ["SU1f", "SU1b"] + x * ["X"],
                "dve": ["TRILA", "SUB", "MIN", "LT"] + x * ["QKD"] + ["PM", "TT0"]
                + [f"{n}{r}{d}" for r in r5 for n in (("SQT", "TT") if r < 5 else ("TT",)) for d in "fb"]
                + ["U"] + [f"{n}{c}{d}" for c in (0, 1) for n in ("U", "S") for d in "fb"] + x * ["Y0", "X0", "Y1", "X1"],
                "act": ["E"] + x * ["EG"] + ["KTOK", "VTOK", "PT"] + [f"SQ{r}{d}" for r in r5 for d in "fb"] + ["WT"],
                "pool": ["ETS", "ETI"] + x * ["QD"] + ["KBG", "KT0", "KT1", "VB", "SD0", "SD1"],
            }

        class Delta:

            def __init__(self):
                self.sem = {e: sem(f"delta_{e}") for e in ("pe", "dve", "act", "pool")}
                self.value = {}
                n = {e: 0 for e in self.sem}
                for step in range(NT):
                    for e, names in events(step).items():
                        for name in names:
                            n[e] += 1
                            self.value[e, step, name] = n[e]
                self.said = {e: 0 for e in self.sem}

            def says(self, e, step, name, ins):
                self.said[e] += 1
                assert self.value[e, step, name] == self.said[e], (e, step, name)
                ins.then_inc(self.sem[e], 1)

            def wait(self, eng, e, step, name):
                eng.wait_ge(self.sem[e], self.value[e, step, name])

            def last(self, e):
                return max(v for (x, _, _), v in self.value.items() if x == e)

        delta = Delta()
        MOD_TILES = 6 * KT // DEPTH
        mod_row = ps[4][VD:VD + 2, :]
        mod_sum = ps[5][:, 0:2 * MOD_TILES].rearrange("p (j w) -> p j w", w=2)
        POOL_STEPS = list(np.cumsum([6 + 2 * int(np.log2(win)) for win in WINDOWS]))
        POOL_STEPS = [int(n) for n in POOL_STEPS] + [int(POOL_STEPS[-1]) + 1]
        ROUNDS = CAP // 8
        POS_KNOWN = 5 + 1 + 2 * ROUNDS + 3
        LAYERS_DONE = DEPTH * x_ok.per
        C2 = DEPTH * LAYER_CHUNKS
        C_IN, C_OUT2 = C2, C2 + 5
        DW = DH * P
        IN_RANGES = ((3 * DW + 16 + DW, 4 * DW + 16 + DW), (DW, 2 * DW), (2 * DW, 3 * DW + 16), (0, DW),
                     (3 * DW + 16, 4 * DW + 16))

        def slot(c):
            return c % NSLOT

        def arrivals(c):
            return 32 * (DEPTH * SLOT_CHUNKS[slot(c)] + (c - C2) // NSLOT + 1)

        def ffn_chunk(n):
            half_no, i = (n - N_FFN) // (HALF + KT), (n - N_FFN) % (HALF + KT)
            return (half_no, half_no * HALF + i, True) if i < HALF else (half_no, i - HALF, False)

        def chunk_floats(n):
            return RAW if n < N_FFN or ffn_chunk(n)[2] else HALF * P

        def chunk_used(eng, l, n):
            if n < N_FFN:
                signal_, first = ((res_mm, 0), (xq_mm, 0), (res_mm, KT))[n // (KT // 2)]
                eng.wait_ge(signal_.sem, signal_.at(l, first + 2 * (n % (KT // 2)) + 2))
                return
            half_no, t, hidden_tile = ffn_chunk(n)
            if hidden_tile:
                eng.wait_ge(ffn_mm.sem, ffn_mm.at(l, 2 * t + 2))
            else:
                eng.wait_ge(res_mm.sem, res_mm.at(l, (2 + half_no) * KT + t + 1))

        def part_ready(eng, sig, l, first, k):
            eng.wait_ge(sig.sem, sig.at(l, first + min(2 * k + 3, 2 * KT)))

        def w(c, lo, *shape):
            n = int(np.prod(shape))
            v = ring[:, slot(c), lo:lo + n]
            if len(shape) == 2:
                return v.rearrange("p (a b) -> p a b", a=shape[0])
            return v.rearrange("p (a b c) -> p a b c", a=shape[0], b=shape[1])

        block = ctx.enter_context(nc.Block())

        @block.sync
        def _(sp):
            sp.dma_start(consts[:, :], A["consts"][:, 0:N_FIRST]).then_inc(const_in, 16)
            sp.dma_start(rope_a.bitcast(I32), A["positions"].broadcast_to([P, S])).then_inc(const_in, 16)
            sp.dma_start(xload, A["x"][0].rearrange("(t p) d -> p t d", p=P)).then_inc(x_in, 16)
            sp.dma_start(memload, A["mem"][0].rearrange("(t p) d -> p t d", p=P)).then_inc(x_in, 16)
            sp.wait_ge(ready, 2)
            for dst, name, n in ((Q_BMOD, "b_mod_2", 6 * KT), (Q_N1, "norm1_2", KT), (Q_N2, "norm2_2", KT),
                                 (Q_C, "c_2", KT), (Q_PS, "pool_scale_2", 4), (Q_DN, "dn_norm_2", 1)):
                sp.dma_start(par_rows[dst:dst + n, :], A[name].rearrange("a (r c) -> (a r) c", c=P)).then_inc(small_in, 16)
            for dst, name in ((Q_NF, "norm_f_2"), (Q_CC, "c_ctx_2")):
                sp.dma_start(par_rows[dst:dst + KT, :], A[name].rearrange("(r c) -> r c", c=P)).then_inc(small_in, 16)
            sp.dma_start(tap_rows[0:CONV_K * 3 * DH, :],
                         A["conv_w_2"].rearrange("a k (t p) -> (a k t) p", p=P)).then_inc(small_in, 16)

            with sp.Fori(0, DEPTH) as l:
                def layer(name):
                    return A[name][bass.ds(l, 1)]

                def row(dst, name, lo, n):
                    src = layer(name)[:, lo:lo + n * P].rearrange("a (r c) -> (a r) c", c=P)
                    sp.dma_start(par_rows[dst:dst + n, :], src).then_inc(rows_in, 16)

                def load(c, halves):
                    sp.wait_ge(used, l * LAYER_CHUNKS + c + 1)
                    for dst, src in halves:
                        sp.dma_start(dst, src).then_inc(loaded[slot(c)], 16)

                def matrix(c, name, lo, n, lo2=None):
                    src = layer(name).rearrange("a (k p) n -> p (a k) n", p=P)
                    m = KT // 2
                    if lo2 is None:
                        dst = w(c, 0, KT, n)
                        load(c, [(dst[:, h * m:(h + 1) * m], src[:, h * m:(h + 1) * m, lo:lo + n])
                                 for h in range(2)])
                    else:
                        load(c, [(w(c, h * KT * n, KT, n), src[:, :, at:at + n])
                                 for h, at in enumerate((lo, lo2))])

                matrix(C_QKV, "mix_w_in", 0, CONV0)
                sp.wait_ge(rows_used, l + 1)
                row(PB_CQ, "mix_b_in", 0, 4)
                sp.dma_start(par_rows[PB_KR:PB_KR + 1, 0:QK],
                             layer("mix_b_in")[:, CONV0 - QK:CONV0]).then_inc(rows_in, 16)
                row(PB_A, "mix_b_in", CONV0, 2 * CT)
                row(P_QN, "mla_q_norm", 0, 2)
                row(P_KVN, "mla_kv_norm", 0, 2)
                row(P_DWB, "conv_dw_b", 0, CT)
                row(P_CNG, "conv_norm_g", 0, CT)
                row(P_CNB, "conv_norm_b", 0, CT)
                for j, name in enumerate(("ln1_g", "ln1_b", "ln2_g", "ln2_b", "ln3_g", "ln3_b")):
                    row(P_LN + j * KT, name, 0, KT)
                sp.dma_start(tap_rows[0:TAPS * CT, :],
                             layer("conv_dw_w").rearrange("a k (t p) -> (a k t) p", p=P)).then_inc(rows_in, 16)
                matrix(C_A, "mix_w_in", CONV0, CW)
                matrix(C_G, "mix_w_in", CONV0 + CW, CW)
                nq, nkv = HEADS * QK, HEADS * (NOPE + VD)
                load(C_UP, [(w(C_UP, 0, 2, nq), layer("mla_w_uq").rearrange("a (k p) n -> p (a k) n", p=P)),
                            (w(C_UP, 2 * nq, 2, nkv), layer("mla_w_ukv").rearrange("a (k p) n -> p (a k) n", p=P))])
                w_mod = A["w_mod_2"][0].rearrange("(k p) n -> p k n", p=P)
                for j in range(MOD_CHUNKS):
                    dst, m = w(C_MOD + j, 0, KT, 512), KT // 2
                    load(C_MOD + j, [(dst[:, h * m:(h + 1) * m],
                                      w_mod[:, h * m:(h + 1) * m, bass.ds(l * (MOD_CHUNKS * 512) + j * 512, 512)])
                                     for h in range(2)])
                for j in range(4):
                    matrix(C_XKV + j, "xa_w_kv", j * 512, 512)
                gate_up = layer("ffn_w_in").rearrange("a (k p) n -> p (a k) n", p=P)
                down = layer("ffn_w_down").rearrange("a (k p) n -> p (a k) n", p=P)
                for n in range(SPLIT_CHUNKS):
                    if n == 0:
                        sp.wait_ge(used, l * LAYER_CHUNKS + C_SPLIT + 1)
                    if n >= 2:
                        sp.wait_ge(f_lo.sem, f_lo.at(l, n - 1))
                    if n < N_FFN:
                        src = layer(("mix_w_o", "xa_w_q", "xa_w_o")[n // 4]).rearrange("a (k p) n -> p (a k) n", p=P)
                        dst, lo = raw[n % 2].rearrange("p (k c) -> p k c", k=KT), n % 4 * 2 * P
                        for a in (0, KT // 2):
                            sp.dma_start(dst[:, a:a + KT // 2], src[:, a:a + KT // 2, lo:lo + 2 * P]).then_inc(raw_in[n % 2], 16)
                        continue
                    half_no, t, hidden_tile = ffn_chunk(n)
                    if hidden_tile:
                        dst = raw[n % 2].rearrange("p (j k c) -> p j k c", j=2, k=KT)
                        for j in range(2):
                            lo = j * FFN + t * P
                            sp.dma_start(dst[:, j], gate_up[:, :, lo:lo + P]).then_inc(raw_in[n % 2], 16)
                    else:
                        dst = raw[n % 2][:, 0:HALF * P].rearrange("p (k c) -> p k c", c=P)
                        for a, b in ((0, HALF // 2), (HALF // 2, HALF)):
                            k0 = half_no * HALF
                            sp.dma_start(dst[:, a:b], down[:, k0 + a:k0 + b, t * P:(t + 1) * P]).then_inc(raw_in[n % 2], 16)
            def load2(c, halves):
                sp.wait_ge(used, c + 1)
                for dst, src in halves:
                    sp.dma_start(dst, src).then_inc(loaded[slot(c)], 16)

            def matrix2(c, src, lo, hi):
                src = src.rearrange("(k p) n -> p k n", p=P)
                dst, m = w(c, 0, KT, hi - lo), KT // 2
                load2(c, [(dst[:, h * m:(h + 1) * m], src[:, h * m:(h + 1) * m, lo:hi]) for h in range(2)])

            for j in range(NSLOT):
                matrix2(C_IN + j, A["w_in_2"][0], *IN_RANGES[j])
            sp.wait_ge(x_ok.sem, LAYERS_DONE)
            sp.dma_start(c2, A["consts"][:, K_TRI:K_CNT]).then_inc(small_in, 16)
            sp.dma_start(inv_cnt, A["consts"][:, K_CNT:].rearrange("p (g n) -> p g n", g=4)).then_inc(small_in, 16)
            sp.dma_start(a_log, A["a_log_2"].rearrange("a d h -> a (d h)").broadcast_to([P, U8])).then_inc(small_in, 16)
            sp.dma_start(dt_bias, A["dt_bias_2"].rearrange("a d h -> a (d h)").broadcast_to([P, U8])).then_inc(small_in, 16)
            sp.dma_start(w_rt, A["w_router_2"][0].rearrange("(k p) n -> p k n", p=P)).then_inc(small_in, 16)
            sp.dma_start(pool_w, A["pool_w_2"][0].rearrange("g c d -> c g d")).then_inc(small_in, 16)
            sp.dma_start(ctx_in, A["ctx_2"][0].rearrange("(t p) d -> p t d", p=P)).then_inc(small_in, 16)
            for j in range(NSLOT, 5):
                matrix2(C_IN + j, A["w_in_2"][0], *IN_RANGES[j])
            for j in range(2):
                matrix2(C_OUT2 + j, A["w_out_2"][0], j * 512, (j + 1) * 512)
            with sp.Fori(0, NE) as e:
                for c in range(EXP_CHUNKS):
                    sp.wait_ge(e_lo.sem, e * EXP_CHUNKS + c + 1)
                    name = ("w_gate_2", "w_up_2")[c // 2 % 2] if c < 8 else "w_down_2"
                    src = A[name][0][bass.ds(e, 1)].rearrange("a (k p) n -> p (a k) n", p=P)
                    if c < 8:
                        k0, n0 = 4 * (c % 2), 512 * (c // 4)
                        src = src[:, k0:k0 + 4, n0:n0 + 512]
                    else:
                        src = src[:, 2 * (c - 8):2 * (c - 8) + 2, :]
                    dst = e_raw[c % E_RAW].rearrange("p (k n) -> p k n", k=4 if c < 8 else 2)
                    sp.dma_start(dst, src).then_inc(e_in[c % E_RAW], 16)
            for t in range(ST):
                sp.wait_ge(fin_ev, 2 * (t + 1))
                sp.dma_start(out[0, t * P:(t + 1) * P, :], out_tok[:, t % 2, :]).then_inc(stored[t % 2], 16)
            for i in range(2):
                sp.wait_ge(stored[i], 16 * ST // 2)

        @block.tensor
        def _(pe):
            pe.sem_inc(used, NSLOT)
            pe.wait_ge(const_in, 32)
            pe.wait_ge(x_in, 32)
            for f in range(2 * KT):
                if f >= 4:
                    pe.wait_ge(turned_out, f - 3)
                src, n = (xload, ST) if f < KT else (memload, MT)
                for t in range(n):
                    mm = pe.transpose(ps[f % 4][:, t * P:(t + 1) * P],
                                      src[:, t, (f % KT) * P:(f % KT + 1) * P], ident)
                mm.then_inc(turned, 1)
            pe.wait_ge(turned_out, 2 * KT)
            pe.wait_ge(small_in, 9 * 16)
            pe.transpose(ps[6][:, 0:P], par_rows[:, :], ident).then_inc(p2_mm, 1)
            pe.transpose(ps[7][:, 0:P], tap_rows[:, :], ident).then_inc(p2_mm, 1)
            pe.wait_ge(p2_ev, 2)
            pe.sem_inc(rows_used, 1)
            pe.wait_ge(cond_ok, 2)

            with pe.Fori(0, DEPTH) as l:
                def arrived(c):
                    pe.wait_ge(loaded[slot(c)], l * (32 * SLOT_CHUNKS[slot(c)]) + 32 * (c // NSLOT + 1))

                spent = [0]

                def give_back(n):
                    spent[0] += n

                def say_spent(mm):
                    if spent[0]:
                        mm.then_inc(used, spent[0])
                        spent[0] = 0

                def product(bank, weights, rhs, n=KT, width=S, m=P):
                    for k in range(n):
                        mm = pe.matmul(bank[0:m, 0:width], weights(k), rhs(k), start=(k == 0), stop=(k == n - 1))
                        if k == 0:
                            say_spent(mm)
                    return mm

                def norm_sums(i, z0, bank):
                    for t in range(KT):
                        pe.wait_ge(z_ok.sem, z_ok.at(l, z0 + t + 1))
                        mm = pe.matmul(ps[bank][:, :], ones, zT[:, t, :], start=(t == 0), stop=(t == KT - 1))
                        if t == 0:
                            say_spent(mm)
                    mm.then_inc(mean_mm.sem, 1)
                    for t in range(KT):
                        pe.wait_ge(sq_ok.sem, sq_ok.at(l, i * KT + t + 1))
                        mm = pe.matmul(ps[bank + 1][:, :], ones, squares[:, t % 2, :], start=(t == 0), stop=(t == KT - 1))
                        mm.then_inc(var_mm.sem, 1)

                def split_product(bank, weights, rhs, n, need):
                    for k in range(n):
                        need(k)
                        for wp, rp in ((0, 0), (0, 1), (1, 0)):
                            mm = pe.matmul(bank[:, :], weights(wp, k), rhs(rp, k), start=(k == 0 and wp == rp),
                                           stop=(k == n - 1 and wp == 1))
                    return mm

                def split_tile(bank, n0, t, rhs, ready):
                    n = n0 + t // 2
                    if t % 2 == 0:
                        pe.wait_ge(f_lo.sem, f_lo.at(l, n + 1))
                    ws = tiles(w_split[n % 2], 2 * P)
                    return split_product(bank, lambda i, k: ws[i][:, k, (t % 2) * P:(t % 2 + 1) * P],
                                         lambda i, k: rhs[i][:, k, :], KT, ready if t == 0 else lambda k: None)

                def residual(i, n0, rhs, ready):
                    for t in range(KT):
                        if t >= 4:
                            pe.wait_ge(z_ok.sem, z_ok.at(l, i * KT + t - 3))
                        split_tile(ps[(6, 7, 4, 5)[t % 4]], n0, t, rhs, ready).then_inc(res_mm.sem, 1)

                pe.wait_ge(rows_in, l * (15 * 16) + 15 * 16)
                pe.transpose(ps[6][:, 0:P], par_rows[:, :], ident).then_inc(par_mm.sem, 1)
                pe.transpose(ps[7][:, 0:P], tap_rows[:, :], ident).then_inc(par_mm.sem, 1)
                pe.wait_ge(par_ev.sem, par_ev.at(l, 2))
                pe.sem_inc(rows_used, 1)

                arrived(C_QKV)
                wq = w(C_QKV, 0, KT, CONV0)
                for n in range(5):
                    lo, m = (n * P, P) if n < 4 else (CONV0 - QK, QK)
                    mm = product(ps[n], lambda k: wq[:, k, lo:lo + m], lambda k: xT[:, k, :], m=m)
                    mm.then_inc(proj_mm.sem, 1)
                give_back(1)
                arrived(C_A)
                arrived(C_G)
                for t in range(CT):
                    for j in range(2):
                        n = 5 + 2 * t + j
                        if n >= 8:
                            pe.wait_ge(proj_ev.sem, proj_ev.at(l, n - 7))
                        wc = w(C_A + j, 0, KT, CW)
                        mm = product(ps[n % 8], lambda k: wc[:, k, t * P:(t + 1) * P], lambda k: xT[:, k, :])
                        mm.then_inc(proj_mm.sem, 1)
                give_back(2)

                pe.wait_ge(glu.sem, glu.at(l, 2))
                for n in range(2):
                    for k in range(2):
                        pe.wait_ge(lsq.sem, lsq.at(l, 2 * n + k + 1))
                        mm = pe.matmul(ps[5 + n][:, :], ones, mixT[:, 2 * n + k, :], start=(k == 0), stop=(k == 1))
                    mm.then_inc(lsum.sem, 1)
                pe.wait_ge(proj_ev.sem, proj_ev.at(l, 5))
                pe.matmul(ps[7][0:QK, :], swap, kr_raw[0:QK, :], start=True, stop=True).then_inc(krot_mm.sem, 1)

                arrived(C_UP)
                wuq = w(C_UP, 0, 2, HEADS * QK)
                wukv = w(C_UP, 2 * HEADS * QK, 2, HEADS * (NOPE + VD))
                wv = w(C_UP, 2 * HEADS * QK, 2, HEADS, NOPE + VD)
                pe.wait_ge(glu.sem, glu.at(l, CT))
                pe.wait_ge(lnorm.sem, lnorm.at(l, 2))
                for h in range(HEADS):
                    if h == 7:
                        pe.wait_ge(krot.sem, krot.at(l, 2))
                    if h == 5:
                        pe.wait_ge(lnorm.sem, lnorm.at(l, 4))
                    mm = product(ps[h], lambda k: wuq[:, k, h * QK:(h + 1) * QK], lambda k: cqkv[:, k, :], 2, m=QK)
                    mm.then_inc(up_mm.sem, 1)
                for h in range(HEADS):
                    pe.wait_ge(q_ev.sem, q_ev.at(l, h + 1))
                    lo = h * (NOPE + VD)
                    mm = product(ps[h], lambda k: wukv[:, k, lo:lo + NOPE], lambda k: cqkv[:, 2 + k, :], 2, m=NOPE)
                    mm.then_inc(up_mm.sem, 1)
                for t in range(ST):
                    pe.wait_ge(kv_ev.sem, kv_ev.at(l, t + 1))
                    mm = product(ps[t], lambda k: cqkv[:, 2 + k, t * P:(t + 1) * P], lambda k: wv[:, k, :, NOPE:], 2)
                    mm.then_inc(up_mm.sem, 1)
                give_back(1)
                for h in range(HEADS):
                    b = 4 + h % 4
                    pe.wait_ge(kv_ev.sem, kv_ev.at(l, 5 + h % 4))
                    if h >= 4:
                        pe.wait_ge(qrot_sin.sem, qrot_sin.at(l, h - 3))
                    pe.matmul(ps[b][0:QK, :], swap, qh[0:QK, h, :], start=True, stop=True).then_inc(qrot_mm.sem, 1)

                sc_bank = (0, 1, 6, 7)

                def scores(h):
                    pe.wait_ge(qrot.sem, qrot.at(l, h + 1))
                    for t in range(ST):
                        n = h * ST + t
                        if n == 0:
                            pe.wait_ge(kv_ev.sem, kv_ev.at(l, 12))
                            pe.wait_ge(kcopy.sem, kcopy.at(l, 1))
                            pe.wait_ge(qrot_sin.sem, qrot_sin.at(l, HEADS))
                        if n >= 4:
                            pe.wait_ge(sc_exp.sem, sc_exp.at(l, n - 3))
                        pe.matmul(ps[sc_bank[t]][:, 0:(t + 1) * P], qh[0:QK, h, t * P:(t + 1) * P],
                                  kh[0:QK, h, 0:(t + 1) * P], start=True, stop=True).then_inc(sc_mm.sem, 1)

                def values(h):
                    for kt in range(ST):
                        n = h * ST + kt
                        if n >= 2:
                            pe.wait_ge(pt_ev.sem, pt_ev.at(l, n - 1))
                        for t in range(kt, ST):
                            if kt == 0:
                                pe.wait_ge(sc_norm.sem, sc_norm.at(l, h * ST + t + 1))
                            mm = pe.transpose(ps[2 + n % 2][:, t * P:(t + 1) * P],
                                              probs[:, h % 2, t, kt * P:(kt + 1) * P], ident)
                        mm.then_inc(pt_mm.sem, 1)
                    if h >= 1:
                        pe.wait_ge(pv_ev.sem, pv_ev.at(l, h))
                    for kt in range(ST):
                        pe.wait_ge(pt_ev.sem, pt_ev.at(l, h * ST + kt + 1))
                        mm = pe.matmul(ps[4][0:VD, kt * P:S], vt[:, kt, h * VD:(h + 1) * VD],
                                       probsT[:, kt, kt * P:S], start=(kt == 0), stop=(kt == ST - 1))
                    mm.then_inc(pv_mm.sem, 1)

                def modulation_rows(i):
                    arrived(C_MOD + i)
                    wm = w(C_MOD + i, 0, KT, 512)
                    if i >= 1:
                        pe.wait_ge(mod_row_ev.sem, mod_row_ev.at(l, i))
                    for k in range(KT):
                        mm = pe.matmul(mod_row, cond[:, k, :], wm[:, k, :], start=(k == 0), stop=(k == KT - 1))
                        if k == 0:
                            say_spent(mm)
                    mm.then_inc(mod_rows.sem, 1)
                    give_back(1)

                def modulation_turn(i):
                    pe.wait_ge(mod_row_ev.sem, mod_row_ev.at(l, i + 1))
                    for j in range(4):
                        mm = pe.matmul(mod_sum[:, 4 * i + j, :], gates[0:2, i % 2, j * P:(j + 1) * P], ident[0:2, 0:2],
                                       start=True, stop=True)
                    mm.then_inc(mod_mm.sem, 1)

                scores(0)
                scores(1)
                for h in range(HEADS):
                    if h < MOD_CHUNKS:
                        modulation_rows(h)
                    if h + 2 < HEADS:
                        scores(h + 2)
                    values(h)
                    if h < MOD_CHUNKS:
                        modulation_turn(h)

                pe.wait_ge(sc_exp.sem, sc_exp.at(l, 32))
                for n in range(12):
                    b = sc_bank[n % 4]
                    c = C_XKV + (n // 4 if n < 8 else 2 + (n - 8) % 2)
                    if n in (0, 4, 8, 9):
                        arrived(c)
                    if n >= 4:
                        pe.wait_ge(xkv_ev.sem, xkv_ev.at(l, n - 3))
                    wkv = w(c, 0, KT, 512)
                    if n < 8:
                        mm = product(ps[b], lambda k: wkv[:, k, (n % 4) * P:(n % 4 + 1) * P],
                                     lambda k: memT[:, k, :], width=MEM)
                    else:
                        t = (n - 8) // 2
                        mm = product(ps[b], lambda k: memT[:, k, t * P:(t + 1) * P], lambda k: wkv[:, k, :])
                    mm.then_inc(xkv_mm.sem, 1)
                    if n in (3, 7):
                        give_back(1)

                pe.wait_ge(pt_ev.sem, pt_ev.at(l, 32))
                for t in range(CT):
                    if t < DT:
                        pe.wait_ge(conv.sem, conv.at(l, DT * (TAPS - 1) + t + 1))
                    else:
                        pe.wait_ge(conv_p.sem, conv_p.at(l, 2 * TAPS))
                    mm = pe.matmul(ps[2][:, :], ones, mixT[:, CT + t, :], start=(t == 0), stop=(t == CT - 1))
                mm.then_inc(cstat_mm.sem, 1)
                for t in range(CT):
                    pe.wait_ge(csq.sem, csq.at(l, t + 1))
                    mm = pe.matmul(ps[3][:, :], ones, squares[:, t % 2, :], start=(t == 0), stop=(t == CT - 1))
                    mm.then_inc(cvar.sem, 1)

                pe.wait_ge(pv_ev.sem, pv_ev.at(l, HEADS))
                pe.wait_ge(mod_in.sem, mod_in.at(l, 1))
                pe.wait_ge(xkv_ev.sem, xkv_ev.at(l, 12))
                residual(0, N_MO, m_split, lambda k: part_ready(pe, m_part, l, 0, k))
                norm_sums(0, 0, 0)

                for t in range(KT):
                    if t >= 4:
                        pe.wait_ge(xq_ev.sem, xq_ev.at(l, t - 3))
                    split_tile(ps[2 + t % 4], N_XQ, t, xq_split, lambda k: part_ready(pe, x_part, l, 0, k))\
                        .then_inc(xq_mm.sem, 1)

                def xscores(h):
                    pe.wait_ge(xq_ev.sem, xq_ev.at(l, min(2 * h + 2, KT)))
                    for j in range(2):
                        n = 2 * h + j
                        if n >= 4:
                            pe.wait_ge(xs_exp.sem, xs_exp.at(l, 2 * (n - 3)))
                        for i in range(2):
                            t = 2 * j + i
                            for k in range(2):
                                mm = pe.matmul(ps[sc_bank[n % 4]][:, i * MEM:(i + 1) * MEM],
                                               qx[:, 2 * h + k, t * P:(t + 1) * P], xk[:, 2 * h + k, :],
                                               start=(k == 0), stop=(k == 1))
                        mm.then_inc(xs_mm.sem, 1)

                def xvalues(h):
                    for kt in range(MT):
                        n = 2 * h + kt
                        if n >= 2:
                            pe.wait_ge(xt_ev.sem, xt_ev.at(l, n - 1))
                        else:
                            pe.wait_ge(xq_ev.sem, xq_ev.at(l, KT))
                        for t in range(ST):
                            if kt == 0:
                                pe.wait_ge(xs_norm.sem, xs_norm.at(l, ST * h + t + 1))
                            mm = pe.transpose(ps[2 + kt][:, t * P:(t + 1) * P],
                                              probs[:, h % 2, t, kt * P:(kt + 1) * P], ident)
                        mm.then_inc(xt_mm.sem, 1)
                    for v in range(2):
                        n = 2 * h + v
                        if n >= 2:
                            pe.wait_ge(xo_ev.sem, xo_ev.at(l, n - 1))
                        for kt in range(MT):
                            pe.wait_ge(xt_ev.sem, xt_ev.at(l, 2 * h + kt + 1))
                            mm = pe.matmul(ps[4 + v][:, :], xv[:, kt, h * XD + v * P:h * XD + (v + 1) * P],
                                           probsT[:, kt, :], start=(kt == 0), stop=(kt == MT - 1))
                        mm.then_inc(xo_mm.sem, 1)

                for h in range(XH + 1):
                    if h < XH:
                        xscores(h)
                    if h >= 1:
                        xvalues(h - 1)
                residual(1, N_XO, o_split, lambda k: pe.wait_ge(xo_ev.sem, xo_ev.at(l, k + 1)))
                norm_sums(1, KT, 0)

                out_bank = (6, 7, 0, 1)
                for n in range(N_FFN, SPLIT_CHUNKS):
                    half_no, t, hidden_tile = ffn_chunk(n)
                    pe.wait_ge(f_lo.sem, f_lo.at(l, n + 1))
                    if hidden_tile:
                        if t >= 4:
                            pe.wait_ge(ffn_ok.sem, ffn_ok.at(l, t - 3))
                        if t in (HALF, HALF + 1):
                            pe.wait_ge(z_ok.sem, z_ok.at(l, 2 * KT + (6 if t == HALF else KT)))

                        def x_ready(k):
                            if t == 0:
                                part_ready(pe, x_part, l, 2 * KT, k)

                        for j in range(2):
                            wf = [x.rearrange("p (j k c) -> p j k c", j=2, k=KT) for x in w_split[n % 2]]
                            mm = split_product(ps[2 * (t % 4) + j], lambda i, k: wf[i][:, j, k, :],
                                               lambda i, k: x_split[i][:, k, :], KT, x_ready)
                            mm.then_inc(ffn_mm.sem, 1)
                    else:
                        if t == 0:
                            pe.wait_ge(ffn_ok.sem, ffn_ok.at(l, half_no * HALF + HALF - 2))
                        if t >= 4:
                            pe.wait_ge(z_ok.sem, z_ok.at(l, (2 + half_no) * KT + t - 3))

                        def hidden_ready(k):
                            if t == 0:
                                pe.wait_ge(h_part.sem, h_part.at(l, 2 * (half_no * HALF + k) + 2))

                        wd = [x[:, 0:HALF * P].rearrange("p (k c) -> p k c", c=P) for x in w_split[n % 2]]
                        mm = split_product(ps[out_bank[t % 4]], lambda i, k: wd[i][:, k, :],
                                           lambda i, k: h_split[i][:, k, :], HALF, hidden_ready)
                        mm.then_inc(res_mm.sem, 2 if n == SPLIT_CHUNKS - 1 else 1)
                give_back(LAYER_CHUNKS - C_SPLIT + 2)
                norm_sums(2, 3 * KT, 2)
                pe.wait_ge(x_ok.sem, x_ok.at(l, 3 * KT))

            def arrived2(c):
                pe.wait_ge(loaded[slot(c)], arrivals(c))

            spent = [0]

            def give_back(n):
                spent[0] += n

            def say_spent(mm):
                if spent[0]:
                    mm.then_inc(used, spent[0])
                    spent[0] = 0

            def product(out, weights, rhs, n=KT):
                for k in range(n):
                    mm = pe.matmul(out, weights(k), rhs(k), start=(k == 0), stop=(k == n - 1))
                    if k == 0:
                        say_spent(mm)
                return mm

            pe.wait_ge(small_in, 16 * 16)
            for f in range(KT):
                if f >= 4:
                    pe.wait_ge(ctx_ev, f - 3)
                for t in range(CTX // P):
                    mm = pe.transpose(ps[2 + f % 4][:, t * P:(t + 1) * P], ctx_in[:, t, f * P:(f + 1) * P], ident)
                mm.then_inc(ctx_mm, 1)

            def rms_sums(m, n=S):
                for t in range(KT):
                    pe.wait_ge(n_sq, m * KT + t + 1)
                    mm = pe.matmul(ps[1 + m % 2][:, 0:n], ones, squares[:, t % 2, 0:n], start=(t == 0), stop=(t == KT - 1))
                    mm.then_inc(n_mm, 1)

            rms_sums(0)
            rms_sums(1, CTX)

            pe.wait_ge(mod_ok, 4)
            pe.wait_ge(n_out, 2 * KT)
            g = 0
            for j in range(4):
                c = C_IN + j
                arrived2(c)
                lo, hi = IN_RANGES[j]
                wi = w(c, 0, KT, hi - lo)
                for t in range(4):
                    if g >= 4:
                        pe.wait_ge(pj_ev, g - 3)
                    wt = lambda k: wi[:, k, t * P:(t + 1) * P]
                    mm = product(ps[2 * (g % 4)], wt, lambda k: zT[:, k, :])
                    if j in (1, 2):
                        mm = product(ps[2 * (g % 4) + 1][:, 0:CTX], wt, lambda k: hz[:, k, :])
                    mm.then_inc(pj_mm, 1)
                    g += 1
                if j == 2:
                    pe.wait_ge(pj_ev, g - 3)
                    for t in range(NT):
                        src, t0 = (hz, t) if t < CTX // P else (zT, t - CTX // P)
                        mm = product(ps[2 * (g % 4)][:, 16 * t:16 * t + 16], lambda k: src[:, k, t0 * P:(t0 + 1) * P],
                                     lambda k: wi[:, k, 4 * P:4 * P + 16])
                    mm.then_inc(pj_mm, 1)
                    g += 1
                give_back(1)

            GATE = C_IN + 4
            wi = w(GATE, 0, KT, DW)
            for i in range(2 * DH):
                b = 2 * (i % 2)
                if i % 2 == 0:
                    t = i // 2
                    if t == 0:
                        arrived2(GATE)
                    pe.wait_ge(pj_ev, g if t == 0 else g - 1)
                    product(ps[4 + 2 * (t % 2)], lambda k: wi[:, k, t * P:(t + 1) * P], lambda k: zT[:, k, :]).then_inc(pj_mm, 1)
                    g += 1
                    if t == DH - 1:
                        give_back(1)
                if i >= 2:
                    pe.wait_ge(l2_std, i - 1)
                pe.wait_ge(l2_sq, i + 1)
                mm = pe.matmul(ps[b][:, :], ones, pre[:, i % 2, 0:S], start=True, stop=True)
                say_spent(mm)
                mm = pe.matmul(ps[b + 1][:, 0:CTX], ones, pre[:, i % 2, S:S + CTX], start=True, stop=True)
                mm.then_inc(l2_mm, 1)

            pe.wait_ge(pj_ev, g)
            pe.wait_ge(ab_v, 4)
            gs = ps[4][:, 0:NT * U8].rearrange("p (t u) -> p t u", u=U8)
            for d in range(2):
                pe.matmul(gs[:, :, d * DH:(d + 1) * DH], tri[:, d, :], la[:, :, d * DH:(d + 1) * DH], start=True, stop=True)
            pe.matmul(ps[5][:, 0:NT * U8], same, la.rearrange("p t u -> p (t u)"), start=True, stop=True)
            pe.matmul(ps[6][:, 0:2 * NT * U8], ones, la_half.rearrange("p t c -> p (t c)"), start=True, stop=True)\
                .then_inc(ab_mm, 1)

            for i in range(4):
                pe.wait_ge(pl_ok, POOL_STEPS[i])
                if i == 0:
                    pe.wait_ge(ab_a, 7)
                pe.matmul(ps[4 + i][:, :], pool_w[:, i, :], u[:, i, :], start=True, stop=True).then_inc(pl_mm, 1)
            pe.wait_ge(pl_ev, 4)
            pe.wait_ge(l2_std, 2 * DH)

            for step in range(NT):
                x = step >= CTX // P

                def needs(e, name, at_step=step):
                    delta.wait(pe, e, at_step, name)

                def says(name, mm):
                    delta.says("pe", step, name, mm)

                def cols(un):
                    t = tile_of(step, un // DH)
                    return slice(t * P, (t + 1) * P)

                def xcols(un):
                    t = tile_of(step, un // DH) - CTX // P
                    return slice(t * P, (t + 1) * P)

                def each(i, lhsT, rhs, turn=False, units=slice(0, U8)):
                    for un in range(U8)[units]:
                        o = pair(i)[:, un, :]
                        mm = pe.transpose(o, lhsT(un), ident) if turn else \
                            pe.matmul(o, lhsT(un), rhs(un), start=True, stop=True)
                    return mm

                needs("dve", "TRILA")
                if step == 0:
                    pe.wait_ge(l2_ok, 2 * DH)
                for d in range(2):
                    mm = pe.matmul(ps[d][:, :], ones, E[:, d * DH:(d + 1) * DH, :].rearrange("p u n -> p (u n)"),
                                   start=True, stop=True)
                says("G", mm)
                key = lambda un: kT[:, un % DH, cols(un)]
                says("KK", each(1, key, key))
                if x:
                    says("QK", each(2, key, lambda un: qT[:, un % DH, xcols(un)]))
                says("KTOK", each(3, key, None, True))
                needs("dve", "SUB")
                if x:
                    needs("act", "EG")
                says("VTOK", each(0, lambda un: vT[:, un % DH, cols(un)], None, True))
                needs("dve", "LT")
                says("L", each(1, lambda un: ETS[:, un, :], None, True))
                needs("dve", "PM")
                says("PT", each(2, lambda un: PA[:, un, :], None, True))
                needs("act", "PT")
                Ps, PTs = (PA, PB), (PTA, PTB)
                for r in range(1, 6):
                    p0, pt0, p1 = Ps[(r - 1) % 2], PTs[(r - 1) % 2], Ps[r % 2]
                    for d, units in DIRS.items():
                        if r == 1:
                            needs("act", "VTOK")
                        else:
                            needs("dve", f"SQT{r - 1}{d}")
                        says(f"SQ{r}{d}", each(3, lambda un: pt0[:, un, :], lambda un: p0[:, un, :], units=units))
                    if r < 5:
                        for d, units in DIRS.items():
                            says(f"SQT{r}{d}", each(0, lambda un: p0[:, un, :], lambda un: pt0[:, un, :], units=units))
                    for d, units in DIRS.items():
                        needs("act", f"SQ{r}{d}")
                        needs("dve", f"TT{r - 1}{d}" if r > 1 else "TT0")
                        says(f"TT{r}{d}", each(1 if r % 2 else 2, lambda un: p1[:, un, :], lambda un: TT[:, un, :], units=units))
                needs("dve", "TT5b")
                needs("pool", "VB")
                says("WT", each(3, lambda un: KBG[:, un, :], lambda un: TT[:, un, :]))
                says("U", each(0, lambda un: TT[:, un, :], lambda un: VB[:, un, :]))
                needs("act", "WT")
                for c in range(2):
                    for d, units in DIRS.items():
                        if c == 1:
                            needs("dve", f"S0{d}")
                        elif step:
                            needs("dve", f"S1{d}", step - 1)
                        elif d == "f":
                            pe.wait_ge(pl_ok, POOL_STEPS[-1])
                        says(f"WS{c}{d}", each(1, lambda un: PTB[:, un, :], lambda un: ST8[:, un, :], units=units))
                    if x:
                        for un in range(U8):
                            h = c if un < DH else 1 - c
                            part = slice(h * CHUNK, (h + 1) * CHUNK)
                            mm = pe.matmul(pair(3)[:, un, part], ST8[:, un, :], EG[:, un, part], start=True, stop=True)
                        says(f"Y{c}", mm)
                    for d, units in DIRS.items():
                        needs("dve", f"U{c}{d}")
                        says(f"SU{c}{d}", each(2, lambda un: (KT0 if c == 0 else KT1)[:, un, :], lambda un: PTA[:, un, :],
                                               units=units))
                if x:
                    says("X", each(0, lambda un: PTA[:, un, :], lambda un: ETI[:, un, :]))

            for h in range(DH):
                pe.wait_ge(l2_sq, 2 * DH + h + 1)
                if h == 0:
                    pe.wait_ge(delta.sem["dve"], delta.last("dve"))
                if h >= 2:
                    pe.wait_ge(l2_std, 2 * DH + h - 1)
                pe.matmul(ps[h % 2][:, :], ones, squares[:, h % 2, :], start=True, stop=True).then_inc(l2_mm, 1)
            pe.wait_ge(l2_ok, 2 * DH + DH)
            for t in range(KT):
                c = C_OUT2 + t // 4
                if t % 4 == 0:
                    arrived2(c)
                if t >= 4:
                    pe.wait_ge(wo_ok, t - 3)
                wo = w(c, 0, KT, 512)
                mm = product(ps[4 + t % 4], lambda k: wo[:, k, (t % 4) * P:(t % 4 + 1) * P], lambda k: mix2[:, k, :])
                mm.then_inc(wo_mm, 1)
                if t % 4 == 3:
                    give_back(1)

            pe.wait_ge(wo_ok, KT)
            pe.sem_inc(e_used.sem, E_SPLIT - 1)
            rms_sums(2)
            pe.wait_ge(n_out, 3 * KT)
            for t in range(ST):
                mm = product(ps[0][:, t * NE:(t + 1) * NE], lambda k: zT[:, k, t * P:(t + 1) * P], lambda k: w_rt[:, k, :])
            mm.then_inc(rt_mm, 1)
            for t in range(ST):
                for hf in range(2):
                    n = 2 * t + hf
                    if n >= 6:
                        pe.wait_ge(ht_lo, n - 5)
                    for f in range(4):
                        mm = pe.transpose(ps[2 + n % 6][:, f * P:(f + 1) * P],
                                          zT[:, 4 * hf + f, t * P:(t + 1) * P], ident)
                    mm.then_inc(ht_mm, 1)
            pe.wait_ge(rt_v, 5)
            for t in range(ST):
                mm = pe.transpose(ps[1][0:NE, t * P:(t + 1) * P], aff[:, t, :], ident)
            mm.then_inc(rt_mm, 1)
            pe.wait_ge(rt_v, POS_KNOWN)
            slot_rows = std[0:NE, :]
            for t in range(ST):
                mm = pe.transpose(ps[2][:, t * NE:(t + 1) * NE], slot_rows[:, t * P:(t + 1) * P], ident[0:NE, 0:NE])
            mm.then_inc(rt_mm, 1)
            pe.wait_ge(se_ok, ST)
            pe.wait_ge(ht_lo, 2 * ST)
            for f in range(KT):
                for hf in range(2):
                    n = 2 * f + hf
                    if n >= 4:
                        pe.wait_ge(xe_ev, n - 3)
                    for i in range(2 * ST):
                        t, part = i // 2, h_tok[i % 2]
                        mm = pe.matmul(ps[4 + n % 4][:, :], part[:, t, f * P:(f + 1) * P], sel[:, t, hf * 512:(hf + 1) * 512],
                                       start=(i == 0), stop=(i == 2 * ST - 1))
                    mm.then_inc(xe_mm, 1)
            pe.wait_ge(sw_ok, ST)
            for q in range(NE // 2):
                if q >= 4:
                    pe.wait_ge(sw_ev, q - 3)
                for t in range(ST):
                    mm = pe.transpose(ps[q % 4][:, t * P:(t + 1) * P], sel_w[:, t, q * P:(q + 1) * P], ident)
                mm.then_inc(sw_mm, 1)
            pe.wait_ge(sw_ev, NE // 2)
            pe.wait_ge(xe_ev, 2 * KT)
            pe.sem_inc(e_used.sem, 1)

            with pe.Fori(0, NE // TURN) as q:
                for j in range(TURN):
                    def turn(hf):
                        pe.wait_ge(ex_hid.sem, ex_hid.at(q, 2 * j + hf + 1))
                        for f in range(4):
                            mm = pe.transpose(ps[4 + 3 * hf][:, f * P:(f + 1) * P], hid[:, f * P:(f + 1) * P], ident)
                        mm.then_inc(ex_tm.sem, 1)

                    pe.wait_ge(ex_x.sem, ex_x.at(q, 2 * j + 2))
                    for c in range(EXP_CHUNKS):
                        if c == 7:
                            turn(0)
                        if c == 10:
                            turn(1)
                        if c == 8 and j >= 1:
                            pe.wait_ge(ex_ye.sem, ex_ye.at(q, 2 * j))
                        if c in (8, 10):
                            pe.wait_ge(ex_hl.sem, ex_hl.at(q, 2 * j + (c - 8) // 2 + 1))
                        pe.wait_ge(e_lo.sem, e_lo.at(q, E_RAW + EXP_CHUNKS * j + c + 1))
                        if c < 8:
                            wg = tiles(e_split[c % E_SPLIT], 512)
                            for i in range(4):
                                k = 4 * (c % 2) + i
                                for wp, part in ((0, HI), (1, HI), (0, LO)):
                                    mm = pe.matmul(ps[c // 2][0:CAP, :], xs[:, k, part], wg[wp][:, i, :],
                                                   start=(k == 0 and wp == 0 and part is HI),
                                                   stop=(k == KT - 1 and part is LO))
                        else:
                            wd = tiles(e_split[c % E_SPLIT], D)
                            for i in range(2):
                                f = 2 * (c - 8) + i
                                for n in range(2):
                                    for wp in range(2):
                                        mm = pe.matmul(ps[5 + n][:, :], hidT[:, f, :], wd[wp][:, i, n * 512:(n + 1) * 512],
                                                       start=(f == 0 and wp == 0), stop=(f == KT - 1 and wp == 1))
                        mm.then_inc(e_used.sem, 1)

            pe.wait_ge(ex_ye.sem, 2 * NE)
            for f in range(KT):
                mm = product(ps[f], lambda q: ye[:, q, f * P:(f + 1) * P], lambda q: sel_wT[:, q, :], NE // 2)
                mm.then_inc(cb_mm, 1)
            pe.wait_ge(cb_ok, KT)
            rms_sums(3)
            for t in range(ST):
                for hf in range(2):
                    n = 2 * t + hf
                    if n == 0:
                        pe.wait_ge(n_out, 4 * KT)
                    if n >= 4:
                        pe.wait_ge(fin_ev, n - 3)
                    for f in range(4):
                        mm = pe.transpose(ps[4 + n % 4][:, f * P:(f + 1) * P], zT[:, 4 * hf + f, t * P:(t + 1) * P], ident)
                    mm.then_inc(fin_mm, 1)

        @block.scalar
        def _(act):
            act.wait_ge(const_in, 32)
            act.wait_ge(ready, 1)
            act.wait_ge(rope_v, 8)
            nc.scalar.activation(sinT[:, :], rope_b, ACT.Sin).then_inc(rope_s, 1)
            act.wait_ge(rope_v, 10)
            nc.scalar.activation(cosT[:, :], kr_raw, ACT.Sin).then_inc(rope_s, 1)
            for f in range(2 * KT):
                act.wait_ge(turned, f + 1)
                dst = xT[:, f, :] if f < KT else memT[:, f - KT, :]
                nc.scalar.activation(dst, ps[f % 4][:, 0:S if f < KT else MEM], ACT.Copy).then_inc(turned_out, 1)
            A1 = nc.scalar.activation
            act.wait_ge(p2_mm, 1)
            A1(par2, ps[6][:, 0:NPAR2], ACT.Copy).then_inc(p2_ev, 1)
            act.wait_ge(p2_mm, 2)
            A1(taps2, ps[7][:, 0:CONV_K * 3 * DH], ACT.Copy).then_inc(p2_ev, 1)
            act.wait_ge(p2_ev, 1)
            for j, lo in enumerate((Q_C, Q_CC)):
                A1(cond[:, :, j], par2[:, lo:lo + KT], ACT.Silu).then_inc(cond_ok, 1)

            with act.Fori(0, DEPTH) as l:
                def col(j, m=P):
                    return par[0:m, j:j + 1]

                def norm(i, bank=1):
                    for t in range(KT):
                        act.wait_ge(cen.sem, cen.at(l, i * KT + t + 1))
                        if t >= 2:
                            act.wait_ge(var_mm.sem, var_mm.at(l, i * KT + t - 1))
                        nc.scalar.activation(squares[:, t % 2, :], zT[:, t, :], ACT.Square).then_inc(sq_ok.sem, 1)
                    act.wait_ge(var_mm.sem, var_mm.at(l, (i + 1) * KT))
                    nc.scalar.activation(std[:, :], ps[bank][:, :], ACT.Sqrt, bias=eps[:, 0:1], scale=1.0 / D)\
                        .then_inc(std_ok.sem, 1)
                    for t in range(KT):
                        act.wait_ge(scaled.sem, scaled.at(l, i * KT + t + 1))
                        g = P_LN + 2 * i * KT + t
                        nc.scalar.activation(xT[:, t, :], zT[:, t, :], ACT.Identity, bias=col(g + KT), scale=col(g))\
                            .then_inc(x_ok.sem, 1)

                act.wait_ge(par_mm.sem, par_mm.at(l, 1))
                nc.scalar.activation(par[:, :], ps[6][:, 0:NPAR], ACT.Copy).then_inc(par_ev.sem, 1)
                act.wait_ge(par_mm.sem, par_mm.at(l, 2))
                nc.scalar.activation(taps[:, :], ps[7][:, 0:TAPS * CT], ACT.Copy).then_inc(par_ev.sem, 1)
                act.wait_ge(par_ev.sem, par_ev.at(l, 2))

                for n in range(5):
                    act.wait_ge(proj_mm.sem, proj_mm.at(l, n + 1))
                    m = P if n < 4 else QK
                    dst = cqkv[:, n, :] if n < 4 else kr_raw[0:QK, :]
                    nc.scalar.activation(dst, ps[n][0:m, :], ACT.Identity, bias=col(PB_CQ + n, m)).then_inc(proj_ev.sem, 1)
                for n in range(4):
                    act.wait_ge(proj_ev.sem, proj_ev.at(l, n + 1))
                    nc.scalar.activation(mixT[:, n, :], cqkv[:, n, :], ACT.Square).then_inc(lsq.sem, 1)
                for t in range(CT):
                    act.wait_ge(proj_mm.sem, proj_mm.at(l, 7 + 2 * t))
                    if t >= 2:
                        act.wait_ge(glu.sem, glu.at(l, t - 1))
                    nc.scalar.activation(gates[:, t % 2, :], ps[(6 + 2 * t) % 8][:, :], ACT.Sigmoid, bias=col(PB_G + t))\
                        .then_inc(sig_ev.sem, 1)
                for n in range(2):
                    act.wait_ge(lsum.sem, lsum.at(l, n + 1))
                    act.wait_ge(glu.sem, glu.at(l, CT))
                    nc.scalar.activation(gates[:, n, :], ps[5 + n][:, :], ACT.Sqrt, bias=eps[:, 1:2], scale=1.0 / LORA)\
                        .then_inc(lstd.sem, 1)
                for h in range(HEADS):
                    act.wait_ge(up_mm.sem, up_mm.at(l, h + 1))
                    nc.scalar.activation(qh[0:QK, h, :], ps[h][0:QK, :], ACT.Copy).then_inc(q_ev.sem, 1)
                for h in range(HEADS):
                    act.wait_ge(up_mm.sem, up_mm.at(l, HEADS + h + 1))
                    nc.scalar.activation(kh[0:NOPE, h, :], ps[h][0:NOPE, :], ACT.Copy).then_inc(kv_ev.sem, 1)
                for t in range(ST):
                    act.wait_ge(up_mm.sem, up_mm.at(l, 2 * HEADS + t + 1))
                    nc.scalar.activation(vt[:, t, :], ps[t][:, :], ACT.Copy).then_inc(kv_ev.sem, 1)

                sc_bank = (0, 1, 6, 7)

                def exps(h):
                    for t in range(ST):
                        n = h * ST + t
                        act.wait_ge(sc_max.sem, sc_max.at(l, n + 1))
                        if h >= 2:
                            act.wait_ge(pt_mm.sem, pt_mm.at(l, (h - 1) * ST))
                        j = n % 8
                        nc.scalar.activation(probs[:, h % 2, t, 0:(t + 1) * P], ps[sc_bank[t]][:, 0:(t + 1) * P],
                                             ACT.Exp, bias=stat[:, 1, j:j + 1], scale=QK ** -0.5,
                                             accum_out=stat[:, 2, j:j + 1]).then_inc(sc_exp.sem, 1)
                        if n >= 2:
                            normalise(n - 2)

                def normalise(n):
                    h, t, j = n // ST, n % ST, n % 8
                    act.wait_ge(sc_rec.sem, sc_rec.at(l, n + 1))
                    p = probs[:, h % 2, t, 0:(t + 1) * P]
                    nc.scalar.activation(p, p, ACT.Copy, scale=stat[:, 3, j:j + 1]).then_inc(sc_norm.sem, 1)

                def turned_probs(h):
                    for kt in range(ST):
                        n = h * ST + kt
                        act.wait_ge(pt_mm.sem, pt_mm.at(l, n + 1))
                        if h >= 1 and kt == 0:
                            act.wait_ge(pv_mm.sem, pv_mm.at(l, h))
                        nc.scalar.activation(probsT[:, kt, kt * P:S], ps[2 + n % 2][:, kt * P:S], ACT.Copy)\
                            .then_inc(pt_ev.sem, 1)

                act.wait_ge(kcopy.sem, kcopy.at(l, 1))
                act.wait_ge(qrot.sem, qrot.at(l, HEADS))
                for h in range(HEADS + 1):
                    if h < HEADS:
                        exps(h)
                    else:
                        normalise(HEADS * ST - 2)
                        normalise(HEADS * ST - 1)
                    if 1 <= h <= MOD_CHUNKS:
                        act.wait_ge(mod_rows.sem, mod_rows.at(l, h))
                        A1(gates[0:2, (h - 1) % 2, :], mod_row, ACT.Copy).then_inc(mod_row_ev.sem, 1)
                    if h >= 1:
                        turned_probs(h - 1)

                for n in range(12):
                    act.wait_ge(xkv_mm.sem, xkv_mm.at(l, n + 1))
                    b = ps[sc_bank[n % 4]]
                    if n < 8:
                        nc.scalar.activation(xk[:, n, :], b[:, 0:MEM], ACT.Copy).then_inc(xkv_ev.sem, 1)
                    else:
                        t, j = (n - 8) // 2, n % 2
                        nc.scalar.activation(xv[:, t, j * 512:(j + 1) * 512], b[:, :], ACT.Copy).then_inc(xkv_ev.sem, 1)

                def high(n):
                    if n < 2:
                        act.wait_ge(xkv_mm.sem, xkv_mm.at(l, 12))
                    else:
                        chunk_used(act, l, n - 2)
                    act.wait_ge(raw_in[n % 2], l * (16 * SPLIT_CHUNKS) + 32 * (n // 2 + 1))
                    m = chunk_floats(n)
                    nc.scalar.activation(w_split[n % 2][0][:, 0:m], raw[n % 2][:, 0:m], ACT.Copy).then_inc(f_hi.sem, 1)

                high(0)
                high(1)
                for t in range(CT):
                    act.wait_ge(ccen.sem, ccen.at(l, t + 1))
                    if t >= 2:
                        act.wait_ge(cvar.sem, cvar.at(l, t - 1))
                    nc.scalar.activation(squares[:, t % 2, :], mixT[:, CT + t, :], ACT.Square).then_inc(csq.sem, 1)
                act.wait_ge(cvar.sem, cvar.at(l, CT))
                nc.scalar.activation(std[:, :], ps[3][:, :], ACT.Sqrt, bias=eps[:, 0:1], scale=1.0 / CW)\
                    .then_inc(cstd.sem, 1)
                for t in range(CT):
                    act.wait_ge(cmul.sem, cmul.at(l, t + 1))
                    nc.scalar.activation(mixT[:, CT + t, :], mixT[:, CT + t, :], ACT.Silu, bias=col(P_CNB + t),
                                         scale=col(P_CNG + t)).then_inc(cout.sem, 1)
                for n in range(N_MO + 2, N_XQ + 2):
                    high(n)
                norm(0)

                for t in range(KT):
                    act.wait_ge(xq_mm.sem, xq_mm.at(l, t + 1))
                    nc.scalar.activation(qx[:, t, :], ps[2 + t % 4][:, :], ACT.Copy).then_inc(xq_ev.sem, 1)
                    if t % 2 == 1:
                        high(N_XQ + 2 + t // 2)

                def xexps(h):
                    for t in range(ST):
                        n = 2 * h + t // 2
                        act.wait_ge(xs_max.sem, xs_max.at(l, n + 1))
                        if h >= 2:
                            act.wait_ge(xt_mm.sem, xt_mm.at(l, (h - 1) * MT))
                        j = (h * ST + t) % 8
                        nc.scalar.activation(probs[:, h % 2, t, 0:MEM],
                                             ps[sc_bank[n % 4]][:, (t % 2) * MEM:(t % 2 + 1) * MEM], ACT.Exp,
                                             bias=stat[:, 1, j:j + 1], scale=XD ** -0.5,
                                             accum_out=stat[:, 2, j:j + 1]).then_inc(xs_exp.sem, 1)

                def xturned(h):
                    for kt in range(MT):
                        act.wait_ge(xt_mm.sem, xt_mm.at(l, MT * h + kt + 1))
                        if h >= 1 and kt == 0:
                            act.wait_ge(xo_mm.sem, xo_mm.at(l, 2 * h))
                        nc.scalar.activation(probsT[:, kt, :], ps[2 + kt][:, :], ACT.Copy).then_inc(xt_ev.sem, 1)

                for h in range(XH + 1):
                    if h < XH:
                        xexps(h)
                    if h >= 1:
                        xturned(h - 1)

                for n in range(N_XO + 2, N_FFN + 2):
                    high(n)
                norm(1)
                for n in range(N_FFN, SPLIT_CHUNKS):
                    half_no, t, hidden_tile = ffn_chunk(n)
                    if hidden_tile:
                        act.wait_ge(ffn_mm.sem, ffn_mm.at(l, 2 * t + 1))
                        if t >= 2:
                            act.wait_ge(ffn_ok.sem, ffn_ok.at(l, t - 1))
                        nc.scalar.activation(gates[:, t % 2, :], ps[2 * (t % 4)][:, :], ACT.Silu).then_inc(ffn_act.sem, 1)
                    if n + 2 < SPLIT_CHUNKS:
                        high(n + 2)
                norm(2, 3)

            for f in range(KT):
                act.wait_ge(ctx_mm, f + 1)
                A1(ctxT[:, f, :], ps[2 + f % 4][:, 0:CTX], ACT.Copy).then_inc(ctx_ev, 1)

            def rms(m, src, dst, scale, bias, n=S, changed=None):
                for t in range(KT):
                    if changed is not None:
                        act.wait_ge(changed, t + 1)
                    if t >= 2:
                        act.wait_ge(n_mm, m * KT + t - 1)
                    A1(squares[:, t % 2, 0:n], src[:, t, :], ACT.Square).then_inc(n_sq, 1)
                act.wait_ge(n_mm, (m + 1) * KT)
                if m == 1:
                    act.wait_ge(n_mul, KT)
                A1(std[:, 0:n], ps[1 + m % 2][:, 0:n], ACT.Sqrt, bias=eps[:, 1:2], scale=1.0 / D).then_inc(n_std, 1)
                for t in range(KT):
                    act.wait_ge(n_mul, m * KT + t + 1)
                    A1(dst[:, t, :], dst[:, t, :], ACT.Identity, scale=scale(t), bias=bias(t) if bias else 0.0)\
                        .then_inc(n_out, 1)

            act.wait_ge(ctx_ev, KT)
            act.wait_ge(mod_ok, 4)
            rms(0, xT, zT, lambda t: gain[:, 0, t:t + 1], lambda t: mod[:, t, 0:1])
            rms(1, ctxT, hz, lambda t: gain[:, 1, t:t + 1], lambda t: mod[:, t, 1:2], CTX)

            def swish(c):
                act.wait_ge(cv_ok, CONV_K * (c + 1))
                t = c % DH
                if c < 2 * DH:
                    dst = (kT, vT)[c // DH]
                    A1(dst[:, t, CTX:], acc[:, c % 2, 0:S], ACT.Silu).then_inc(cv_out, 1)
                    A1(dst[:, t, 0:CTX], acc[:, c % 2, S + 3:S + 3 + CTX], ACT.Silu).then_inc(cv_out, 1)
                else:
                    A1(qT[:, t, :], acc[:, c % 2, 0:S], ACT.Silu).then_inc(cv_out, 1)

            act.wait_ge(padded, 1)
            g = 0
            for j in range(4):
                for t in range(4):
                    act.wait_ge(pj_mm, g + 1)
                    b = ps[2 * (g % 4)]
                    if j == 0:
                        A1(u[:, t, :], b, ACT.Copy).then_inc(pj_ev, 1)
                    else:
                        c = 4 * (j - 1) + t
                        if c >= 2:
                            act.wait_ge(cv_ok, CONV_K * (c - 1))
                        if j < 3:
                            A1(pre[:, c % 2, S + 5:S + 5 + CTX], ps[2 * (g % 4) + 1][:, 0:CTX], ACT.Copy)
                        A1(pre[:, c % 2, 2:2 + S], b, ACT.Copy).then_inc(pj_ev, 1)
                        if c >= 1:
                            swish(c - 1)
                    g += 1
                if j == 2:
                    act.wait_ge(pj_mm, g + 1)
                    src = ps[2 * (g % 4)][:, 0:16 * NT].rearrange("p (t a u) -> p t a u", a=2, u=U8)
                    A1(ab[:, :, :, 0:DH], src[:, :, :, 0:DH], ACT.Copy)
                    for step in range(NT):
                        ins = A1(ab[:, step, :, DH:], src[:, tile_of(step, 1), :, DH:], ACT.Copy)
                    ins.then_inc(pj_ev, 1)
                    g += 1
                if j == 3:
                    swish(11)

            for i in range(2 * DH + 2):
                if i >= 2 and i % 2 == 0:
                    t = i // 2 - 1
                    act.wait_ge(pj_mm, g + 1)
                    A1(gateT[:, t, :], ps[4 + 2 * (t % 2)], ACT.Copy).then_inc(pj_ev, 1)
                    g += 1
                if i < 2 * DH:
                    if i == 0:
                        act.wait_ge(cv_out, 4 * DH + DH)
                    if i >= 2:
                        act.wait_ge(l2_mm, i - 1)
                    src = kT[:, i, :] if i < DH else qT[:, i - DH, :]
                    if i < DH:
                        A1(pre[:, i % 2, 0:S], src[:, CTX:], ACT.Square)
                        A1(pre[:, i % 2, S:S + CTX], src[:, 0:CTX], ACT.Square).then_inc(l2_sq, 1)
                    else:
                        A1(pre[:, i % 2, 0:S], src, ACT.Square)
                        A1(pre[:, i % 2, S:S + CTX], src[:, 0:CTX], ACT.Square).then_inc(l2_sq, 1)
                if i >= 2:
                    m = i - 2
                    act.wait_ge(l2_mm, m + 1)
                    if m >= 2:
                        act.wait_ge(l2_ok, m - 1)
                    A1(acc[:, m % 2, 0:S], ps[2 * (m % 2)][:, :], ACT.Sqrt, bias=eps[:, 1:2])
                    A1(acc[:, m % 2, S:S + CTX], ps[2 * (m % 2) + 1][:, 0:CTX], ACT.Sqrt, bias=eps[:, 1:2]).then_inc(l2_std, 1)

            act.wait_ge(pj_ev, g)
            A1(gateT, gateT, ACT.Silu)
            act.wait_ge(ab_v, 1)
            A1(sp_e, sp_e, ACT.Exp, scale=-1.0).then_inc(ab_a, 1)
            A1(a_log, a_log, ACT.Exp).then_inc(ab_a, 1)
            act.wait_ge(ab_a, 2)
            A1(sp_e, sp_e, ACT.Ln, bias=1.0).then_inc(ab_a, 1)
            A1(beta, ab[:, :, 1, :], ACT.Sigmoid).then_inc(ab_a, 1)
            act.wait_ge(ab_mm, 1)
            A1(gsum.rearrange("p t u -> p (t u)"), ps[4][:, 0:NT * U8], ACT.Copy).then_inc(ab_a, 1)
            A1(eg.rearrange("p t u -> p (t u)"), ps[4][:, 0:NT * U8], ACT.Exp).then_inc(ab_a, 1)
            act.wait_ge(ab_v, 5)
            A1(sdec.rearrange("p t c -> p (t c)"), ps[6][:, 0:2 * NT * U8], ACT.Exp).then_inc(ab_a, 1)
            A1(tail, tail, ACT.Exp).then_inc(ab_a, 1)

            for i in range(4):
                act.wait_ge(pl_mm, i + 1)
                A1(mix2[:, DH + i, :], ps[4 + i][:, :], ACT.Copy, scale=par2[:, Q_PS + i:Q_PS + i + 1]).then_inc(pl_ev, 1)

            for step in range(NT):
                x = step >= CTX // P

                def needs(e, name):
                    delta.wait(act, e, step, name)

                def says(name, ins):
                    delta.says("act", step, name, ins)

                needs("dve", "MIN")
                says("E", A1(E, E, ACT.Exp))
                if x:
                    says("EG", A1(EG, pair(0), ACT.Exp))
                needs("pe", "KTOK")
                says("KTOK", A1(KT1, pair(3), ACT.Copy))
                needs("pe", "VTOK")
                says("VTOK", A1(VB, pair(0), ACT.Copy))
                needs("pe", "PT")
                says("PT", A1(PTA, pair(2), ACT.Copy))
                for r in range(1, 6):
                    for d, units in DIRS.items():
                        needs("pe", f"SQ{r}{d}")
                        says(f"SQ{r}{d}", A1((PA, PB)[r % 2][:, units, :], pair(3)[:, units, :], ACT.Copy))
                needs("pe", "WT")
                says("WT", A1(PTB, pair(3), ACT.Copy))

            def head_std(h):
                act.wait_ge(l2_mm, 2 * DH + h + 1)
                A1(head_dev[:, h, :], ps[h % 2][:, :], ACT.Sqrt, bias=eps[:, 1:2], scale=1.0 / P).then_inc(l2_std, 1)

            for h in range(DH):
                if h == 0:
                    act.wait_ge(delta.sem["dve"], delta.last("dve"))
                if h >= 2:
                    act.wait_ge(l2_mm, 2 * DH + h - 1)
                A1(squares[:, h % 2, :], mix2[:, h, :], ACT.Square).then_inc(l2_sq, 1)
                if h >= 1:
                    head_std(h - 1)
            head_std(DH - 1)

            rms(2, xT, zT, lambda t: gain[:, 2, t:t + 1], lambda t: mod[:, 3 * KT + t, 0:1], changed=wo_ok)
            act.wait_ge(rt_v, 2)
            A1(aff, aff, ACT.Exp).then_inc(rt_a, 1)
            for n in range(2 * ST):
                act.wait_ge(ht_mm, n + 1)
                A1(h_tok[0][:, n // 2, (n % 2) * 512:(n % 2 + 1) * 512], ps[2 + n % 6][:, :], ACT.Copy).then_inc(ht_ev, 1)
            for n in range(2 * KT):
                act.wait_ge(xe_mm, n + 1)
                A1(xeT[:, n // 2, (n % 2) * 512:(n % 2 + 1) * 512], ps[4 + n % 4][:, :], ACT.Copy).then_inc(xe_ev, 1)
            for q in range(NE // 2):
                act.wait_ge(sw_mm, q + 1)
                A1(sel_wT[:, q, :], ps[q % 4][:, :], ACT.Copy).then_inc(sw_ev, 1)

            with act.Fori(0, NE // TURN) as q:
                def used_up(j, c):
                    act.wait_ge(e_used.sem, e_used.at(q, E_SPLIT + EXP_CHUNKS * j + c + 1))

                def high(j, lo, hi):
                    for c in range(lo, hi):
                        act.wait_ge(e_in[c % E_RAW], q * (16 * TURN * EXP_CHUNKS // E_RAW)
                                    + 16 * (EXP_CHUNKS // E_RAW * j + c // E_RAW + 1))
                        act.wait_ge(e_used.sem, e_used.at(q, EXP_CHUNKS * j + c + 1))
                        A1(e_split[c % E_SPLIT][0], e_raw[c % E_RAW], ACT.Copy).then_inc(e_hi.sem, 1)

                def silu(j, hf):
                    used_up(j, 4 * hf + 1)
                    if 2 * j + hf:
                        act.wait_ge(ex_hid.sem, ex_hid.at(q, 2 * j + hf))
                    A1(gates[0:CAP, 0, :], ps[2 * hf][0:CAP, :], ACT.Silu).then_inc(ex_silu.sem, 1)

                def hidden_high(j, hf):
                    act.wait_ge(ex_tm.sem, ex_tm.at(q, 2 * j + hf + 1))
                    A1(hidT[:, 4 * hf:4 * hf + 4, HI], ps[4 + 3 * hf].rearrange("p (f c) -> p f c", c=P)[:, :, 0:CAP],
                       ACT.Copy).then_inc(ex_ht.sem, 1)

                def out_low(j):
                    used_up(j, EXP_CHUNKS - 1)
                    for n in range(2):
                        A1(std[0:CAP, :] if n else gates[0:CAP, 1, :], ps[5 + n][LO, :], ACT.Copy).then_inc(ex_yb.sem, 1)

                for j in range(TURN):
                    high(j, 0, 2)
                    if j >= 1:
                        out_low(j - 1)
                    high(j, 2, 5)
                    silu(j, 0)
                    high(j, 5, 9)
                    silu(j, 1)
                    high(j, 9, 10)
                    hidden_high(j, 0)
                    high(j, 10, 12)
                    hidden_high(j, 1)
                out_low(TURN - 1)
            rms(3, xT, zT, lambda t: par2[:, Q_NF + t:Q_NF + t + 1], None, changed=cb_ok)
            for n in range(2 * ST):
                t, hf = n // 2, n % 2
                act.wait_ge(fin_mm, n + 1)
                if t >= 2 and hf == 0:
                    act.wait_ge(stored[t % 2], 16 * (t // 2))
                A1(out_tok[:, t % 2, hf * 512:(hf + 1) * 512], ps[4 + n % 4][:, :], ACT.Copy).then_inc(fin_ev, 1)

        @block.gpsimd
        def _(pool):
            with pool.Fori(0, DEPTH) as l:
                pool.wait_ge(krot.sem, krot.at(l, 2))
                def every(x):
                    return x[NOPE:QK, :].rearrange("p (a n) -> p a n", a=1).broadcast_to([ROPE, HEADS, S])

                nc.gpsimd.tensor_tensor(kh[NOPE:QK, :, :], every(rope_a), every(rope_b), ALU.add).then_inc(kcopy.sem, 1)
                for h in range(HEADS):
                    q = qh[NOPE:QK, h, :]
                    pool.wait_ge(qrot_mm.sem, qrot_mm.at(l, h + 1))
                    nc.gpsimd.tensor_tensor(q, q, cosT[NOPE:QK, :], ALU.mult).then_inc(qrot_cos.sem, 1)
                    pool.wait_ge(qrot_cos.sem, qrot_cos.at(l, h + 1))
                    pool.wait_ge(qrot_sin.sem, qrot_sin.at(l, h + 1))
                    nc.gpsimd.tensor_tensor(q, q, (rope_a if h % 2 else rope_b)[NOPE:QK, :], ALU.add)\
                        .then_inc(qrot.sem, 1)
                sums = mixT[:, CT + DT, :]
                for k in range(TAPS):
                    x, c = hpad[:, DT, k:k + S], taps[:, k * CT + DT:k * CT + DT + 1]
                    c = c.broadcast_to([P, S])
                    if k == 0:
                        pool.wait_ge(qrot.sem, qrot.at(l, HEADS))
                        nc.gpsimd.tensor_tensor(sums, x, c, ALU.mult).then_inc(conv_p.sem, 1)
                        term = par[:, P_DWB + DT:P_DWB + DT + 1].broadcast_to([P, S])
                    else:
                        term = squares[:, k % 2, :]
                        nc.gpsimd.tensor_tensor(term, x, c, ALU.mult).then_inc(conv_p.sem, 1)
                    pool.wait_ge(conv_p.sem, conv_p.at(l, 2 * k + 1))
                    nc.gpsimd.tensor_tensor(sums, sums, term, ALU.add).then_inc(conv_p.sem, 1)

            G = nc.gpsimd
            count = [0]

            def behind(ins):
                ins.then_inc(pl_ok, 1)
                count[0] += 1
                pool.wait_ge(pl_ok, count[0])

            pool.wait_ge(small_in, 16 * 16)
            for i, win in enumerate(WINDOWS):
                buf = [pool_a, pool_b]
                W = GRID_W + win
                if i == 0:
                    pool.wait_ge(ctx_ev, KT)
                b0 = buf[0][:, 0:ROWS * W].rearrange("p (r c) -> p r c", c=W)
                behind(G.memset(b0, 0.0))
                pool.wait_ge(pj_ev, i + 1)
                ug = u[:, i, :].rearrange("p (r c) -> p r c", c=GRID_W)
                behind(G.tensor_copy(b0[:, :, win // 2:win // 2 + GRID_W], ug))
                cur, s, width = 0, 1, W
                while s < win:
                    src = buf[cur][:, 0:ROWS * W].rearrange("p (r c) -> p r c", c=W)
                    dst = buf[1 - cur][:, 0:ROWS * W].rearrange("p (r c) -> p r c", c=W)
                    width -= s
                    behind(G.tensor_tensor(dst[:, :, 0:width], src[:, :, 0:width], src[:, :, s:s + width], ALU.add))
                    cur, s = 1 - cur, 2 * s
                src = buf[cur][:, 0:ROWS * W].rearrange("p (r c) -> p r c", c=W)
                R = ROWS + win
                dst = buf[1 - cur][:, 0:R * GRID_W].rearrange("p (r c) -> p r c", c=GRID_W)
                behind(G.memset(dst, 0.0))
                behind(G.tensor_copy(dst[:, win // 2:win // 2 + ROWS, :], src[:, :, 0:GRID_W]))
                cur, s, height = 1 - cur, 1, R
                while s < win:
                    height -= s
                    src, dst = buf[cur], buf[1 - cur]
                    behind(G.tensor_tensor(dst[:, 0:height * GRID_W], src[:, 0:height * GRID_W],
                                           src[:, s * GRID_W:(s + height) * GRID_W], ALU.add))
                    cur, s = 1 - cur, 2 * s
                m = buf[cur][:, 0:S]
                behind(G.tensor_tensor(m, m, inv_cnt[:, i, :], ALU.mult))
                behind(G.tensor_tensor(u[:, i, :], m, u[:, i, :], ALU.subtract))
                assert count[0] == POOL_STEPS[i], (i, count)
            G.memset(mix2[:, 0:DH, :], 0.0)
            pool.wait_ge(pj_mm, 21)
            behind(G.memset(ST8, 0.0))
            assert count[0] == POOL_STEPS[-1], count

            for step in range(NT):
                x = step >= CTX // P

                def needs(e, name, at_step=step):
                    delta.wait(pool, e, at_step, name)

                def says(name, ins):
                    delta.says("pool", step, name, ins)

                def masked(m):
                    return [m[:, d:d + 1, :].broadcast_to([P, DH, P]) for d in range(2)]

                needs("act", "E")
                for name, dst, m in (("ETS", ETS, strict), ("ETI", ETI, tri)):
                    if step and name == "ETI":
                        needs("pe", "X" if step - 1 >= CTX // P else "SU1b", step - 1)
                    for d in range(2):
                        r = slice(d * DH, (d + 1) * DH)
                        ins = G.tensor_tensor(dst[:, r, :], E[:, r, :], masked(m)[d], ALU.mult)
                    says(name, ins)
                if x:
                    needs("act", "EG")
                    for d in range(2):
                        r = slice(d * DH, (d + 1) * DH)
                        t = tile_of(step, d) - CTX // P
                        ins = G.tensor_tensor(EG[:, r, :], EG[:, r, :], qT[:, :, t * P:(t + 1) * P], ALU.mult)
                    says("QD", ins)

                def scaled(dst, src, vec8):
                    return G.tensor_tensor(dst, src, vec8.unsqueeze(2).broadcast_to([P, U8, P]), ALU.mult)

                th = tail_half[:, step * U8:(step + 1) * U8, :]
                sd = sdec[:, step * U8:(step + 1) * U8, :]
                needs("act", "KTOK")
                if step == 0:
                    pool.wait_ge(ab_v, 8)
                says("KBG", scaled(KBG, KT1, beg[:, step, :]))
                says("KT0", scaled(KT0, KT1, th[:, :, 0]))
                needs("pool", "KT0")
                says("KT1", scaled(KT1, KT1, th[:, :, 1]))
                needs("act", "VTOK")
                says("VB", scaled(VB, VB, beta[:, step, :]))
                if step:
                    needs("dve", "S1b", step - 1)
                says("SD0", scaled(SD, ST8, sd[:, :, 0]))
                needs("dve", "S0b")
                says("SD1", scaled(SD, ST8, sd[:, :, 1]))

            for t in range(ST):
                pool.wait_ge(se_ok, t + 1)
                G.tensor_tensor(sel_w[:, t, :].rearrange("p (e c) -> p e c", c=CAP),
                                sel[:, t, :].bitcast(F32).rearrange("p (e c) -> p e c", c=CAP),
                                aff[:, t, :].unsqueeze(2).broadcast_to([P, NE, CAP]), ALU.mult).then_inc(sw_ok, 1)

        @block.vector
        def _(dve):
            V = nc.vector
            V.memset(par_rows[:, :], 0.0).then_inc(ready, 1)
            V.memset(eps[:, 0:1], LN_EPS)
            V.memset(eps[:, 1:2], RMS_EPS)
            V.memset(hpad[:, :, 0:TAPS - 1], 0.0)
            V.memset(tap_rows[:, :], 0.0).then_inc(ready, 1)

            dve.wait_ge(const_in, 32)
            V.tensor_copy(rope_b, rope_a.bitcast(I32)).then_inc(rope_v, 1)
            dve.wait_ge(rope_v, 1)
            V.tensor_scalar(rope_b, rope_b, consts[:, K_FREQ:K_FREQ + 1], None, ALU.mult).then_inc(rope_v, 1)
            dve.wait_ge(rope_v, 2)
            V.tensor_scalar(rope_a, rope_b, 1.0 / TWO_PI, ROUND, ALU.mult, ALU.add).then_inc(rope_v, 1)
            dve.wait_ge(rope_v, 3)
            V.tensor_scalar(rope_a, rope_a, -ROUND, None, ALU.add).then_inc(rope_v, 1)
            for n, c in enumerate((PI_A, PI_B, PI_C)):
                dve.wait_ge(rope_v, 4 + n)
                V.scalar_tensor_tensor(out=rope_b, in0=rope_a, scalar=-c, in1=rope_b, op0=ALU.mult, op1=ALU.add)\
                    .then_inc(rope_v, 1)
            dve.wait_ge(rope_v, 7)
            V.tensor_scalar(rope_b, rope_b, PI_MAX, -PI_MAX, ALU.min, ALU.max).then_inc(rope_v, 1)
            dve.wait_ge(rope_v, 8)
            V.scalar_tensor_tensor(out=rope_a, in0=rope_b, scalar=-1.0, in1=rope_b, op0=ALU.mult, op1=ALU.max)\
                .then_inc(rope_v, 1)
            dve.wait_ge(rope_v, 9)
            V.tensor_scalar(kr_raw, rope_a, -1.0, np.pi / 2, ALU.mult, ALU.add).then_inc(rope_v, 1)

            with dve.Fori(0, DEPTH) as l:
                behind = [0]

                def done(ins):
                    ins.then_inc(vec.sem, 1)
                    behind[0] += 1
                    return vec.at(l, behind[0])

                def low(n):
                    dve.wait_ge(f_hi.sem, f_hi.at(l, n + 1))
                    m, (hi, lo) = chunk_floats(n), w_split[n % 2]
                    V.tensor_tensor(lo[:, 0:m], raw[n % 2][:, 0:m], hi[:, 0:m].bitcast(F32), ALU.subtract).then_inc(f_lo.sem, 1)

                def add_in(i, t):
                    dve.wait_ge(res_mm.sem, res_mm.at(l, i * KT + t + 1))
                    V.scalar_tensor_tensor(out=zT[:, t, :], in0=xT[:, t, :], scalar=ALPHA,
                                           in1=ps[((6, 7, 0, 1) if i == 2 else (6, 7, 4, 5))[t % 4]][:, :],
                                           op0=ALU.mult, op1=ALU.add).then_inc(z_ok.sem, 1)

                def split_step(k, sig, first, src, parts):
                    if k < KT:
                        V.tensor_copy(parts[0][:, k, :], src[:, k, :]).then_inc(sig.sem, 1)
                    if k >= 1:
                        dve.wait_ge(sig.sem, sig.at(l, first + max(1, 2 * (k - 1))))
                        V.tensor_tensor(parts[1][:, k - 1, :], src[:, k - 1, :], parts[0][:, k - 1, :].bitcast(F32),
                                        ALU.subtract).then_inc(sig.sem, 1)

                def norm(i):
                    dve.wait_ge(mean_mm.sem, mean_mm.at(l, i + 1))
                    for t in range(KT):
                        V.scalar_tensor_tensor(out=zT[:, t, :], in0=ps[2 if i == 2 else 0][:, :], scalar=-1.0 / D,
                                               in1=zT[:, t, :], op0=ALU.mult, op1=ALU.add).then_inc(cen.sem, 1)
                    if i < 2:
                        low((N_XQ, N_FFN)[i] + 1)
                    dve.wait_ge(std_ok.sem, std_ok.at(l, i + 1))
                    n = done(V.reciprocal(std[:, :], std[:, :]))
                    dve.wait_ge(vec.sem, n)
                    for t in range(KT + 3):
                        if t < KT:
                            V.tensor_tensor(zT[:, t, :], zT[:, t, :], std[:, :], ALU.mult).then_inc(scaled.sem, 1)
                        if i < 2 and t >= 2:
                            if t - 2 < KT:
                                dve.wait_ge(x_ok.sem, x_ok.at(l, i * KT + t - 1))
                            split_step(t - 2, x_part, 2 * KT * i, xT, (xq_split, x_split)[i])

                dve.wait_ge(par_ev.sem, par_ev.at(l, 2))
                for t in range(CT):
                    dve.wait_ge(sig_ev.sem, sig_ev.at(l, t + 1))
                    V.scalar_tensor_tensor(out=hpad[:, t, TAPS - 1:], in0=ps[(5 + 2 * t) % 8][:, :],
                                           scalar=par[:, PB_A + t:PB_A + t + 1], in1=gates[:, t % 2, :],
                                           op0=ALU.add, op1=ALU.mult).then_inc(glu.sem, 1)
                for n in range(2):
                    dve.wait_ge(lstd.sem, lstd.at(l, n + 1))
                    v = done(V.reciprocal(gates[:, n, :], gates[:, n, :]))
                    dve.wait_ge(vec.sem, v)
                    for k in range(2):
                        j = P_QN + 2 * n + k
                        V.scalar_tensor_tensor(out=cqkv[:, 2 * n + k, :], in0=cqkv[:, 2 * n + k, :],
                                               scalar=par[:, j:j + 1], in1=gates[:, n, :],
                                               op0=ALU.mult, op1=ALU.mult).then_inc(lnorm.sem, 1)
                r = slice(NOPE, QK)
                dve.wait_ge(krot_mm.sem, krot_mm.at(l, 1))
                V.tensor_tensor(rope_a[r, :], ps[7][r, :], sinT[r, :], ALU.mult).then_inc(krot.sem, 1)
                V.tensor_tensor(rope_b[r, :], kr_raw[r, :], cosT[r, :], ALU.mult).then_inc(krot.sem, 1)
                dve.wait_ge(kcopy.sem, kcopy.at(l, 1))
                for h in range(HEADS):
                    dve.wait_ge(qrot_mm.sem, qrot_mm.at(l, h + 1))
                    if h >= 2:
                        dve.wait_ge(qrot.sem, qrot.at(l, h - 1))
                    V.tensor_tensor((rope_a if h % 2 else rope_b)[r, :], ps[4 + h % 4][r, :], sinT[r, :], ALU.mult)\
                        .then_inc(qrot_sin.sem, 1)

                sc_bank = (0, 1, 6, 7)

                def maximum(n):
                    t, j = n % ST, n % 8
                    b = ps[sc_bank[t]]
                    dve.wait_ge(sc_mm.sem, sc_mm.at(l, n + 1))
                    v = done(V.memset(b[0:CHUNK, (t + 1) * P - CHUNK:(t + 1) * P], NEG))
                    dve.wait_ge(vec.sem, v)
                    v = done(V.tensor_reduce(stat[:, 0, j:j + 1], b[:, 0:(t + 1) * P], AX, ALU.max))
                    dve.wait_ge(vec.sem, v)
                    V.tensor_scalar(stat[:, 1, j:j + 1], stat[:, 0, j:j + 1], -QK ** -0.5, None, ALU.mult)\
                        .then_inc(sc_max.sem, 1)

                def reciprocal(n):
                    j = n % 8
                    dve.wait_ge(sc_exp.sem, sc_exp.at(l, n + 1))
                    V.reciprocal(stat[:, 3, j:j + 1], stat[:, 2, j:j + 1]).then_inc(sc_rec.sem, 1)

                def tap(k):
                    for t in range(DT):
                        acc, x = mixT[:, CT + t, :], hpad[:, t, k:k + S]
                        c = taps[:, k * CT + t:k * CT + t + 1]
                        if k == 0:
                            V.tensor_scalar(acc, x, c, par[:, P_DWB + t:P_DWB + t + 1], ALU.mult, ALU.add)\
                                .then_inc(conv.sem, 1)
                        else:
                            dve.wait_ge(conv.sem, conv.at(l, DT * (k - 1) + t + 1))
                            V.scalar_tensor_tensor(out=acc, in0=x, scalar=c, in1=acc, op0=ALU.mult, op1=ALU.add)\
                                .then_inc(conv.sem, 1)

                def head_out(h):
                    dve.wait_ge(pv_mm.sem, pv_mm.at(l, h + 1))
                    lo = (h % 2) * VD
                    V.tensor_copy(mixT[lo:lo + VD, h // 2, :], ps[4][0:VD, :]).then_inc(pv_ev.sem, 1)

                LAG = 1
                for n in range(HEADS * ST + LAG):
                    if n < HEADS * ST:
                        maximum(n)
                    if n >= LAG:
                        reciprocal(n - LAG)
                    if n < TAPS:
                        tap(n)
                    if n >= 2 * ST and n % ST == 3:
                        head_out(n // ST - 2)
                head_out(HEADS - 2)
                head_out(HEADS - 1)
                dve.wait_ge(mod_mm.sem, mod_mm.at(l, MOD_CHUNKS))
                part = bass.ds(l * MOD_TILES, MOD_TILES)
                V.tensor_tensor(mod[:, part, :], mod_sum, par2[:, part].unsqueeze(2).broadcast_to([P, MOD_TILES, 2]),
                                ALU.add).then_inc(mod_in.sem, 1)

                for k in range(CT):
                    split_step(k, m_part, 0, mixT, m_split)
                dve.wait_ge(cstat_mm.sem, cstat_mm.at(l, 1))
                for t in range(CT):
                    V.scalar_tensor_tensor(out=mixT[:, CT + t, :], in0=ps[2][:, :], scalar=-1.0 / CW,
                                           in1=mixT[:, CT + t, :], op0=ALU.mult, op1=ALU.add).then_inc(ccen.sem, 1)
                low(N_MO)
                dve.wait_ge(cstd.sem, cstd.at(l, 1))
                v = done(V.reciprocal(std[:, :], std[:, :]))
                dve.wait_ge(vec.sem, v)
                for t in range(CT):
                    V.tensor_tensor(mixT[:, CT + t, :], mixT[:, CT + t, :], std[:, :], ALU.mult).then_inc(cmul.sem, 1)
                low(N_MO + 1)
                for k in range(CT, KT + 1):
                    if k < KT:
                        dve.wait_ge(cout.sem, cout.at(l, k - CT + 1))
                    split_step(k, m_part, 0, mixT, m_split)
                for t in range(KT):
                    add_in(0, t)
                    if t in (1, 3, 5):
                        low(N_MO + 2 + t // 2)
                norm(0)
                low(N_XQ + 2)
                low(N_XQ + 3)

                def xmaximum(n):
                    j = (2 * n) % 8
                    dve.wait_ge(xs_mm.sem, xs_mm.at(l, n + 1))
                    v = done(V.tensor_reduce(stat[:, 0, j:j + 2],
                                             ps[sc_bank[n % 4]][:, :].rearrange("p (a m) -> p a m", a=2), AX, ALU.max))
                    dve.wait_ge(vec.sem, v)
                    V.tensor_scalar(stat[:, 1, j:j + 2], stat[:, 0, j:j + 2], -XD ** -0.5, None, ALU.mult)\
                        .then_inc(xs_max.sem, 1)

                def xnormalise(n):
                    j = (2 * n) % 8
                    dve.wait_ge(xs_exp.sem, xs_exp.at(l, 2 * n + 2))
                    v = done(V.reciprocal(stat[:, 3, j:j + 2], stat[:, 2, j:j + 2]))
                    dve.wait_ge(vec.sem, v)
                    for i in range(2):
                        p = probs[:, (n // 2) % 2, 2 * (n % 2) + i, 0:MEM]
                        V.tensor_scalar(p, p, stat[:, 3, j + i:j + i + 1], None, ALU.mult).then_inc(xs_norm.sem, 1)

                def xhead_out(h):
                    for v in range(2):
                        dve.wait_ge(xo_mm.sem, xo_mm.at(l, 2 * h + v + 1))
                        n = done(V.tensor_copy(o_split[0][:, 2 * h + v, :], ps[4 + v][:, :]))
                        dve.wait_ge(vec.sem, n)
                        V.tensor_tensor(o_split[1][:, 2 * h + v, :], ps[4 + v][:, :], o_split[0][:, 2 * h + v, :].bitcast(F32),
                                        ALU.subtract).then_inc(xo_ev.sem, 1)

                for h in range(XH + 1):
                    if h < XH:
                        for j in range(2):
                            xmaximum(2 * h + j)
                        for j in range(2):
                            xnormalise(2 * h + j)
                    if h == 0:
                        low(N_XO)
                        low(N_XO + 1)
                    if h >= 1:
                        xhead_out(h - 1)
                for t in range(KT):
                    add_in(1, t)
                    if t in (1, 3, 5):
                        low(N_XO + 2 + t // 2)
                norm(1)
                for n in range(N_FFN, SPLIT_CHUNKS):
                    half_no, t, hidden_tile = ffn_chunk(n)
                    if hidden_tile:
                        dve.wait_ge(ffn_act.sem, ffn_act.at(l, t + 1))
                        dve.wait_ge(ffn_mm.sem, ffn_mm.at(l, 2 * t + 2))
                        whole, i = squares[:, t % 2, :], t % HALF
                        V.tensor_tensor(whole, gates[:, t % 2, :], ps[2 * (t % 4) + 1][:, :], ALU.mult)\
                            .then_inc(ffn_ok.sem, 1)
                        dve.wait_ge(ffn_ok.sem, ffn_ok.at(l, t + 1))
                        V.tensor_copy(h_split[0][:, i, :], whole).then_inc(h_part.sem, 1)
                        dve.wait_ge(h_part.sem, h_part.at(l, 2 * t + 1))
                        V.tensor_tensor(h_split[1][:, i, :], whole, h_split[0][:, i, :].bitcast(F32), ALU.subtract)\
                            .then_inc(h_part.sem, 1)
                    elif half_no == 0:
                        add_in(2, t)
                    else:
                        dve.wait_ge(res_mm.sem, res_mm.at(l, 3 * KT + t + 1))
                        V.tensor_tensor(zT[:, t, :], zT[:, t, :], ps[(6, 7, 0, 1)[t % 4]][:, :], ALU.add)\
                            .then_inc(z_ok.sem, 2 if t == KT - 1 else 1)
                    if n + 2 < SPLIT_CHUNKS:
                        low(n + 2)
                norm(2)
                assert behind[0] == vec.per, behind


            n2 = [0]

            def done(ins):
                ins.then_inc(vec2, 1)
                n2[0] += 1
                return n2[0]

            dve.wait_ge(p2_ev, 2)
            dve.wait_ge(mod_in.sem, DEPTH)
            for i, (which, col, norm) in enumerate(((1, 0, Q_N1), (1, 1, Q_N1), (4, 0, Q_N2))):
                V.scalar_tensor_tensor(out=gain[:, i, :], in0=mod[:, which * KT:(which + 1) * KT, col], scalar=1.0,
                                       in1=par2[:, norm:norm + KT], op0=ALU.add, op1=ALU.mult).then_inc(mod_ok, 1)
            V.tensor_copy(gain[:, 3, :], par2[:, Q_NF:Q_NF + KT]).then_inc(mod_ok, 1)

            def rms(m, src, dst, n=S):
                dve.wait_ge(n_std, m + 1)
                v = done(V.reciprocal(std[:, 0:n], std[:, 0:n]))
                dve.wait_ge(vec2, v)
                for t in range(KT):
                    V.tensor_tensor(dst[:, t, :], src[:, t, :], std[:, 0:n], ALU.mult).then_inc(n_mul, 1)

            rms(0, xT, zT)
            rms(1, ctxT, hz, CTX)
            dve.wait_ge(n_mul, 2 * KT)
            V.memset(pre[:, :, 0:2], 0.0)
            V.memset(pre[:, :, S + 2:S + 5], 0.0)
            V.memset(pre[:, :, PRE - 1:PRE], 0.0).then_inc(padded, 1)
            dve.wait_ge(n_out, 2 * KT)

            for c in range(3 * DH):
                tile = (c + DH) % (3 * DH)
                n = PRE - 3 if c < 2 * DH else S
                dve.wait_ge(pj_ev, 4 + c + 1 + (1 if c >= 2 * DH else 0))
                if c >= 2:
                    dve.wait_ge(cv_out, 2 * (c - 1) if c - 2 < 2 * DH else 4 * DH + c - 1 - 2 * DH)
                for k in range(CONV_K):
                    tap_col = taps2[:, k * 3 * DH + tile:k * 3 * DH + tile + 1]
                    x = pre[:, c % 2, k:k + n]
                    if k == 0:
                        V.tensor_scalar(acc[:, c % 2, 0:n], x, tap_col, None, ALU.mult).then_inc(cv_ok, 1)
                    else:
                        dve.wait_ge(cv_ok, CONV_K * c + k)
                        V.scalar_tensor_tensor(out=acc[:, c % 2, 0:n], in0=x, scalar=tap_col, in1=acc[:, c % 2, 0:n],
                                               op0=ALU.mult, op1=ALU.add).then_inc(cv_ok, 1)

            dve.wait_ge(small_in, 16 * 16)
            s3 = sp_s.rearrange("p (t u) -> p t u", u=U8)
            dve.wait_ge(pj_ev, 13)
            v = done(V.tensor_tensor(s3, ab[:, :, 0, :], dt_bias.unsqueeze(1).broadcast_to([P, NT, U8]), ALU.add))
            dve.wait_ge(vec2, v)
            V.scalar_tensor_tensor(out=sp_e, in0=sp_s, scalar=-1.0, in1=sp_s, op0=ALU.mult, op1=ALU.max).then_inc(ab_v, 1)

            for i in range(2 * DH):
                dve.wait_ge(l2_std, i + 1)
                n = S + CTX if i < DH else S
                v = done(V.reciprocal(acc[:, i % 2, 0:n], acc[:, i % 2, 0:n]))
                dve.wait_ge(vec2, v)
                if i < DH:
                    V.tensor_tensor(kT[:, i, CTX:], kT[:, i, CTX:], acc[:, i % 2, 0:S], ALU.mult)
                    V.tensor_tensor(kT[:, i, 0:CTX], kT[:, i, 0:CTX], acc[:, i % 2, S:S + CTX], ALU.mult).then_inc(l2_ok, 1)
                else:
                    q = qT[:, i - DH, :]
                    V.scalar_tensor_tensor(out=q, in0=q, scalar=float(P) ** -0.5, in1=acc[:, i % 2, 0:S],
                                           op0=ALU.mult, op1=ALU.mult).then_inc(l2_ok, 1)

            dve.wait_ge(ab_a, 3)
            v = done(V.scalar_tensor_tensor(out=sp_s, in0=sp_s, scalar=0.0, in1=sp_e, op0=ALU.max, op1=ALU.add))
            dve.wait_ge(vec2, v)
            V.scalar_tensor_tensor(out=la, in0=s3, scalar=-1.0, in1=a_log.unsqueeze(1).broadcast_to([P, NT, U8]),
                                   op0=ALU.mult, op1=ALU.mult).then_inc(ab_v, 1)
            dve.wait_ge(ab_v, 2)
            dve.wait_ge(ab_a, 4)
            V.tensor_scalar(nbeta, beta, -1.0, None, ALU.mult).then_inc(ab_v, 1)

            def halves(dst, src):
                for t in range(NT):
                    ins = V.tensor_tensor(dst[:, t * U8:(t + 1) * U8, :], half,
                                          src[:, t, :].unsqueeze(2).broadcast_to([P, U8, 2]), ALU.mult)
                return ins

            halves(la_half, la).then_inc(ab_v, 1)
            dve.wait_ge(ab_mm, 1)
            dve.wait_ge(ab_a, 6)
            V.tensor_tensor(tail.rearrange("p t u -> p (t u)"), ps[5][:, 0:NT * U8], gsum.rearrange("p t u -> p (t u)"),
                            ALU.subtract).then_inc(ab_v, 1)
            V.tensor_tensor(beg, beta, eg, ALU.mult).then_inc(ab_v, 1)
            dve.wait_ge(ab_a, 8)
            halves(tail_half, tail).then_inc(ab_v, 1)
            V.tensor_copy(sp_s[:, 0:1], sp_s[:, 0:1]).then_inc(ab_v, 1)

            for step in range(NT):
                x = step >= CTX // P

                def needs(e, name, at_step=step):
                    delta.wait(dve, e, at_step, name)

                def says(name, ins):
                    delta.says("dve", step, name, ins)

                def every(v8):
                    return v8.unsqueeze(2).broadcast_to([P, U8, P])

                if step:
                    needs("pool", "ETI", step - 1)
                for d in range(2):
                    r = slice(d * DH, (d + 1) * DH)
                    ins = V.tensor_tensor(E[:, r, :], tri[:, d:d + 1, :].broadcast_to([P, DH, P]),
                                          la[:, step, r].unsqueeze(2).broadcast_to([P, DH, P]), ALU.mult)
                says("TRILA", ins)
                needs("pe", "G")
                says("SUB", V.tensor_tensor(E, pair(0), every(gsum[:, step, :]), ALU.subtract))
                needs("dve", "SUB")
                says("MIN", V.tensor_scalar(E, E, 0.0, None, ALU.min))
                needs("pe", "KK")
                needs("pool", "ETS")
                says("LT", V.tensor_tensor(ETS, pair(1), ETS, ALU.mult))
                if x:
                    needs("pe", "QK")
                    needs("pool", "ETI")
                    says("QKD", V.tensor_tensor(ETI, pair(2), ETI, ALU.mult))
                needs("pe", "L")
                says("PM", V.tensor_tensor(PA, pair(1), every(nbeta[:, step, :]), ALU.mult))
                needs("act", "PT")
                says("TT0", V.tensor_tensor(TT, PTA, ident.unsqueeze(1).broadcast_to([P, U8, P]), ALU.add))
                for r in range(1, 6):
                    if r < 5:
                        for d, units in DIRS.items():
                            needs("pe", f"SQT{r}{d}")
                            says(f"SQT{r}{d}", V.tensor_copy((PTA, PTB)[r % 2][:, units, :], pair(0)[:, units, :]))
                    for d, units in DIRS.items():
                        needs("pe", f"TT{r}{d}")
                        says(f"TT{r}{d}", V.tensor_tensor(TT[:, units, :], TT[:, units, :],
                                                          pair(1 if r % 2 else 2)[:, units, :], ALU.add))
                needs("pe", "U")
                says("U", V.tensor_copy(PA, pair(0)))
                needs("dve", "U")
                for c in range(2):
                    for d, units in DIRS.items():
                        needs("pe", f"WS{c}{d}")
                        h = c if d == "f" else 1 - c
                        rows = slice(h * CHUNK, (h + 1) * CHUNK)
                        says(f"U{c}{d}", V.tensor_tensor(PTA[rows, units, :], PA[rows, units, :], pair(1)[rows, units, :],
                                                         ALU.subtract))
                    for d, units in DIRS.items():
                        needs("pe", f"SU{c}{d}")
                        needs("pool", f"SD{c}")
                        says(f"S{c}{d}", V.tensor_tensor(ST8[:, units, :], SD[:, units, :], pair(2)[:, units, :], ALU.add))
                if x:
                    needs("pe", "X")
                    for d in range(2):
                        t = tile_of(step, d) - CTX // P
                        o = mix2[:, 0:DH, t * P:(t + 1) * P]
                        un = slice(d * DH, (d + 1) * DH)
                        says(f"Y{d}", V.tensor_tensor(o, o, pair(3)[:, un, :], ALU.add))
                        needs("dve", f"Y{d}")
                        says(f"X{d}", V.tensor_tensor(o, o, pair(0)[:, un, :], ALU.add))

            for h in range(DH):
                dve.wait_ge(l2_std, 2 * DH + h + 1)
                r, o = head_dev[:, h, :], mix2[:, h, :]
                v = done(V.reciprocal(r, r))
                dve.wait_ge(vec2, v)
                v = done(V.scalar_tensor_tensor(out=o, in0=o, scalar=par2[:, Q_DN:Q_DN + 1], in1=r, op0=ALU.mult, op1=ALU.mult))
                dve.wait_ge(vec2, v)
                V.tensor_tensor(o, o, gateT[:, h, :], ALU.mult).then_inc(l2_ok, 1)
            for t in range(KT):
                dve.wait_ge(wo_mm, t + 1)
                V.scalar_tensor_tensor(out=xT[:, t, :], in0=ps[4 + t % 4][:, :], scalar=mod[:, 2 * KT + t, 0:1],
                                       in1=xT[:, t, :], op0=ALU.mult, op1=ALU.add).then_inc(wo_ok, 1)
            rms(2, xT, zT)

            m4, s4 = sp_s[:, 0:ST], sp_s[:, ST:2 * ST]
            logits = ps[0][:, 0:ST * NE].rearrange("p (t e) -> p t e", e=NE)
            dve.wait_ge(rt_mm, 1)
            V.tensor_reduce(m4, logits, AX, ALU.max).then_inc(rt_v, 1)
            dve.wait_ge(rt_v, 1)
            V.tensor_tensor(aff, logits, m4.unsqueeze(2).broadcast_to([P, ST, NE]), ALU.subtract).then_inc(rt_v, 1)
            dve.wait_ge(rt_a, 1)
            V.tensor_reduce(s4, aff, AX, ALU.add).then_inc(rt_v, 1)
            dve.wait_ge(rt_v, 3)
            V.reciprocal(s4, s4).then_inc(rt_v, 1)
            dve.wait_ge(rt_v, 4)
            V.tensor_tensor(aff, aff, s4.unsqueeze(2).broadcast_to([P, ST, NE]), ALU.mult).then_inc(rt_v, 1)
            rv = [5]

            def next_rt(ins):
                ins.then_inc(rt_v, 1)
                rv[0] += 1
                dve.wait_ge(rt_v, rv[0])

            work, cum, zero = squares[0:NE, 0, :], squares[0:NE, 1, :], std[0:NE, :]
            best = stat[0:NE, 0, :]
            for n in range(2 * ST):
                dve.wait_ge(ht_ev, n + 1)
                cols = slice((n % 2) * 512, (n % 2 + 1) * 512)
                V.tensor_tensor(h_tok[1][:, n // 2, cols], ps[2 + n % 6][:, :], h_tok[0][:, n // 2, cols].bitcast(F32),
                                ALU.subtract).then_inc(ht_lo, 1)
            dve.wait_ge(rt_mm, 2)
            dve.sem_inc(e_lo.sem, 2)
            next_rt(V.tensor_copy(work, ps[1][0:NE, :]))
            for r in range(ROUNDS):
                next_rt(V.max(best, work))
                if r == ROUNDS - 1:
                    V.memset(zero, 0.0)
                ins = V.match_replace(work, best, work, -1.0)
                next_rt(ins)
            next_rt(V.tensor_scalar(work, work, 0.0, None, ALU.is_lt))
            next_rt(V.tensor_tensor_scan(cum, zero, work, 0.0, ALU.add, ALU.add))
            next_rt(V.tensor_tensor(zero, cum, work, ALU.mult))
            assert rv[0] == POS_KNOWN, rv
            dve.sem_inc(e_lo.sem, 1)
            dve.wait_ge(rt_mm, 3)
            v = done(V.tensor_copy(pos, ps[2][:, 0:ST * NE].rearrange("p (t e) -> p t e", e=NE)))
            dve.wait_ge(vec2, v)
            for t in range(ST):
                V.tensor_tensor(sel[:, t, :].rearrange("p (e c) -> p e c", c=CAP),
                                iota.unsqueeze(1).broadcast_to([P, NE, CAP]),
                                pos[:, t, :].unsqueeze(2).broadcast_to([P, NE, CAP]), ALU.is_equal).then_inc(se_ok, 1)

            dve.wait_ge(xe_ev, 2 * KT)
            dve.wait_ge(sw_ev, NE // 2)
            dve.sem_inc(e_lo.sem, 1)
            with dve.Fori(0, NE // TURN) as q:
                def tokens(j):
                    x = xeT[:, :, bass.ds(q * (TURN * CAP) + j * CAP, CAP)]
                    V.tensor_scalar(xs[:, :, HI], x, 1.0, None, ALU.mult).then_inc(ex_x.sem, 1)
                    dve.wait_ge(ex_x.sem, ex_x.at(q, 2 * j + 1))
                    V.tensor_tensor(xs[:, :, LO], x, xs[:, :, HI].bitcast(F32), ALU.subtract).then_inc(ex_x.sem, 1)

                def low(j, lo, hi):
                    for c in range(lo, hi):
                        dve.wait_ge(e_hi.sem, e_hi.at(q, EXP_CHUNKS * j + c + 1))
                        high_part, low_part = e_split[c % E_SPLIT]
                        V.tensor_tensor(low_part, e_raw[c % E_RAW], high_part.bitcast(F32), ALU.subtract).then_inc(e_lo.sem, 1)

                def hidden_values(j, hf):
                    dve.wait_ge(ex_silu.sem, ex_silu.at(q, 2 * j + hf + 1))
                    dve.wait_ge(e_used.sem, e_used.at(q, E_SPLIT + EXP_CHUNKS * j + 4 * hf + 4))
                    V.tensor_tensor(hid[0:CAP, :], gates[0:CAP, 0, :], ps[2 * hf + 1][0:CAP, :], ALU.mult).then_inc(ex_hid.sem, 1)

                def hidden_low(j, hf):
                    dve.wait_ge(ex_ht.sem, ex_ht.at(q, 2 * j + hf + 1))
                    f = slice(4 * hf, 4 * hf + 4)
                    V.tensor_tensor(hidT[:, f, LO], ps[4 + 3 * hf].rearrange("p (f c) -> p f c", c=P)[:, :, 0:CAP],
                                    hidT[:, f, HI].bitcast(F32), ALU.subtract).then_inc(ex_hl.sem, 1)

                def out_sum(j):
                    for n in range(2):
                        dve.wait_ge(ex_yb.sem, ex_yb.at(q, 2 * j + n + 1))
                        V.tensor_tensor(ye[j % 2 * CAP:(j % 2 + 1) * CAP, bass.ds(q * (TURN // 2) + j // 2, 1), n * 512:(n + 1) * 512],
                                        ps[5 + n][0:CAP, :].unsqueeze(1),
                                        (std[0:CAP, :] if n else gates[0:CAP, 1, :]).unsqueeze(1), ALU.add).then_inc(ex_ye.sem, 1)

                tokens(0)
                for j in range(TURN):
                    low(j, 0, 2)
                    if j >= 1:
                        out_sum(j - 1)
                    low(j, 2, 6)
                    hidden_values(j, 0)
                    low(j, 6, 9)
                    hidden_low(j, 0)
                    low(j, 9, 10)
                    hidden_values(j, 1)
                    if j + 1 < TURN:
                        tokens(j + 1)
                    low(j, 10, 12)
                    hidden_low(j, 1)
                out_sum(TURN - 1)
            for f in range(KT):
                dve.wait_ge(cb_mm, f + 1)
                V.scalar_tensor_tensor(out=xT[:, f, :], in0=ps[f][:, :], scalar=mod[:, 5 * KT + f, 0:1], in1=xT[:, f, :],
                                       op0=ALU.mult, op1=ALU.add).then_inc(cb_ok, 1)
            rms(3, xT, zT)


def kernel(**inputs):
    import concourse.bacc as bacc
    from concourse.bass_utils import run_bass_kernel_spmd

    nc = bacc.Bacc("TRN2", target_bir_lowering=False, num_devices=1)
    arrays, aps = {}, {}
    for name, a in {**inputs, "consts": shape_constants()}.items():
        a = np.ascontiguousarray(a)
        arrays[f"in_{name}"] = a
        aps[name] = nc.dram_tensor(f"in_{name}", a.shape, mybir.dt.from_np(a.dtype), kind="ExternalInput").ap()
    out = nc.dram_tensor("out", (1, S, D), F32, kind="ExternalOutput").ap()
    build(nc, aps, out)
    r = run_bass_kernel_spmd(nc, [arrays], core_ids=[0])
    return r.results[0]["out"]
```
